# Optimizing a Trainium2 kernel written in Bass

```python
import math
import jax, jax.numpy as jnp
from jax import lax
import numpy as np

D_MODEL = 1024
BATCH = 1
SEQ = 256
DEPTH = 2

MEM_TOKENS = 256
HEAD_DIM = 64
MIX_WIDTH = D_MODEL
MEM_HEADS = 4
MEM_WIDTH = MEM_HEADS * HEAD_DIM
MAIN_WIDTH = MIX_WIDTH - MEM_WIDTH
S5_GROUP_DIM = 16
S5_GROUPS = MAIN_WIDTH // S5_GROUP_DIM
S5_STATE = 64
S5_DT_MIN = 0.001
S5_DT_MAX = 0.1
MOBA_HEADS = MAIN_WIDTH // HEAD_DIM
MOBA_KV_HEADS = 4
MOBA_GROUP = MOBA_HEADS // MOBA_KV_HEADS
KV_WIDTH = MOBA_KV_HEADS * HEAD_DIM
MOBA_BLOCK = 256
MOBA_TOP_BLOCKS = 3
MOBA_Q_CHUNK = 16
D_FF_DENSE = 256 * ((8 * D_MODEL // 3 + 255) // 256)
N_EXPERTS = 8
TOP_K = 2
D_FF_EXPERT = 7 * D_MODEL // 2
N_A_LAYERS = DEPTH // 2
RMS_EPS = 1e-6
NEG_INF = -1e30

kernel_name = "yoco_s5_moba_mem_moe_trunk"

def rms_norm(x, g):
    xf = x.astype(jnp.float32)
    y = xf * lax.rsqrt(jnp.mean(xf * xf, axis=-1, keepdims=True) + RMS_EPS)
    return (y * g.astype(jnp.float32)).astype(x.dtype)

def s5_mixer(u, lam_re, lam_im, log_dt, b_re, b_im, c_re, c_im, d_skip, w_glu, b_glu):
    f32 = jnp.float32
    bsz, s, _ = u.shape
    uf = u.astype(f32).reshape(bsz, s, S5_GROUPS, S5_GROUP_DIM)
    lam = lax.complex(lam_re.astype(f32), lam_im.astype(f32))
    dt = jnp.exp(log_dt.astype(f32))[:, None]
    lam_bar = jnp.exp(lam * dt)
    b = lax.complex(b_re.astype(f32), b_im.astype(f32))
    b_bar = ((lam_bar - 1.0) / lam)[..., None] * b
    bu = jnp.einsum('gpn,bsgn->bsgp', b_bar, uf)
    a = jnp.broadcast_to(lam_bar, bu.shape)

    def combine(left, right):
        a_l, b_l = left
        a_r, b_r = right
        return a_r * a_l, a_r * b_l + b_r

    _, states = lax.associative_scan(combine, (a, bu), axis=1)
    c = lax.complex(c_re.astype(f32), c_im.astype(f32))
    y = jnp.einsum('gnp,bsgp->bsgn', c, states).real \
        + d_skip.astype(f32).reshape(S5_GROUPS, S5_GROUP_DIM) * uf
    y = y.reshape(bsz, s, MAIN_WIDTH)
    g = jax.nn.gelu(y)
    out = g * jax.nn.sigmoid(g @ w_glu.astype(f32) + b_glu.astype(f32))
    return out.astype(u.dtype)

def memory_attention(q, mem, mem_norm, w_mem_k, w_mem_v, q_gain, k_gain):
    bsz, s, _ = q.shape
    mem_n = rms_norm(mem, mem_norm)
    qh = rms_norm(q.reshape(bsz, s, MEM_HEADS, HEAD_DIM), q_gain)
    kh = rms_norm((mem_n @ w_mem_k).reshape(bsz, MEM_TOKENS, MEM_HEADS, HEAD_DIM), k_gain)
    vh = (mem_n @ w_mem_v).reshape(bsz, MEM_TOKENS, MEM_HEADS, HEAD_DIM)
    logits = jnp.einsum('bshd,bmhd->bhsm', qh, kh).astype(jnp.float32) * (HEAD_DIM ** -0.5)
    p = jax.nn.softmax(logits, axis=-1).astype(vh.dtype)
    o = jnp.einsum('bhsm,bmhd->bshd', p, vh)
    return o.reshape(bsz, s, MEM_WIDTH)

def shared_kv(h, kv_norm, w_k, w_v, k_gain):
    bsz, s, _ = h.shape
    hn = rms_norm(h, kv_norm)
    k = rms_norm((hn @ w_k).reshape(bsz, s, MOBA_KV_HEADS, HEAD_DIM), k_gain)
    v = (hn @ w_v).reshape(bsz, s, MOBA_KV_HEADS, HEAD_DIM)
    nb = -(-s // MOBA_BLOCK)
    pad = nb * MOBA_BLOCK - s
    k = jnp.pad(k, ((0, 0), (0, pad), (0, 0), (0, 0)))
    v = jnp.pad(v, ((0, 0), (0, pad), (0, 0), (0, 0)))
    k_blocks = k.reshape(bsz, nb, MOBA_BLOCK, MOBA_KV_HEADS, HEAD_DIM).transpose(0, 3, 1, 2, 4)
    v_blocks = v.reshape(bsz, nb, MOBA_BLOCK, MOBA_KV_HEADS, HEAD_DIM).transpose(0, 3, 1, 2, 4)
    k_means = jnp.mean(k_blocks.astype(jnp.float32), axis=3).astype(k.dtype)
    return k_blocks, v_blocks, k_means

def moba_attention(q, k_blocks, v_blocks, k_means, q_gain):
    bsz, s, _ = q.shape
    nb = k_blocks.shape[2]
    k_sel = min(MOBA_TOP_BLOCKS, nb)
    n_chunks = s // MOBA_Q_CHUNK
    scale = HEAD_DIM ** -0.5
    qh = rms_norm(q.reshape(bsz, s, MOBA_HEADS, HEAD_DIM), q_gain)
    qh = qh.reshape(bsz, s, MOBA_KV_HEADS, MOBA_GROUP, HEAD_DIM)
    b_idx = jnp.arange(bsz)[:, None, None, None, None]
    h_idx = jnp.arange(MOBA_KV_HEADS)[None, :, None, None, None]
    blk_ids = jnp.arange(nb)
    slot_ids = jnp.arange(k_sel)

    def chunk(ci):
        start = ci * MOBA_Q_CHUNK
        qc = lax.dynamic_slice_in_dim(qh, start, MOBA_Q_CHUNK, axis=1)
        blk = start // MOBA_BLOCK
        gate = jnp.einsum('bqkgd,bknd->bkgqn', qc, k_means).astype(jnp.float32)
        gate = jnp.where(blk_ids < blk, gate, NEG_INF)
        _, top_i = lax.top_k(gate, k_sel)
        valid = slot_ids < blk
        ks = k_blocks[b_idx, h_idx, top_i]
        vs = v_blocks[b_idx, h_idx, top_i]
        s_sel = jnp.einsum('bqkgd,bkgqnjd->bkgqnj', qc, ks).astype(jnp.float32) * scale
        s_sel = jnp.where(valid[:, None], s_sel, NEG_INF)
        k_own = lax.dynamic_index_in_dim(k_blocks, blk, axis=2, keepdims=False)
        v_own = lax.dynamic_index_in_dim(v_blocks, blk, axis=2, keepdims=False)
        s_own = jnp.einsum('bqkgd,bkjd->bkgqj', qc, k_own).astype(jnp.float32) * scale
        q_pos = start + jnp.arange(MOBA_Q_CHUNK)
        k_pos = blk * MOBA_BLOCK + jnp.arange(MOBA_BLOCK)
        s_own = jnp.where(k_pos[None, :] <= q_pos[:, None], s_own, NEG_INF)
        logits = jnp.concatenate(
            [s_sel.reshape(bsz, MOBA_KV_HEADS, MOBA_GROUP, MOBA_Q_CHUNK, k_sel * MOBA_BLOCK), s_own],
            axis=-1)
        p = jax.nn.softmax(logits, axis=-1).astype(vs.dtype)
        p_sel = p[..., :k_sel * MOBA_BLOCK].reshape(
            bsz, MOBA_KV_HEADS, MOBA_GROUP, MOBA_Q_CHUNK, k_sel, MOBA_BLOCK)
        p_own = p[..., k_sel * MOBA_BLOCK:]
        o = jnp.einsum('bkgqnj,bkgqnjd->bqkgd', p_sel, vs) \
            + jnp.einsum('bkgqj,bkjd->bqkgd', p_own, v_own)
        return o

    outs = lax.map(chunk, jnp.arange(n_chunks))
    return outs.transpose(1, 0, 2, 3, 4, 5).reshape(bsz, s, MAIN_WIDTH)

def swiglu(h, w_gate, w_up, w_down):
    return (jax.nn.silu(h @ w_gate) * (h @ w_up)) @ w_down

def moe_swiglu(h, w_router, w_gate, w_up, w_down):
    bsz, s, d = h.shape
    t = bsz * s
    ht = h.reshape(t, d)
    logits = (ht @ w_router).astype(jnp.float32)
    top_vals, top_idx = lax.top_k(logits, TOP_K)
    gates = jax.nn.softmax(top_vals, axis=-1)
    flat_e = top_idx.reshape(-1)
    order = jnp.argsort(flat_e)
    tok = order // TOP_K
    xs = ht[tok]
    group_sizes = jnp.bincount(flat_e, length=N_EXPERTS).astype(jnp.int32)
    g = lax.ragged_dot(xs, w_gate, group_sizes)
    u = lax.ragged_dot(xs, w_up, group_sizes)
    y = lax.ragged_dot(jax.nn.silu(g) * u, w_down, group_sizes)
    y = y * gates.reshape(-1)[order][:, None].astype(y.dtype)
    out = jax.ops.segment_sum(y, tok, num_segments=t)
    return out.reshape(bsz, s, d)

def setup_inputs(seed: int = 0) -> dict:
    key = jax.random.key(seed)
    keys = iter(jax.random.split(key, 64))
    f32 = jnp.float32

    def normal(shape, scale):
        return scale * jax.random.normal(next(keys), shape, f32)

    def gain(n):
        return 1.0 + normal((n,), 0.02)

    n_idx = jnp.arange(S5_STATE, dtype=f32)[None, :]
    inp = {}
    inp["x"] = normal((BATCH, SEQ, D_MODEL), 1.0)
    inp["mem"] = normal((BATCH, MEM_TOKENS, D_MODEL), 1.0)
    inp["l0_mix_norm"] = gain(D_MODEL)
    inp["l0_w_in"] = normal((D_MODEL, MIX_WIDTH), D_MODEL ** -0.5)
    inp["l0_s5_lam_re"] = -0.5 + normal((S5_GROUPS, S5_STATE), 0.01)
    inp["l0_s5_lam_im"] = math.pi * n_idx + normal((S5_GROUPS, S5_STATE), 0.01)
    inp["l0_s5_log_dt"] = jax.random.uniform(next(keys), (S5_GROUPS,), f32,
                                             math.log(S5_DT_MIN), math.log(S5_DT_MAX))
    inp["l0_s5_b_re"] = normal((S5_GROUPS, S5_STATE, S5_GROUP_DIM), (2 * S5_GROUP_DIM) ** -0.5)
    inp["l0_s5_b_im"] = normal((S5_GROUPS, S5_STATE, S5_GROUP_DIM), (2 * S5_GROUP_DIM) ** -0.5)
    inp["l0_s5_c_re"] = normal((S5_GROUPS, S5_GROUP_DIM, S5_STATE), S5_STATE ** -0.5)
    inp["l0_s5_c_im"] = normal((S5_GROUPS, S5_GROUP_DIM, S5_STATE), S5_STATE ** -0.5)
    inp["l0_s5_d"] = normal((MAIN_WIDTH,), 1.0)
    inp["l0_s5_w_glu"] = normal((MAIN_WIDTH, MAIN_WIDTH), MAIN_WIDTH ** -0.5)
    inp["l0_s5_b_glu"] = normal((MAIN_WIDTH,), 0.01)
    inp["l0_mem_norm"] = gain(D_MODEL)
    inp["l0_w_mem_k"] = normal((D_MODEL, MEM_WIDTH), D_MODEL ** -0.5)
    inp["l0_w_mem_v"] = normal((D_MODEL, MEM_WIDTH), D_MODEL ** -0.5)
    inp["l0_mem_q_gain"] = gain(HEAD_DIM)
    inp["l0_mem_k_gain"] = gain(HEAD_DIM)
    inp["l0_w_out"] = normal((MIX_WIDTH, D_MODEL), MIX_WIDTH ** -0.5)
    inp["l0_ffn_norm"] = gain(D_MODEL)
    inp["l0_ffn_w_gate"] = normal((D_MODEL, D_FF_DENSE), D_MODEL ** -0.5)
    inp["l0_ffn_w_up"] = normal((D_MODEL, D_FF_DENSE), D_MODEL ** -0.5)
    inp["l0_ffn_w_down"] = normal((D_FF_DENSE, D_MODEL), D_FF_DENSE ** -0.5)
    inp["kv_norm"] = gain(D_MODEL)
    inp["kv_w_k"] = normal((D_MODEL, KV_WIDTH), D_MODEL ** -0.5)
    inp["kv_w_v"] = normal((D_MODEL, KV_WIDTH), D_MODEL ** -0.5)
    inp["kv_k_gain"] = gain(HEAD_DIM)
    inp["l1_mix_norm"] = gain(D_MODEL)
    inp["l1_w_in"] = normal((D_MODEL, MIX_WIDTH), D_MODEL ** -0.5)
    inp["l1_moba_q_gain"] = gain(HEAD_DIM)
    inp["l1_mem_norm"] = gain(D_MODEL)
    inp["l1_w_mem_k"] = normal((D_MODEL, MEM_WIDTH), D_MODEL ** -0.5)
    inp["l1_w_mem_v"] = normal((D_MODEL, MEM_WIDTH), D_MODEL ** -0.5)
    inp["l1_mem_q_gain"] = gain(HEAD_DIM)
    inp["l1_mem_k_gain"] = gain(HEAD_DIM)
    inp["l1_w_out"] = normal((MIX_WIDTH, D_MODEL), MIX_WIDTH ** -0.5)
    inp["l1_ffn_norm"] = gain(D_MODEL)
    inp["l1_moe_router"] = normal((D_MODEL, N_EXPERTS), D_MODEL ** -0.5)
    inp["l1_moe_w_gate"] = normal((N_EXPERTS, D_MODEL, D_FF_EXPERT), D_MODEL ** -0.5)
    inp["l1_moe_w_up"] = normal((N_EXPERTS, D_MODEL, D_FF_EXPERT), D_MODEL ** -0.5)
    inp["l1_moe_w_down"] = normal((N_EXPERTS, D_FF_EXPERT, D_MODEL), D_FF_EXPERT ** -0.5)
    return inp

def reference(x, mem,
              l0_mix_norm, l0_w_in, l0_s5_lam_re, l0_s5_lam_im, l0_s5_log_dt,
              l0_s5_b_re, l0_s5_b_im, l0_s5_c_re, l0_s5_c_im, l0_s5_d, l0_s5_w_glu, l0_s5_b_glu,
              l0_mem_norm, l0_w_mem_k, l0_w_mem_v, l0_mem_q_gain, l0_mem_k_gain,
              l0_w_out, l0_ffn_norm, l0_ffn_w_gate, l0_ffn_w_up, l0_ffn_w_down,
              kv_norm, kv_w_k, kv_w_v, kv_k_gain,
              l1_mix_norm, l1_w_in, l1_moba_q_gain,
              l1_mem_norm, l1_w_mem_k, l1_w_mem_v, l1_mem_q_gain, l1_mem_k_gain,
              l1_w_out, l1_ffn_norm, l1_moe_router, l1_moe_w_gate, l1_moe_w_up, l1_moe_w_down):
    layers = [
        dict(mix_norm=l0_mix_norm, w_in=l0_w_in,
             main=(l0_s5_lam_re, l0_s5_lam_im, l0_s5_log_dt, l0_s5_b_re, l0_s5_b_im,
                   l0_s5_c_re, l0_s5_c_im, l0_s5_d, l0_s5_w_glu, l0_s5_b_glu),
             mem=(l0_mem_norm, l0_w_mem_k, l0_w_mem_v, l0_mem_q_gain, l0_mem_k_gain),
             w_out=l0_w_out, ffn_norm=l0_ffn_norm,
             ffn=(l0_ffn_w_gate, l0_ffn_w_up, l0_ffn_w_down)),
        dict(mix_norm=l1_mix_norm, w_in=l1_w_in,
             main=(l1_moba_q_gain,),
             mem=(l1_mem_norm, l1_w_mem_k, l1_w_mem_v, l1_mem_q_gain, l1_mem_k_gain),
             w_out=l1_w_out, ffn_norm=l1_ffn_norm,
             ffn=(l1_moe_router, l1_moe_w_gate, l1_moe_w_up, l1_moe_w_down)),
    ]
    kv = None
    for i in range(DEPTH):
        p = layers[i]
        h = rms_norm(x, p["mix_norm"])
        proj = h @ p["w_in"]
        main_in = proj[..., :MAIN_WIDTH]
        q_mem = proj[..., MAIN_WIDTH:]
        if i < N_A_LAYERS:
            main = s5_mixer(main_in, *p["main"])
        else:
            if kv is None:
                kv = shared_kv(x, kv_norm, kv_w_k, kv_w_v, kv_k_gain)
            main = moba_attention(main_in, *kv, *p["main"])
        mem_out = memory_attention(q_mem, mem, *p["mem"])
        x = x + jnp.concatenate([main, mem_out], axis=-1) @ p["w_out"]
        h = rms_norm(x, p["ffn_norm"])
        if i % 2 == 0:
            x = x + swiglu(h, *p["ffn"])
        else:
            x = x + moe_swiglu(h, *p["ffn"])
    return x


_drawn_inputs = setup_inputs


def setup_inputs(seed=0):
    import zlib

    import numpy as np

    out = dict(_drawn_inputs(seed))
    spreads = {}
    factors = {'l0_mix_norm': 4.243,
     'l0_s5_lam_re': 51.432,
     'l0_s5_b_glu': 8.0,
     'l0_mem_norm': 4.743,
     'l0_mem_q_gain': 4.449,
     'l0_mem_k_gain': 7.117,
     'l0_ffn_norm': 2.672,
     'kv_norm': 5.546,
     'kv_k_gain': 6.159,
     'l1_mix_norm': 6.754,
     'l1_moba_q_gain': 6.085,
     'l1_mem_norm': 8.0,
     'l1_mem_q_gain': 7.171,
     'l1_mem_k_gain': 8.0,
     'l1_ffn_norm': 8.0}
    for name, (base, spread) in spreads.items():
        noise = np.random.default_rng([zlib.crc32(name.encode()), seed]).standard_normal(out[name].shape)
        drawn = base * np.exp(spread * noise) if base else spread * noise
        out[name] = __import__('jax').numpy.asarray(drawn.astype(out[name].dtype))
    for name, factor in factors.items():
        out[name] = (out[name] * factor).astype(out[name].dtype)
    return out
```

```python
import math

import numpy as np
import concourse.bass as bass
from concourse import mybir
from contextlib import ExitStack

P = 128
T = 256
TM = T // P
D = 1024
KT = D // P
HD = 64
GROUPS, GDIM, NSTATE = 48, 16, 64
MAIN = GROUPS * GDIM
PAIRS = GROUPS // 2
STEPS = 8
CHUNKS = T // STEPS
FF0 = 2816
NE, FFE = 8, 3584
CAP = 96
PASSES = -(-T // CAP)
NC_E = FFE // 512
EPS = 1e-6
SCALE = HD ** -0.5
NEG = -1e30
SLOT = 4096
NSLOT = 7

G_MIX0, G_MEM0, G_FFN0, G_KV, G_MIX1, G_MEM1, G_FFN1, G_BGLU = (8 * n for n in range(8))
G_ROWS = 8 * 7 + 6


def trunk(nc, w, out):
    fp, i32 = mybir.dt.float32, mybir.dt.int32
    ALU, ACT, AX = mybir.AluOpType, mybir.ActivationFunctionType, mybir.AxisListType
    ctx = ExitStack()
    with ctx:
        ctx.enter_context(nc.allow_non_contiguous_dma(reason="short head gain vectors"))
        sems = {}

        def S(name):
            if name not in sems:
                sems[name] = ctx.enter_context(nc.semaphore(name))
            return sems[name]

        arena = ctx.enter_context(nc.sbuf_tensor("arena", [P, 53200], fp))
        PS = [ctx.enter_context(nc.psum_tensor(f"bank{b}", [P, 512], fp)) for b in range(8)]

        def at(off, *shape, rows=P, row0=0):
            n = int(np.prod(shape))
            v = arena[row0:row0 + rows, off:off + n]
            if len(shape) == 2:
                v = v.rearrange("p (a b) -> p a b", a=shape[0])
            if len(shape) == 3:
                v = v.rearrange("p (a b c) -> p a b c", a=shape[0], b=shape[1])
            return v

        def cut(off, end):
            cur = [off]

            def take(*shape, rows=P):
                n = int(np.prod(shape))
                v = at(cur[0], *shape, rows=rows)
                cur[0] += n
                assert cur[0] <= end, (cur[0], end)
                return v
            return take

        RING = 0
        XS = at(28672, TM, D)
        HS0 = 30720
        HS = at(HS0, TM, D)
        HT = at(32768, KT, T)
        CT = at(34816, KT, T)
        A0, B0, C0 = 36864, 43008, 49152
        take_c = cut(C0, 53200)
        kT = [take_c(4, T, rows=HD), take_c(4, T, rows=HD)]
        vM = [take_c(TM, 256), take_c(TM, 256)]
        ident = take_c(P)
        iota = take_c(CAP)
        gT = take_c(G_ROWS)
        hg = take_c(5, rows=HD)
        hgk = take_c(1, rows=HD)
        gp = take_c(3, rows=HD)
        mh = take_c(32)
        ss = take_c(4)
        rs = take_c(4)
        hss = take_c(64)
        hrs = take_c(64)
        smx = take_c(4)
        snm = take_c(2, 4)
        ssum = take_c(2, 4)
        srec = take_c(2, 4)
        A8 = take_c(2, 2, PAIRS)
        ROUT = take_c(KT, NE)
        flag = take_c(1).bitcast(i32)

        Tm = at(12288, GROUPS, P)
        Bm = at(18432, 2, PAIRS, P)
        KX = 24576
        W0bd = at(KX, 2, PAIRS, 32)
        prod = at(KX + 1536, 2, 4, 2 * P)
        MD = at(KX + 3584, PAIRS, GDIM, rows=32)
        Ug = at(KX, GROUPS, CHUNKS)
        VX = at(KX + 1536, 2, PAIRS, CHUNKS)
        stp = at(KX + 3072, 2, 2, PAIRS)
        sq0 = at(KX + 3584, 512)
        CA = at(A0, 2, PAIRS, P)
        Wt = at(B0, 2, PAIRS, P)
        Kst = at(B0, PAIRS, P, rows=32)
        U4 = at(B0, STEPS, MAIN, rows=CHUNKS)
        U5 = at(RING, GROUPS, P, rows=CHUNKS)
        Ysb = at(B0, STEPS, PAIRS * GDIM, rows=64)
        Xbd = at(B0 + 3072, 2, PAIRS, 64)
        GT6 = at(32768, 6, T)
        misc = cut(8192, 12288)
        braw = misc(2, PAIRS, GDIM)
        cT = misc(2, PAIRS, GDIM)
        cnat = misc(2, 3, P)
        Dbc = misc(PAIRS, GDIM, rows=32)
        mask16 = misc(GDIM, rows=32)
        grow = misc(P, rows=G_ROWS)
        tr = cut(18432, 24576)
        lam_r, lam_i, ldt, edt = tr(P, rows=PAIRS), tr(P, rows=PAIRS), tr(2, rows=PAIRS), tr(2, rows=PAIRS)
        zr, zi, er, kk, rr, sn, cs, ebase = (tr(P, rows=PAIRS) for _ in range(8))
        fr, fi, t0, t1, t2 = (tr(P, rows=PAIRS) for _ in range(5))
        pw = tr(2, 8, P, rows=PAIRS)
        cm = tr(2, 8, P, rows=PAIRS)
        u0 = at(8192 + 3000, 4 * P, rows=PAIRS)
        u1 = at(8192 + 3000 + 512, 4 * P, rows=PAIRS)
        assert 3000 + 1024 <= SLOT
        MKR = at(12288, 4, 256)
        sqk = at(12288 + 1024, 1024)
        PB0, PT0, QT0 = at(HS0, 4, 2 * T), at(A0, 4, 2 * T), at(34816, 4, T, rows=HD)
        SIG = at(A0 + 4608, 2, T)
        HID0 = at(B0, 2, 4, T)
        SG0 = at(B0 + 2048, 4, T)
        PT1, KVR, VKV, kTkv = at(A0, 4, 2 * T), at(A0 + 2048, TM, 256), at(A0 + 2560, TM, 256), at(A0 + 3072, 4, T, rows=HD)
        TRI, ONES = at(A0 + 4096, P), at(A0 + 4224, P)
        MSK = at(A0 + 5120, P)
        QT1, PB1 = at(B0, 16, T, rows=HD), at(B0 + 4096, 4, 2 * T)
        sq1 = at(B0 + 4096, 2 * D)
        mo = cut(B0, B0 + 6144)
        XG, PICK, PG, HID = mo(KT, CAP), mo(TM, CAP), mo(TM, CAP), mo(2, 4 * CAP)
        YT, YR, GATE, SG1 = mo(KT, CAP), mo(D), mo(T), mo(2, 4 * CAP)
        LG, SEL, RNK, EX, GT_, POS0 = (mo(TM, NE) for _ in range(6))
        CMP, CMP2, LOWER = mo(NE, NE), mo(NE, NE), mo(NE, NE)
        POS, GW = mo(TM, PASSES * NE + 1), mo(TM, PASSES * NE)
        vt = mo(16)
        HID = HID.rearrange("p c (f t) -> p c f t", f=4)

        def mkrow(l, m):
            return MKR[:, 2 * l + m]

        M0_HEADS = [(h, kT[0][:, h], vM[0][:, :, h * HD:(h + 1) * HD], 6 + h // 2, h % 2) for h in range(4)]
        A1_HEADS = [(h, kTkv[:, h // 3], VKV[:, :, (h // 3) * HD:(h // 3 + 1) * HD], h // 2, h % 2) for h in range(12)] \
            + [(h, kT[1][:, h - 12], vM[1][:, :, (h - 12) * HD:(h - 11) * HD], h // 2, h % 2) for h in range(12, 16)]

        def cols(name, n0, n, kt=KT):
            return [(lambda s: s[:, 0:kt * n].rearrange("p (k n) -> p k n", k=kt),
                     w[name][:, n0:n0 + n].rearrange("(k p) n -> p k n", p=P))]

        def kv_pair(a, b):
            return [(lambda s: s[:, 0:2048].rearrange("p (k n) -> p k n", k=KT), w[a].rearrange("(k p) n -> p k n", p=P)),
                    (lambda s: s[:, 2048:4096].rearrange("p (k n) -> p k n", k=KT), w[b].rearrange("(k p) n -> p k n", p=P))]

        def rows_of(name, r0, r):
            return [(lambda s: s[:, 0:r // P * D].rearrange("p (k n) -> p k n", n=D),
                     w[name][r0:r0 + r, :].rearrange("(k p) n -> p k n", p=P))]

        FCH = [512] * 5 + [256]
        stream = [("memkv1", kv_pair("l1_w_mem_k", "l1_w_mem_v")), ("memkv0", kv_pair("l0_w_mem_k", "l0_w_mem_v")),
                  ("win0a", cols("l0_w_in", 0, 512)), ("win0b", cols("l0_w_in", 512, 512)),
                  ("glua", cols("l0_s5_w_glu", 0, 512, 6)), ("glub", cols("l0_s5_w_glu", 512, 256, 6)),
                  ("wout0a", cols("l0_w_out", 0, 512)), ("wout0b", cols("l0_w_out", 512, 512))]
        for c in range(len(FCH) + 1):
            if c < len(FCH):
                stream.append((f"g{c}", cols("l0_ffn_w_gate", 512 * c, FCH[c])))
                stream.append((f"u{c}", cols("l0_ffn_w_up", 512 * c, FCH[c])))
            if c >= 1:
                stream.append((f"d{c - 1}", rows_of("l0_ffn_w_down", 512 * (c - 1), FCH[c - 1])))
        stream += [("kv", kv_pair("kv_w_k", "kv_w_v")),
                   ("win1a", cols("l1_w_in", 0, 512)), ("win1b", cols("l1_w_in", 512, 512)),
                   ("wout1a", cols("l1_w_out", 0, 512)), ("wout1b", cols("l1_w_out", 512, 512))]
        NA = len(stream)
        NAMES = [n for n, _ in stream]

        def slot_of(n):
            return n % 2 if n < 6 else (n - 4) % NSLOT

        filled, need = [0] * NSLOT, []
        for n, (_, dmas) in enumerate(stream):
            filled[slot_of(n)] += 16 * len(dmas)
            need.append(filled[slot_of(n)])
        items = [("g", 0), ("u", 0)]
        for c in range(1, NC_E):
            items += [("g", c), ("u", c), ("d", c - 1)]
        items += [("d", NC_E - 1)]
        NI = len(items)
        assert NI == 3 * NSLOT
        full = [S(f"slot_full{s}") for s in range(NSLOT)]

        def e_slot(q):
            return slot_of(NA + q)

        def e_need(q):
            s = e_slot(q)
            return filled[s] + 16 * (sum(e_slot(r) == s for r in range(q + 1)))

        bank_full = [S(f"bank_full{b}") for b in range(8)]
        bank_free = [S(f"bank_free{b}") for b in range(8)]
        uses, units = [0] * 8, {}
        PER = [4, 4, 3, 3, 1, 1, 5, 4]
        TALLY = {"pick": (1, 1), "pgate": (0, 1), "down1": (0, NC_E - 1)}

        class Turn:
            def __init__(self, i, start):
                self.i, self.start = i, start

            def value(self, base, per):
                return self.i * per + (base - self.start * per)

            def count(self, name, k):
                pre, per = TALLY[name]
                return self.i * per + (pre + k)

            def weights(self, base):
                return self.i * (3 * 16) + base

        def unit(pe, key, b, turn=None):
            n = uses[b]
            uses[b] += 1
            units[key] = (b, n)
            if turn is not None:
                pe.wait_ge(bank_free[b], turn.value(n, PER[b]))
            elif n:
                pe.wait_ge(bank_free[b], n)
            return PS[b]

        def ready(ins, key):
            ins.then_inc(bank_full[units[key][0]], 1)

        def got(eng, key, turn=None):
            b, n = units[key]
            eng.wait_ge(bank_full[b], n + 1 if turn is None else turn.value(n + 1, PER[b]))
            return PS[b]

        def free(ins, key):
            ins.then_inc(bank_free[units[key][0]], 1)

        def read_out(eng, key, turn=None):
            b, n = units[key]
            eng.wait_ge(bank_free[b], n + 1 if turn is None else turn.value(n + 1, PER[b]))

        item_done = {}

        block = ctx.enter_context(nc.Block())

        @block.tensor
        def _(pe):
            mm = nc.tensor.matmul
            st = [0]

            def item(name):
                n = st[0]
                assert NAMES[n] == name, (NAMES[n], name)
                st[0] += 1
                pe.wait_ge(full[slot_of(n)], need[n])
                return at(slot_of(n) * SLOT, SLOT)

            def transpose(o, i, rows=P):
                return nc.tensor.transpose(o, i, ident[0:rows, 0:rows])

            pe.wait_ge(S("ident"), 2)
            pe.wait_ge(S("ld_gains"), 16 * 8)
            p = unit(pe, "gT", 4)
            ready(transpose(p[:, 0:G_ROWS], grow, G_ROWS), "gT")
            for q in range(4):
                p = unit(pe, ("memT", q), q)
                for k in (2 * q, 2 * q + 1):
                    for m in range(TM):
                        if q == 0 and k == 0:
                            pe.wait_ge(S("mem_rows"), m + 1)
                        last = transpose(p[:, (k % 2) * T + m * P:(k % 2) * T + (m + 1) * P], HS[:, m, k * P:(k + 1) * P])
                ready(last, ("memT", q))
            pe.wait_ge(S("ld_c"), 64)
            for ri in range(2):
                p = unit(pe, ("cT", ri), 4 + ri)
                for a in range(3):
                    last = transpose(p[:, a * P:(a + 1) * P], cnat[:, ri, a])
                ready(last, ("cT", ri))

            def proj_kv(name, src, tag, banks):
                s = item(name)
                for m in range(TM):
                    p = unit(pe, (tag, m), banks[m])
                    for h in range(2):
                        for k in range(KT):
                            last = mm(p[:, h * 256:(h + 1) * 256], lhsT=src[:, k, m * P:(m + 1) * P],
                                      rhs=s[:, h * 2048 + k * 256:h * 2048 + (k + 1) * 256],
                                      start=(k == 0 and h == 0), stop=(k == KT - 1), skip_group_check=True)
                    ready(last, (tag, m))
                item_done[name] = units[(tag, TM - 1)]

            for q in range(4):
                read_out(pe, ("memT", q))
            proj_kv("memkv1", HT, "mkv1", (0, 1))
            for b, src, key in ((6, cm, "cm"), (7, pw, "pw")):
                pe.wait_ge(S("s5_" + key), 1)
                p = unit(pe, "q_" + key, b)
                for ri in range(2):
                    for n in range(8):
                        last = transpose(p[:, (ri * 8 + n) * PAIRS:(ri * 8 + n + 1) * PAIRS], src[:, ri, n], PAIRS)
                ready(last, "q_" + key)
            pe.wait_ge(S("x_rows0"), TM)
            for q in range(4):
                p = unit(pe, ("xT0", q), q)
                for k in (2 * q, 2 * q + 1):
                    for m in range(TM):
                        last = transpose(p[:, (k % 2) * T + m * P:(k % 2) * T + (m + 1) * P], HS[:, m, k * P:(k + 1) * P])
                ready(last, ("xT0", q))
            proj_kv("memkv0", CT, "mkv0", (4, 5))

            def proj_rows(names, src, tag, banks):
                for h, name in enumerate(names):
                    s = item(name)
                    for m in range(TM):
                        p = unit(pe, (tag, h, m), banks[2 * h + m])
                        for k in range(KT):
                            last = mm(p[:, :], lhsT=src[:, k, m * P:(m + 1) * P], rhs=s[:, k * 512:(k + 1) * 512],
                                      start=(k == 0), stop=(k == KT - 1))
                        ready(last, (tag, h, m))
                    item_done[name] = units[(tag, h, TM - 1)]

            for q in range(4):
                read_out(pe, ("xT0", q))
            proj_rows(("win0a", "win0b"), HT, "win0", (0, 1, 2, 3))
            pe.wait_ge(S("mk_rows"), 1)
            for l in (1, 0):
                for m in range(TM):
                    p = unit(pe, ("mkT", l, m), 4 + m)
                    for h in range(4):
                        last = transpose(p[0:HD, h * P:(h + 1) * P], mkrow(l, m)[:, h * HD:(h + 1) * HD])
                    ready(last, ("mkT", l, m))
            pe.wait_ge(S("s5_w"), 12)
            for n in range(12):
                ri, jq = n // 6, n % 6
                p = unit(pe, ("Bm", n), 4 + n % 2)
                for a in range(4):
                    last = transpose(p[:, a * P:(a + 1) * P], Wt[:, ri, jq * 4 + a])
                ready(last, ("Bm", n))
            pe.wait_ge(S("s5_w0"), 4)
            pe.wait_ge(S("s5_ca"), 12)
            for ri in range(2):
                read_out(pe, ("cT", ri))
            for jq in range(6):
                p = unit(pe, ("K", jq), 4 + jq % 2)
                for a in range(4):
                    j = jq * 4 + a
                    for ri in range(2):
                        mm(p[0:32, a * P:a * P + GDIM], lhsT=W0bd[:, ri, j], rhs=cT[:, ri, j],
                           start=(a == 0 and ri == 0), stop=(ri == 1), skip_group_check=True)
                    for ri in range(2):
                        last = mm(p[0:32, a * P + GDIM:(a + 1) * P], lhsT=W0bd[:, ri, j], rhs=CA[:, ri, j, 0:7 * GDIM],
                                  start=False, stop=(ri == 1), skip_group_check=True)
                ready(last, ("K", jq))
            pe.wait_ge(S("u5_act"), 3)
            pe.wait_ge(S("u5_dve"), 3)
            pe.wait_ge(S("u5_pool"), 2)
            for n in range(3):
                p = unit(pe, ("Ug", n), n)
                for a in range(16):
                    g = n * 16 + a
                    last = transpose(p[:, a * CHUNKS:(a + 1) * CHUNKS], U5[:, g], CHUNKS)
                ready(last, ("Ug", n))
            for n in range(12):
                read_out(pe, ("Bm", n))
            for n in range(3):
                read_out(pe, ("Ug", n))
            vb = [unit(pe, ("V", n), 3 + n) for n in range(3)]
            for j in range(PAIRS):
                for ri in range(2):
                    b, c0 = (vb[ri], j * CHUNKS) if j < 16 else (vb[2], (ri * 8 + j - 16) * CHUNKS)
                    for g2 in range(2):
                        last = mm(b[g2 * 64:(g2 + 1) * 64, c0:c0 + CHUNKS], lhsT=Bm[:, ri, j, g2 * 64:(g2 + 1) * 64],
                                  rhs=Ug[:, g2 * PAIRS + j], start=True, stop=True, skip_group_check=True)
                        if j == 15 and g2 == 1:
                            ready(last, ("V", ri))
            ready(last, ("V", 2))
            pe.wait_ge(S("q0_rows"), 1)
            for m in range(TM):
                p = unit(pe, ("q0T", m), 6 + m)
                for h in range(4):
                    last = transpose(p[0:HD, h * P:(h + 1) * P], HS[:, m, MAIN + h * HD:MAIN + (h + 1) * HD])
                ready(last, ("q0T", m))
            pe.wait_ge(S("tm"), 16 * 16)
            yb = [unit(pe, ("Y", n), n) for n in range(6)]
            for j in range(PAIRS):
                for g2 in range(2):
                    mm(yb[j // 4][g2 * 32:(g2 + 1) * 32, (j % 4) * P:(j % 4 + 1) * P], lhsT=Ug[:, g2 * PAIRS + j],
                       rhs=Tm[:, g2 * PAIRS + j], start=(j % 4 == 0), stop=False, skip_group_check=True)
            pe.wait_ge(S("xbd"), 4)
            for j in range(PAIRS):
                for ri in range(2):
                    last = mm(yb[j // 4][0:64, (j % 4) * P:(j % 4 + 1) * P], lhsT=Xbd[:, ri, j], rhs=CA[:, ri, j],
                              start=False, stop=(ri == 1), skip_group_check=True)
                if j % 4 == 3:
                    ready(last, ("Y", j // 4))
            for n in range(6):
                read_out(pe, ("Y", n))
            for n in range(3):
                p = unit(pe, ("yT", n), 6 + n % 2)
                for k in range(STEPS):
                    last = transpose(p[:, k * 64:(k + 1) * 64], Ysb[:, k, n * P:(n + 1) * P], 64)
                ready(last, ("yT", n))

            def attention(tag, heads, qT, masked, pbuf, pt_sb, banks):
                LB, PB = banks
                ng = len(heads) // 2

                def logits(n):
                    for a in range(2):
                        qh, kt_, _, _, _ = heads[2 * n + a]
                        p = unit(pe, (tag, "L", n, a), LB[2 * (n % 2) + a])
                        for m in range(TM):
                            nk = P * (m + 1) if masked(2 * n + a) else T
                            last = mm(p[:, m * T:m * T + nk], lhsT=qT[:, qh, m * P:(m + 1) * P], rhs=kt_[:, 0:nk],
                                      start=True, stop=True, skip_group_check=True)
                        ready(last, (tag, "L", n, a))

                def flip(n):
                    for a in range(2):
                        pe.wait_ge(S(tag + "_p"), 2 * n + a + 1)
                        p = unit(pe, (tag, "PT", n, a), PB[a])
                        for kt_ in range(TM):
                            for m in range(TM):
                                if masked(2 * n + a) and kt_ > m:
                                    continue
                                last = transpose(p[:, kt_ * T + m * P:kt_ * T + (m + 1) * P],
                                                 pbuf[:, (n % 2) * 2 + a, m * T + kt_ * P:m * T + (kt_ + 1) * P])
                        ready(last, (tag, "PT", n, a))

                def outs(n):
                    for a in range(2):
                        _, _, v, _, half = heads[2 * n + a]
                        read_out(pe, (tag, "PT", n, a))
                        p = unit(pe, (tag, "O", n, a), PB[a])
                        o = p[64 * half:64 * half + 64, 0:T]
                        mm(o, lhsT=v[:, 0], rhs=pt_sb[:, (n % 2) * 2 + a, 0:T], start=True, stop=False,
                           skip_group_check=True)
                        m0 = P if masked(2 * n + a) else 0
                        last = mm(o[:, m0:T], lhsT=v[:, 1], rhs=pt_sb[:, (n % 2) * 2 + a, T + m0:2 * T],
                                  start=False, stop=True, skip_group_check=True)
                        ready(last, (tag, "O", n, a))

                return logits, flip, outs, ng

            lg, fl, ou, ng = attention("m0", M0_HEADS, QT0, lambda h: False, PB0, PT0, ((2, 3, 4, 5), (6, 7)))
            for m in range(TM):
                read_out(pe, ("q0T", m))
                read_out(pe, ("mkT", 0, m))
            lg(0)
            lg(1)
            for n in range(3):
                read_out(pe, ("yT", n))
            sa = item("glua")
            sb_ = item("glub")
            for n in range(6):
                s, n0, wn = (sa, n * P, 512) if n < 4 else (sb_, (n - 4) * P, 256)
                p = unit(pe, ("glu", n), n % 2)
                for k in range(6):
                    last = mm(p[:, 0:T], lhsT=s[:, k * wn + n0:k * wn + n0 + P], rhs=GT6[:, k], start=(k == 0), stop=(k == 5))
                ready(last, ("glu", n))
                if n == 3 or n == 5:
                    item_done["glua" if n == 3 else "glub"] = units[("glu", n)]
            fl(0)
            ou(0)
            fl(1)
            ou(1)

            def proj_out(names, tag, banks, wait):
                for h, name in enumerate(names):
                    s = item(name)
                    for m in range(TM):
                        p = unit(pe, (tag, h, m), banks[2 * h + m])
                        for k in range(KT):
                            last = mm(p[:, :], lhsT=CT[:, k, m * P:(m + 1) * P], rhs=s[:, k * 512:(k + 1) * 512],
                                      start=(k == 0), stop=(k == KT - 1))
                        ready(last, (tag, h, m))
                    item_done[name] = units[(tag, h, TM - 1)]

            pe.wait_ge(S("ct0"), 6)
            for n in range(2):
                for a in range(2):
                    read_out(pe, ("m0", "O", n, a))
            proj_out(("wout0a", "wout0b"), "wout0", (0, 1, 2, 3), None)

            def rows_to_cols(tag):
                pe.wait_ge(S("rows_" + tag), TM)
                for q in range(4):
                    p = unit(pe, ("T" + tag, q), q)
                    for k in (2 * q, 2 * q + 1):
                        for m in range(TM):
                            last = transpose(p[:, (k % 2) * T + m * P:(k % 2) * T + (m + 1) * P],
                                             HS[:, m, k * P:(k + 1) * P])
                    ready(last, ("T" + tag, q))

            rows_to_cols("f0")
            for q in range(4):
                read_out(pe, ("Tf0", q))
            for c in range(len(FCH) + 1):
                if c < len(FCH):
                    sg_, su_ = item(f"g{c}"), item(f"u{c}")
                    nf = FCH[c] // P
                    for f in range(nf):
                        p = unit(pe, ("h", c, f), (4 * c + f) % 4)
                        for h, s in enumerate((sg_, su_)):
                            for k in range(KT):
                                last = mm(p[:, h * T:(h + 1) * T], lhsT=s[:, k * FCH[c] + f * P:k * FCH[c] + (f + 1) * P],
                                          rhs=HT[:, k], start=(k == 0 and h == 0), stop=(k == KT - 1),
                                          skip_group_check=True)
                        ready(last, ("h", c, f))
                    item_done[f"g{c}"] = item_done[f"u{c}"] = units[("h", c, nf - 1)]
                if c >= 1:
                    s = item(f"d{c - 1}")
                    nf = FCH[c - 1] // P
                    if c == 1:
                        acc = [unit(pe, ("ffn", b), 4 + b) for b in range(4)]
                    for f in range(nf):
                        read_out(pe, ("h", c - 1, f))
                    for f in range(nf):
                        for m in range(TM):
                            for n in range(2):
                                last = mm(acc[2 * n + m][:, :], lhsT=HID0[:, (c - 1) % 2, f, m * P:(m + 1) * P],
                                          rhs=s[:, f * D + n * 512:f * D + (n + 1) * 512],
                                          start=(c == 1 and f == 0), stop=(c == len(FCH) and f == nf - 1))
                                if c == len(FCH) and f == nf - 1:
                                    ready(last, ("ffn", 2 * n + m))
                    if c < len(FCH):
                        last.then_inc(S("down0"), 1)
                        item_done[f"d{c - 1}"] = c
                    else:
                        item_done[f"d{c - 1}"] = units[("ffn", 3)]
            rows_to_cols("kv")
            for q in range(4):
                read_out(pe, ("Tkv", q))
            proj_kv("kv", CT, "kv", (4, 5))
            proj_rows(("win1a", "win1b"), HT, "win1", (0, 1, 2, 3))
            pe.wait_ge(S("kv_rows"), 1)
            for m in range(TM):
                p = unit(pe, ("kvT", m), 4 + m)
                for h in range(4):
                    last = transpose(p[0:HD, h * P:(h + 1) * P], KVR[:, m, h * HD:(h + 1) * HD])
                ready(last, ("kvT", m))
            pe.wait_ge(S("q1_rows"), 1)
            for n in range(8):
                m, hq = n % 2, n // 2
                p = unit(pe, ("q1T", n), 4 + n % 4)
                for a in range(4):
                    h = hq * 4 + a
                    last = transpose(p[0:HD, a * P:(a + 1) * P], HS[:, m, h * HD:(h + 1) * HD])
                ready(last, ("q1T", n))
            for m in range(TM):
                read_out(pe, ("kvT", m))
                read_out(pe, ("mkT", 1, m))
            for n in range(8):
                read_out(pe, ("q1T", n))
            lg, fl, ou, ng = attention("a1", A1_HEADS, QT1, lambda h: h < 12, PB1, PT1, ((0, 1, 2, 3), (6, 7)))
            for n in range(ng + 2):
                if n < ng:
                    lg(n)
                if 1 <= n <= ng:
                    fl(n - 1)
                    ou(n - 1)
            for n in range(ng):
                for a in range(2):
                    read_out(pe, ("a1", "O", n, a))
            proj_out(("wout1a", "wout1b"), "wout1", (0, 1, 2, 3), None)
            rows_to_cols("f1")
            for q in range(4):
                read_out(pe, ("Tf1", q))
            pe.wait_ge(S("ld_router"), 16)
            p = unit(pe, "router", 4)
            for m in range(TM):
                for k in range(KT):
                    last = mm(p[:, m * NE:(m + 1) * NE], lhsT=HT[:, k, m * P:(m + 1) * P], rhs=ROUT[:, k],
                              start=(k == 0), stop=(k == KT - 1), skip_group_check=True)
            ready(last, "router")
            pe.wait_ge(S("sel"), 1)
            pe.wait_ge(S("tri"), 3)
            p = unit(pe, "place", 5)
            for col, terms in ((0, ((TRI, 0),)), (1, ((ONES, 0), (TRI, 1))), (2, ((ONES, 0), (ONES, 1)))):
                for q, (mat, m) in enumerate(terms):
                    last = mm(p[:, col * NE:(col + 1) * NE], lhsT=mat, rhs=SEL[:, m],
                              start=(q == 0), stop=(q == len(terms) - 1), skip_group_check=True)
            ready(last, "place")

            y_base = [0, 0]

            def gather(turn, key):
                for b in range(2):
                    p = unit(pe, (key, "xg", b), 6 + b, turn)
                    for kk_ in range(4):
                        k = 4 * b + kk_
                        for m in range(TM):
                            last = mm(p[:, kk_ * CAP:(kk_ + 1) * CAP], lhsT=HS[:, m, k * P:(k + 1) * P],
                                      rhs=PICK[:, m], start=(kk_ == 0 and m == 0), stop=(m == TM - 1),
                                      skip_group_check=True)
                    ready(last, (key, "xg", b))

            def y_rows(turn, key, bt):
                for b in range(2):
                    pe.wait_ge(bank_free[4 + b], uses[4 + b] if bt is None else bt.value(y_base[b], 1))
                for b in range(2):
                    p = unit(pe, (key, "yt", b), 6 + b, bt)
                    for a in range(4):
                        last = transpose(p[0:CAP, a * P:(a + 1) * P], YT[:, 4 * b + a])
                    ready(last, (key, "yt", b))

            def scatter(turn, key, bt):
                for b in range(2):
                    read_out(pe, (key, "yt", b), bt)
                for n in range(2):
                    for m in range(TM):
                        p = unit(pe, (key, "sc", n, m), 6 + m, bt)
                        last = mm(p[:, :], lhsT=GATE[0:CAP, m * P:(m + 1) * P], rhs=YR[0:CAP, n * 512:(n + 1) * 512],
                                  start=True, stop=True)
                        ready(last, (key, "sc", n, m))

            def expert(turn, key):
                def weights(q):
                    pe.wait_ge(full[e_slot(q)], turn.weights(e_need(q)))
                    return at(e_slot(q) * SLOT, SLOT)

                def hidden(c, q):
                    for h in range(2):
                        s = weights(q + h)
                        p = unit(pe, (key, "gu", c, h), 2 * (c % 2) + h, turn)
                        for f in range(4):
                            for k in range(KT):
                                last = mm(p[:, f * CAP:(f + 1) * CAP], lhsT=s[:, k * 512 + f * P:k * 512 + (f + 1) * P],
                                          rhs=XG[:, k], start=(f == 0 and k == 0), stop=(k == KT - 1),
                                          skip_group_check=True)
                        ready(last, (key, "gu", c, h))

                def down(c, q, acc):
                    s = weights(q)
                    read_out(pe, (key, "gu", c, 1), turn)
                    for f in range(4):
                        for d in range(KT):
                            last = mm(acc[d // 4][:, (d % 4) * CAP:(d % 4 + 1) * CAP],
                                      lhsT=s[:, f * D + d * P:f * D + (d + 1) * P], rhs=HID[:, c % 2, f],
                                      start=(c == 0 and f == 0 and d % 4 == 0),
                                      stop=(c == NC_E - 1 and f == 3), skip_group_check=True)
                            if c == NC_E - 1 and f == 3 and d % 4 == 3:
                                ready(last, (key, "y", d // 4))
                    if c < NC_E - 1:
                        last.then_inc(S("down1"), 1)

                for b in range(2):
                    pe.wait_ge(bank_free[6 + b], turn.value(uses[6 + b], PER[6 + b]))
                q = 0
                for c in range(NC_E):
                    hidden(c, q)
                    q += 2
                    if c == 0:
                        y_rows(turn, key, turn)
                    if c == 1:
                        scatter(turn, key, turn)
                        acc = [unit(pe, (key, "y", b), 4 + b, turn) for b in range(2)]
                    if c == 3:
                        pe.wait_ge(S("pgate"), turn.count("pgate", 1))
                        p = unit(pe, (key, "gt"), 6, turn)
                        for m in range(TM):
                            last = transpose(p[0:CAP, m * P:(m + 1) * P], PG[:, m])
                        ready(last, (key, "gt"))
                    if c == NC_E - 1:
                        pe.wait_ge(S("pick"), turn.count("pick", 1))
                        gather(turn, key)
                    if c >= 1:
                        down(c - 1, q, acc)
                        q += 1
                down(NC_E - 1, q, acc)

            pe.wait_ge(S("pick"), 1)
            gather(None, "first")

            def passes(key, first, end):
                base = list(uses)
                y_base[:] = uses[4:6]
                with pe.Fori(first, end) as i:
                    expert(Turn(i, first), key)
                for b in range(8):
                    assert uses[b] - base[b] == PER[b], (b, uses[b] - base[b])
                    uses[b] = base[b] + PER[b] * (end - first)
                y_rows(Turn(end, first), (key, "end"), None)
                scatter(Turn(end, first), (key, "end"), None)

            passes("main", 0, NE)
            pe.wait_ge(S("flag"), 1)
            over = pe.value_load(flag[0:1, 0:1], min_val=0, max_val=1)
            with pe.If(over > 0):
                pe.wait_ge(S("gate_zero"), 1)
                passes("over", NE, PASSES * NE)

        @block.sync
        def _(sp):
            def used(n):
                d = item_done[NAMES[n]]
                if isinstance(d, int):
                    sp.wait_ge(S("down0"), d)
                else:
                    sp.wait_ge(bank_full[d[0]], d[1] + 1)

            def e_used(turn, q, key):
                kind, c = items[q]
                if kind == "d" and c < NC_E - 1:
                    sp.wait_ge(S("down1"), turn.count("down1", c + 1))
                else:
                    k = (key, "y", 1) if kind == "d" else (key, "gu", c, "gu".index(kind))
                    got(sp, k, turn)

            def load_static(n):
                for dst, src in stream[n][1]:
                    sp.dma_start(dst(at(slot_of(n) * SLOT, SLOT)), src).then_inc(full[slot_of(n)], 16)

            for n in range(NA):
                s = slot_of(n)
                prev = [q for q in range(n) if slot_of(q) == s]
                if prev:
                    used(prev[-1])
                    if NAMES[n] in ("glua", "glub"):
                        got(sp, ("Ug", 2))
                else:
                    if n >= 6:
                        got(sp, ("yT", 2))
                load_static(n)

            def load_expert(e, q):
                kind, c = items[q]
                slot = at(e_slot(q) * SLOT, SLOT)
                if kind == "d":
                    src = w["l1_moe_w_down"][bass.ds(e, 1), c * 512:(c + 1) * 512, :].rearrange("e (k p) n -> p (e k) n", p=P)
                    sp.dma_start(slot.rearrange("p (k n) -> p k n", n=D), src).then_inc(full[e_slot(q)], 16)
                else:
                    src = w["l1_moe_w_gate" if kind == "g" else "l1_moe_w_up"][bass.ds(e, 1), :, c * 512:(c + 1) * 512] \
                        .rearrange("e (k p) n -> p (e k) n", p=P)
                    sp.dma_start(slot.rearrange("p (k n) -> p k n", n=512), src).then_inc(full[e_slot(q)], 16)

            for q in range(NSLOT):
                used(max(n for n in range(NA) if slot_of(n) == e_slot(q)))
                load_expert(0, q)

            def passes(key, first, end):
                with sp.Fori(first, end) as i:
                    turn = Turn(i, first)
                    for q in range(NSLOT, NI):
                        e_used(turn, q - NSLOT, key)
                        load_expert(i if first == 0 else i % NE, q)
                    for q in range(NSLOT):
                        e_used(turn, NI - NSLOT + q, key)
                        load_expert((i + 1) % NE, q)

            passes("main", 0, NE)
            sp.wait_ge(S("flag"), 1)
            over = sp.value_load(flag[0:1, 0:1], min_val=0, max_val=1)
            with sp.If(over > 0):
                passes("over", NE, PASSES * NE)
            sp.wait_ge(S("x_final"), 1)
            sp.dma_start(out[0].rearrange("(m p) n -> p m n", p=P), XS).then_inc(S("stored"), 16)
            sp.wait_ge(S("stored"), 16)

        @block.gpsimd
        def _(pool):
            g = nc.gpsimd
            n_chain = [0]

            def link(ins):
                n_chain[0] += 1
                ins.then_inc(S("pool_chain"), 1)
                pool.wait_ge(S("pool_chain"), n_chain[0])

            g.iota(iota, pattern=[[1, CAP]], base=0, channel_multiplier=0, allow_small_or_imprecise_dtypes=True).then_inc(S("iota"), 1)
            link(g.memset(ident, 0.0))
            link(g.affine_select(out=ident, in_=ident, compare_op=ALU.not_equal, fill=1.0, base=0,
                                 pattern=[[-1, P]], channel_multiplier=1))
            g.memset(mh, -0.5).then_inc(S("ident"), 1)
            g.memset(ebase, math.e).then_inc(S("ident"), 1)
            pool.wait_ge(S("ident"), 2)

            def root(tag, n, src, dst, width):
                pool.wait_ge(S("ss_" + tag), n)
                link(g.tensor_scalar(src, src, 1.0 / width, EPS, ALU.mult, ALU.add))
                g.tensor_tensor(dst, src, mh[:, 0:src.shape[-1]], ALU.pow).then_inc(S("rs_" + tag), 1)

            root("mem", 2, ss[:, 0:2], rs[:, 0:2], D)
            pool.wait_ge(S("ld_lam"), 48)
            g.tensor_tensor(edt, ebase[:, 0:2], ldt, ALU.pow).then_inc(S("dt"), 1)
            pool.wait_ge(S("zr"), 1)
            g.tensor_tensor(er, ebase, zr, ALU.pow).then_inc(S("er"), 1)
            root("x0", 2, ss[:, 2:4], rs[:, 2:4], D)
            pool.wait_ge(S("ld_d"), 32)
            link(g.tensor_tensor(mask16, ident[0:32, 0:GDIM], ident[0:32, GDIM:32], ALU.add))
            g.tensor_tensor(MD, Dbc, mask16.unsqueeze(1).to_broadcast([32, PAIRS, GDIM]), ALU.mult).then_inc(S("skip"), 1)
            link(g.memset(W0bd, 0.0))

            def complex_sums(dst, tag, n0, ops):
                for n in range(PAIRS // 2):
                    pool.wait_ge(S("prods"), 4 * (n0 + n + 1))
                    b = (n0 + n) % 2
                    for ri in range(2):
                        last = g.tensor_tensor(dst[:, ri, 2 * n:2 * n + 2], prod[:, b, 2 * ri].rearrange("p (j c) -> p j c", j=2),
                                               prod[:, b, 2 * ri + 1].rearrange("p (j c) -> p j c", j=2), ops[ri])
                        if ri:
                            last.then_inc(S("s5_" + tag), 1)

            complex_sums(Wt, "w", 0, (ALU.subtract, ALU.add))
            pool.wait_ge(S("s5_w"), 12)
            for ri in range(2):
                for g2 in range(2):
                    g.tensor_copy(W0bd[g2 * 64:(g2 + 1) * 64, ri, :, g2 * GDIM:(g2 + 1) * GDIM],
                                  Wt[g2 * 64:(g2 + 1) * 64, ri, :, 7 * GDIM:8 * GDIM]).then_inc(S("s5_w0"), 1)
                    pool.wait_ge(S("s5_w0"), 2 * ri + g2 + 1)
            complex_sums(CA, "ca", 12, (ALU.add, ALU.subtract))
            root("mk", 1, hss[:, 0:16], hrs[:, 0:16], HD)
            for l in range(2):
                for m in range(TM):
                    read_out(pool, ("mkT", l, m))
            g.memset(Tm, 0.0).then_inc(S("tm_zero"), 1)
            root("q0", 1, hss[:, 16:24], hrs[:, 16:24], HD)
            for s in (2, 5):
                pool.wait_ge(S(f"u_step{s}"), 32)
                g.tensor_copy(U5[:, :, s * GDIM:(s + 1) * GDIM], U4[:, s].rearrange("p (g i) -> p g i", i=GDIM)).then_inc(S("u5_pool"), 1)
            for n in range(3):
                read_out(pool, ("Ug", n))
            g.memset(Xbd, 0.0).then_inc(S("xbd_zero"), 1)
            root("f0", 2, ss[:, 0:2], rs[:, 0:2], D)
            got(pool, ("yT", 2))
            link(g.memset(TRI, 1.0))
            g.memset(ONES, 1.0).then_inc(S("tri"), 1)
            link(g.memset(MSK, 0.0))
            g.affine_select(out=TRI, in_=TRI, compare_op=ALU.is_gt, fill=0.0, base=0,
                            pattern=[[1, P]], channel_multiplier=-1).then_inc(S("tri"), 1)
            g.affine_select(out=MSK, in_=MSK, compare_op=ALU.is_ge, fill=NEG, base=0,
                            pattern=[[-1, P]], channel_multiplier=1).then_inc(S("tri"), 1)
            root("kv", 2, ss[:, 2:4], rs[:, 2:4], D)
            root("kvh", 1, hss[:, 0:8], hrs[:, 0:8], HD)
            root("q1", 1, hss[:, 8:40], hrs[:, 8:40], HD)
            root("f1", 2, ss[:, 0:2], rs[:, 0:2], D)

        @block.scalar
        def _(act):
            ac = nc.scalar.activation

            def load(dst, src, sem):
                act.dma_start(dst, src).then_inc(S(sem), 16)

            for m in range(TM):
                load(HS[:, m], w["mem"][0, m * P:(m + 1) * P, :], f"ld_mem{m}")
            load(lam_r.rearrange("j (g p) -> j g p", g=2), w["l0_s5_lam_re"].rearrange("(g j) p -> j g p", g=2), "ld_lam")
            load(lam_i.rearrange("j (g p) -> j g p", g=2), w["l0_s5_lam_im"].rearrange("(g j) p -> j g p", g=2), "ld_lam")
            load(ldt, w["l0_s5_log_dt"].rearrange("(g j) -> j g", g=2), "ld_lam")
            for r, name in ((G_MIX0, "l0_mix_norm"), (G_MEM0, "l0_mem_norm"), (G_FFN0, "l0_ffn_norm"), (G_KV, "kv_norm"),
                            (G_MIX1, "l1_mix_norm"), (G_MEM1, "l1_mem_norm"), (G_FFN1, "l1_ffn_norm")):
                load(grow[r:r + 8, :], w[name].rearrange("(r p) -> r p", p=P), "ld_gains")
            load(grow[G_BGLU:G_BGLU + 6, :], w["l0_s5_b_glu"].rearrange("(r p) -> r p", p=P), "ld_gains")
            for m in range(TM):
                load(XS[:, m], w["x"][0, m * P:(m + 1) * P, :], f"ld_x{m}")
            for ri, name in enumerate(("l0_s5_b_re", "l0_s5_b_im")):
                for g2 in range(2):
                    load(braw[g2 * 64:(g2 + 1) * 64, ri], w[name][g2 * PAIRS:(g2 + 1) * PAIRS].rearrange("j p i -> p j i"), "ld_b")
            for ri, name in enumerate(("l0_s5_c_re", "l0_s5_c_im")):
                for g2 in range(2):
                    load(cnat[:, ri, :, g2 * 64:(g2 + 1) * 64],
                         w[name][g2 * PAIRS:(g2 + 1) * PAIRS].rearrange("(a jj) o p -> (jj o) a p", a=3), "ld_c")
            for g2 in range(2):
                load(Dbc[g2 * GDIM:(g2 + 1) * GDIM], w["l0_s5_d"][g2 * PAIRS * GDIM:(g2 + 1) * PAIRS * GDIM]
                     .rearrange("(a j o) -> a j o", a=1, o=GDIM).to_broadcast([GDIM, PAIRS, GDIM]), "ld_d")
            for n, name in enumerate(("l0_mem_q_gain", "l0_mem_k_gain", "l1_mem_q_gain", "l1_mem_k_gain", "l1_moba_q_gain")):
                load(hg[:, n:n + 1], w[name].rearrange("(p a) -> p a", a=1), "ld_hg")
            load(hgk, w["kv_k_gain"].rearrange("(p a) -> p a", a=1), "ld_hg")
            load(ROUT, w["l1_moe_router"].rearrange("(k p) e -> p k e", p=P), "ld_router")

            def square(src, tag, col, ld=None):
                for m in range(TM):
                    if ld:
                        act.wait_ge(S(f"{ld}{m}"), 16)
                    ac((at(32768, TM, D) if src is HS else HS)[:, m], src[:, m], ACT.Square,
                       accum_out=ss[:, col + m:col + m + 1]).then_inc(S("ss_" + tag), 1)

            def scale_rows(src, tag, col, done):
                act.wait_ge(S("rs_" + tag), 1)
                for m in range(TM):
                    ac(HS[:, m], src[:, m], ACT.Copy, scale=rs[:, col + m:col + m + 1]).then_inc(S(done), 1)

            square(HS, "mem", 0, "ld_mem")
            p = got(act, "gT")
            free(ac(gT, p[:, 0:G_ROWS], ACT.Copy), "gT")
            scale_rows(HS, "mem", 0, "mem_rows")
            act.wait_ge(S("ang"), 1)
            ac(sn, rr, ACT.Sin).then_inc(S("sin"), 1)
            act.wait_ge(S("ang"), 2)
            ac(cs, kk, ACT.Sin).then_inc(S("sin"), 1)

            def gains_out(key, q, outs):
                p = got(act, (key, q))
                for dst, row in outs:
                    for a in range(2):
                        k = 2 * q + a
                        last = ac(dst[:, k], p[:, a * T:(a + 1) * T], ACT.Copy, scale=gT[:, row + k:row + k + 1])
                free(last, (key, q))

            read_out(act, "gT")
            for q in range(4):
                gains_out("memT", q, [(CT, G_MEM0), (HT, G_MEM1)])
            for ri in range(2):
                p = got(act, ("cT", ri))
                free(ac(cT[:, ri], p[:, 0:PAIRS * GDIM], ACT.Copy, scale=1.0 if ri == 0 else -1.0), ("cT", ri))
            square(XS, "x0", 2, "ld_x")
            scale_rows(XS, "x0", 2, "x_rows0")

            def kv_out(tag, rows, vals):
                for m in range(TM):
                    p = got(act, (tag, m))
                    ac(rows(m), p[:, 0:256], ACT.Copy)
                    free(ac(vals(m), p[:, 256:512], ACT.Copy), (tag, m))

            kv_out("mkv1", lambda m: mkrow(1, m), lambda m: vM[1][:, m])
            for q in range(4):
                gains_out("xT0", q, [(HT, G_MIX0)])
            kv_out("mkv0", lambda m: mkrow(0, m), lambda m: vM[0][:, m])
            for h in range(2):
                for m in range(TM):
                    p = got(act, ("win0", h, m))
                    free(ac(HS[:, m, h * 512:(h + 1) * 512], p[:, :], ACT.Copy), ("win0", h, m))
            act.wait_ge(S("gp"), 3)
            for l in (1, 0):
                for m in range(TM):
                    p = got(act, ("mkT", l, m))
                    free(ac(kT[l][:, :, m * P:(m + 1) * P], p[0:HD, :].rearrange("p (h t) -> p h t", h=4), ACT.Copy,
                            scale=gp[:, l:l + 1]), ("mkT", l, m))
            for n in range(12):
                p = got(act, ("Bm", n))
                ri, jq = n // 6, n % 6
                free(ac(Bm[:, ri, jq * 4:jq * 4 + 4], p[:, :].rearrange("p (a c) -> p a c", a=4), ACT.Copy), ("Bm", n))
            for jq in range(6):
                p = got(act, ("K", jq))
                free(ac(Kst[:, jq * 4:jq * 4 + 4], p[0:32, :].rearrange("p (a c) -> p a c", a=4), ACT.Copy), ("K", jq))
            act.wait_ge(S("kst_d"), 1)
            act.wait_ge(S("tm_zero"), 1)
            Tv = Tm.rearrange("p (g j) c -> p g j c", g=2)
            for s in range(STEPS):
                for g2 in range(2):
                    act.dma_start(Tv[s * GDIM:(s + 1) * GDIM, g2, :, s * GDIM:P],
                                  Kst[g2 * GDIM:(g2 + 1) * GDIM, :, 0:P - s * GDIM]).then_inc(S("tm"), 16)
            for h in range(2):
                for m in range(TM):
                    read_out(act, ("win0", h, m))
            act.wait_ge(S("tm"), 16 * 16)
            for s in range(STEPS):
                for m in range(TM):
                    act.dma_start(U4[m * 16:(m + 1) * 16, s], HS[s:P:STEPS, m, 0:MAIN]).then_inc(S(f"u_step{s}"), 16)
            for s in (0, 3, 6):
                act.wait_ge(S(f"u_step{s}"), 32)
                ac(U5[:, :, s * GDIM:(s + 1) * GDIM], U4[:, s].rearrange("p (g i) -> p g i", i=GDIM), ACT.Copy).then_inc(S("u5_act"), 1)
            for n in range(3):
                p = got(act, ("Ug", n))
                free(ac(Ug[:, n * 16:(n + 1) * 16], p[:, :].rearrange("p (a c) -> p a c", a=16), ACT.Copy), ("Ug", n))
            for n in range(3):
                p = got(act, ("V", n))
                dst, src = (VX[:, n, 0:16], p[:, :].rearrange("p (j c) -> p j c", c=CHUNKS)) if n < 2 else \
                    (VX[:, :, 16:24], p[:, :].rearrange("p (r j c) -> p r j c", r=2, c=CHUNKS))
                free(ac(dst, src, ACT.Copy), ("V", n))
            for m in range(TM):
                p = got(act, ("q0T", m))
                free(ac(QT0[:, :, m * P:(m + 1) * P], p[0:HD, :].rearrange("p (h t) -> p h t", h=4), ACT.Copy), ("q0T", m))
            act.wait_ge(S("scan"), 1)
            act.wait_ge(S("xbd_zero"), 1)
            for g2 in range(2):
                ac(Xbd[g2 * 64:(g2 + 1) * 64, 1, :, g2 * 32 + 1:g2 * 32 + 32], VX[g2 * 64:(g2 + 1) * 64, 1, :, 0:31],
                   ACT.Copy).then_inc(S("xbd"), 1)
            for n in range(1, 6, 2):
                p = got(act, ("Y", n))
                free(ac(Ysb[:, :, n * 64:(n + 1) * 64].rearrange("p k (a o) -> p k a o", a=4),
                        p[0:64, :].rearrange("p (a k o) -> p k a o", a=4, k=STEPS), ACT.Copy), ("Y", n))
            for n in range(3):
                p = got(act, ("yT", n))
                for g2 in range(2):
                    last = ac(GT6[:, g2 * 3 + n].rearrange("p (c k) -> p c k", k=STEPS),
                              p[:, :].rearrange("p (k g c) -> p g c k", k=STEPS, g=2)[:, g2], ACT.Gelu_apprx_tanh)
                free(last, ("yT", n))

            def softmax(tag, n, pbuf, masked):
                for a in range(2):
                    act.wait_ge(S(tag + "_max"), 2 * n + a + 1)
                    p = PS_OF(tag, n, a)
                    for m in range(TM):
                        nk = P * (m + 1) if masked(2 * n + a) else T
                        c = 2 * a + m
                        last = ac(pbuf[:, (n % 2) * 2 + a, m * T:m * T + nk], p[:, m * T:m * T + nk], ACT.Exp,
                                  bias=snm[:, n % 2, c:c + 1], accum_out=ssum[:, n % 2, c:c + 1])
                    free(last, (tag, "L", n, a))

            def PS_OF(tag, n, a):
                return PS[units[(tag, "L", n, a)][0]]

            def pt_out(tag, n, pt, masked):
                for a in range(2):
                    p = got(act, (tag, "PT", n, a))
                    d = pt[:, (n % 2) * 2 + a]
                    if masked(2 * n + a):
                        ac(d[:, 0:T], p[:, 0:T], ACT.Copy)
                        last = ac(d[:, T + P:2 * T], p[:, T + P:2 * T], ACT.Copy)
                    else:
                        last = ac(d, p[:, :], ACT.Copy)
                    free(last, (tag, "PT", n, a))

            for n in range(2):
                softmax("m0", n, PB0, lambda h: False)
            for n in range(6):
                if n >= 2:
                    act.wait_ge(S("ct0"), n - 1)
                p = got(act, ("glu", n))
                free(ac(SIG[:, n % 2], p[:, 0:T], ACT.Sigmoid, bias=gT[:, G_BGLU + n:G_BGLU + n + 1]), ("glu", n))
            for n in range(2):
                pt_out("m0", n, PT0, lambda h: False)

            def cols_out(tag, outs):
                for q in (1, 3):
                    gains_out("T" + tag, q, outs)

            def norm(tag, col, parts):
                for key in parts:
                    read_out(act, key)
                square(XS, tag, col)
                scale_rows(XS, tag, col, "rows_" + tag)

            norm("f0", 0, [("wout0", h, m) for h in range(2) for m in range(TM)])
            cols_out("f0", [(HT, G_FFN0)])
            n = 0
            for c in range(len(FCH)):
                for f in range(FCH[c] // P):
                    p = got(act, ("h", c, f))
                    ac(SG0[:, n % 4], p[:, 0:T], ACT.Silu).then_inc(S("sg0"), 1)
                    n += 1
            norm("kv", 2, [("ffn", b) for b in range(4)])
            cols_out("kv", [(CT, G_KV), (HT, G_MIX1)])
            kv_out("kv", lambda m: KVR[:, m], lambda m: VKV[:, m])
            for h in range(2):
                for m in range(TM):
                    p = got(act, ("win1", h, m))
                    free(ac(HS[:, m, h * 512:(h + 1) * 512], p[:, :], ACT.Copy), ("win1", h, m))
            for m in range(TM):
                p = got(act, ("kvT", m))
                free(ac(kTkv[:, :, m * P:(m + 1) * P], p[0:HD, :].rearrange("p (h t) -> p h t", h=4), ACT.Copy,
                        scale=gp[:, 2:3]), ("kvT", m))
            for n in range(1, 8, 2):
                p = got(act, ("q1T", n))
                free(ac(QT1[:, (n // 2) * 4:(n // 2) * 4 + 4, (n % 2) * P:(n % 2 + 1) * P],
                        p[0:HD, :].rearrange("p (h t) -> p h t", h=4), ACT.Copy), ("q1T", n))
            for n in range(9):
                if n < 8:
                    softmax("a1", n, PB1, lambda h: h < 12)
                if n >= 1:
                    pt_out("a1", n - 1, PT1, lambda h: h < 12)
            norm("f1", 0, [("wout1", h, m) for h in range(2) for m in range(TM)])
            cols_out("f1", [(HT, G_FFN1)])
            act.wait_ge(S("rt_d"), 1)
            ac(EX, LG, ACT.Exp).then_inc(S("rt_e"), 1)

            def xg_out(turn, key):
                p = got(act, (key, "xg", 1), turn)
                for a in range(4):
                    last = ac(XG[:, 4 + a], p[:, a * CAP:(a + 1) * CAP], ACT.Copy, scale=gT[:, G_FFN1 + 4 + a:G_FFN1 + 5 + a])
                free(last, (key, "xg", 1))

            def yr_out(turn, key, bt):
                p = got(act, (key, "yt", 1), bt)
                free(ac(YR[0:CAP, 512:1024], p[0:CAP, :], ACT.Copy), (key, "yt", 1))

            def expert(turn, key):
                for c in range(NC_E):
                    p = got(act, (key, "gu", c, 0), turn)
                    free(ac(SG1[:, c % 2], p[:, 0:4 * CAP], ACT.Silu), (key, "gu", c, 0))
                    if c == 0:
                        yr_out(turn, key, turn)
                    if c == 4:
                        p = got(act, (key, "gt"), turn)
                        free(ac(GATE[0:CAP], p[0:CAP, 0:T], ACT.Copy), (key, "gt"))
                xg_out(turn, key)
                p = got(act, (key, "y", 1), turn)
                free(ac(YT[:, 4:8], p[:, 0:4 * CAP].rearrange("p (a t) -> p a t", a=4), ACT.Copy), (key, "y", 1))

            xg_out(None, "first")

            def passes(key, first, end):
                with act.Fori(first, end) as i:
                    expert(Turn(i, first), key)
                yr_out(Turn(end, first), (key, "end"), None)

            passes("main", 0, NE)
            act.wait_ge(S("flag"), 1)
            over = act.value_load(flag[0:1, 0:1], min_val=0, max_val=1)
            with act.If(over > 0):
                passes("over", NE, PASSES * NE)

        @block.vector
        def _(dve):
            v = nc.vector
            n_chain = [0]

            def link(ins):
                n_chain[0] += 1
                ins.then_inc(S("dve_chain"), 1)
                dve.wait_ge(S("dve_chain"), n_chain[0])
                return ins

            tt, tsc = v.tensor_tensor, v.tensor_scalar

            def bc2(x):
                return x.unsqueeze(2).to_broadcast([PAIRS, 2, NSTATE])

            def v2(x):
                return x.rearrange("p (g s) -> p g s", g=2)

            dve.wait_ge(S("ld_lam"), 48)
            dve.wait_ge(S("dt"), 1)
            tt(v2(zr), v2(lam_r), bc2(edt), ALU.mult).then_inc(S("zr"), 1)
            link(tt(v2(zi), v2(lam_i), bc2(edt), ALU.mult))
            link(tsc(kk, zi, 1.0 / (2 * math.pi), None, ALU.mult))
            link(tsc(kk, kk, 12582912.0, None, ALU.add))
            link(tsc(kk, kk, -12582912.0, None, ALU.add))
            c1 = 6.28125
            c2 = 0.0019350051879882812
            c3 = 2 * math.pi - c1 - c2
            link(v.scalar_tensor_tensor(out=rr, in0=kk, scalar=-c1, in1=zi, op0=ALU.mult, op1=ALU.add))
            link(v.scalar_tensor_tensor(out=rr, in0=kk, scalar=-c2, in1=rr, op0=ALU.mult, op1=ALU.add))
            link(v.scalar_tensor_tensor(out=rr, in0=kk, scalar=-c3, in1=rr, op0=ALU.mult, op1=ALU.add))
            pi = 3.1415925
            link(tsc(rr, rr, -pi, pi, ALU.max, ALU.min))
            tsc(t0, rr, -1.0, None, ALU.mult).then_inc(S("ang"), 1)
            dve.wait_ge(S("ang"), 1)
            link(tt(t0, t0, rr, ALU.max))
            tsc(kk, t0, -1.0, math.pi / 2, ALU.mult, ALU.add).then_inc(S("ang"), 1)
            link(tt(t1, lam_r, lam_r, ALU.mult))
            link(tt(t2, lam_i, lam_i, ALU.mult))
            link(tt(t1, t1, t2, ALU.add))
            link(v.reciprocal(zi, t1))
            dve.wait_ge(S("er"), 1)
            dve.wait_ge(S("sin"), 2)
            link(tt(pw[:, 0, 0], er, cs, ALU.mult))
            link(tt(pw[:, 1, 0], er, sn, ALU.mult))
            link(tsc(t0, pw[:, 0, 0], -1.0, None, ALU.add))
            ai = pw[:, 1, 0]
            link(tt(t1, t0, lam_r, ALU.mult))
            link(tt(t2, ai, lam_i, ALU.mult))
            link(tt(t1, t1, t2, ALU.add))
            link(tt(fr, t1, zi, ALU.mult))
            link(tt(t1, ai, lam_r, ALU.mult))
            link(tt(t2, t0, lam_i, ALU.mult))
            link(tt(t1, t1, t2, ALU.subtract))
            link(tt(fi, t1, zi, ALU.mult))

            def cmul(dr, di, ar, ai_, br, bi, n):
                w0, w1 = (x[:, 0:n * P].rearrange("p (n c) -> p n c", n=n) for x in (u0, u1))
                b_ = lambda x: x.unsqueeze(1).to_broadcast([PAIRS, n, P])
                tt(w0, ar, b_(br), ALU.mult)
                link(tt(w1, ai_, b_(bi), ALU.mult))
                link(tt(dr, w0, w1, ALU.subtract))
                tt(w0, ar, b_(bi), ALU.mult)
                link(tt(w1, ai_, b_(br), ALU.mult))
                return link(tt(di, w0, w1, ALU.add))

            cmul(pw[:, 0, 1:2], pw[:, 1, 1:2], pw[:, 0, 0:1], pw[:, 1, 0:1], pw[:, 0, 0], pw[:, 1, 0], 1)
            cmul(pw[:, 0, 2:4], pw[:, 1, 2:4], pw[:, 0, 0:2], pw[:, 1, 0:2], pw[:, 0, 1], pw[:, 1, 1], 2)
            cmul(pw[:, 0, 4:8], pw[:, 1, 4:8], pw[:, 0, 0:4], pw[:, 1, 0:4], pw[:, 0, 3], pw[:, 1, 3], 4)
            v.tensor_copy(cm[:, 0, 7], fr)
            link(v.tensor_copy(cm[:, 1, 7], fi))
            for s0, n in ((3, 4), (0, 3)):
                for s in range(s0, s0 + n):
                    m = 7 - s
                    cmul(cm[:, 0, s:s + 1], cm[:, 1, s:s + 1], pw[:, 0, m - 1:m], pw[:, 1, m - 1:m], fr, fi, 1)
            tsc(t0[0:1, 0:1], t0[0:1, 0:1], 1.0, None, ALU.mult).then_inc(S("s5_cm"), 1)
            tsc(t1[0:1, 0:1], t1[0:1, 0:1], 1.0, None, ALU.mult).then_inc(S("s5_pw"), 1)

            def products(bank, key, x, n0, combos, tag):
                p = got(dve, key)
                fac = p[:, 0:16 * PAIRS].rearrange("p (r n j) -> p r j n", r=2, n=8)
                for n in range(PAIRS // 2):
                    t = n0 + n
                    if t >= 2:
                        dve.wait_ge(S("s5_w") if t - 2 < 12 else S("s5_ca"), t - 1 if t - 2 < 12 else t - 13)
                    for q, (fri, xri) in enumerate(combos):
                        last = tt(prod[:, t % 2, q].rearrange("p (j n i) -> p j n i", j=2, n=8),
                                  fac[:, fri, 2 * n:2 * n + 2].unsqueeze(3).to_broadcast([P, 2, 8, GDIM]),
                                  x[:, xri, 2 * n:2 * n + 2].unsqueeze(2).to_broadcast([P, 2, 8, GDIM]), ALU.mult)
                        last.then_inc(S("prods"), 1)
                return p, last

            dve.wait_ge(S("ld_b"), 64)
            p, last = products(6, "q_cm", braw, 0, ((0, 0), (1, 1), (0, 1), (1, 0)), "w")
            for ri in range(2):
                read_out(dve, ("cT", ri))
            read_out(dve, "gT")
            p, last = products(7, "q_pw", cT, 12, ((0, 0), (1, 1), (0, 1), (1, 0)), "ca")
            for o, (a, b) in enumerate(((0, 1), (1, 0))):
                re = p[:, 7 * PAIRS:8 * PAIRS]
                im = p[:, 15 * PAIRS:16 * PAIRS]
                cp = v.tensor_copy(A8[:, o, o], re)
                if o == 0:
                    free(cp, "q_cm")
                last = tsc(A8[:, o, 1 - o], im, -1.0 if o == 0 else 1.0, None, ALU.mult)
            free(last, "q_pw")
            dve.wait_ge(S("ld_hg"), 96)
            for n, (a, b) in enumerate(((hg[:, 0:1], hg[:, 1:2]), (hg[:, 2:3], hg[:, 3:4]), (hg[:, 4:5], hgk))):
                tsc(gp[:, n:n + 1], a, b, SCALE, ALU.mult, ALU.mult).then_inc(S("gp"), 1)

            def head_norm(rows, nh, tag, c0, sq, done):
                sqv = sq.rearrange("p (h d) -> p h d", d=HD)
                k = 0
                for r, n in rows:
                    last = tt(sqv[:, k:k + n], r, r, ALU.mult)
                    k += n
                link(last)
                v.tensor_reduce(out=hss[:, c0:c0 + nh], in_=sqv[:, 0:nh], axis=AX.X, op=ALU.add).then_inc(S("ss_" + tag), 1)
                dve.wait_ge(S("rs_" + tag), 1)
                k = c0
                for r, n in rows:
                    last = tt(r, r, hrs[:, k:k + n].unsqueeze(2).to_broadcast([P, n, HD]), ALU.mult)
                    k += n
                last.then_inc(S(done), 1)

            def heads_of(x):
                return x.rearrange("p (h d) -> p h d", d=HD)

            for m in range(TM):
                read_out(dve, ("mkv1", m))
                read_out(dve, ("mkv0", m))
            head_norm([(heads_of(MKR.rearrange("p a b -> p (a b)")), 16)], 16, "mk", 0, sqk, "mk_rows")
            for jq in range(6):
                read_out(dve, ("K", jq))
            dve.wait_ge(S("skip"), 1)
            tt(Kst[:, :, 0:GDIM], Kst[:, :, 0:GDIM], MD, ALU.add).then_inc(S("kst_d"), 1)
            dve.wait_ge(S("kst_d"), 1)
            for h in range(2):
                for m in range(TM):
                    read_out(dve, ("win0", h, m))
            head_norm([(heads_of(HS[:, m, MAIN:D]), 4) for m in range(TM)], 8, "q0", 16, sq0, "q0_rows")
            for s in (1, 4, 7):
                dve.wait_ge(S(f"u_step{s}"), 32)
                v.tensor_copy(U5[:, :, s * GDIM:(s + 1) * GDIM], U4[:, s].rearrange("p (g i) -> p g i", i=GDIM)).then_inc(S("u5_dve"), 1)
            for n in range(3):
                read_out(dve, ("V", n))
            for c in range(1, CHUNKS - 1):
                link(tt(stp, A8, VX[:, :, :, c - 1].unsqueeze(1).to_broadcast([P, 2, 2, PAIRS]), ALU.mult))
                link(tt(stp[:, :, 0], stp[:, :, 0], stp[:, :, 1], ALU.add))
                link(tt(VX[:, :, :, c], VX[:, :, :, c], stp[:, :, 0], ALU.add))
            v.memset(stp[:, 0, 0, 0:1], 0.0).then_inc(S("scan"), 1)
            dve.wait_ge(S("xbd_zero"), 1)
            for g2 in range(2):
                v.tensor_copy(Xbd[g2 * 64:(g2 + 1) * 64, 0, :, g2 * 32 + 1:g2 * 32 + 32],
                              VX[g2 * 64:(g2 + 1) * 64, 0, :, 0:31]).then_inc(S("xbd"), 1)
            for n in range(0, 6, 2):
                p = got(dve, ("Y", n))
                free(v.tensor_copy(Ysb[:, :, n * 64:(n + 1) * 64].rearrange("p k (a o) -> p k a o", a=4),
                                   p[0:64, :].rearrange("p (a k o) -> p k a o", a=4, k=STEPS)), ("Y", n))

            def maxima(tag, n, masked):
                for a in range(2):
                    p = got(dve, (tag, "L", n, a))
                    c = 2 * a
                    if masked(2 * n + a):
                        tt(p[:, 0:P], p[:, 0:P], MSK, ALU.add)
                        link(tt(p[:, T + P:2 * T], p[:, T + P:2 * T], MSK, ALU.add))
                        v.tensor_reduce(out=snm[:, n % 2, c:c + 1], in_=p[:, 0:P], axis=AX.X, op=ALU.max, negate=True)
                        last = v.tensor_reduce(out=snm[:, n % 2, c + 1:c + 2], in_=p[:, T:2 * T], axis=AX.X, op=ALU.max,
                                               negate=True)
                    else:
                        last = v.tensor_reduce(out=snm[:, n % 2, c:c + 2], in_=p[:, :].rearrange("p (m k) -> p m k", m=2),
                                               axis=AX.X, op=ALU.max, negate=True)
                    last.then_inc(S(tag + "_max"), 1)

            def normalise(tag, n, pbuf, masked):
                for a in range(2):
                    read_out(dve, (tag, "L", n, a))
                link(v.reciprocal(srec[:, n % 2], ssum[:, n % 2]))
                for a in range(2):
                    for m in range(TM):
                        nk = P * (m + 1) if masked(2 * n + a) else T
                        x = pbuf[:, (n % 2) * 2 + a, m * T:m * T + nk]
                        last = tsc(x, x, srec[:, n % 2, 2 * a + m:2 * a + m + 1], None, ALU.mult)
                    last.then_inc(S(tag + "_p"), 1)

            def o_out(tag, n, heads):
                for a in range(2):
                    _, _, _, tile, half = heads[2 * n + a]
                    p = got(dve, (tag, "O", n, a))
                    free(v.tensor_copy(CT[64 * half:64 * half + 64, tile], p[64 * half:64 * half + 64, 0:T])
                         , (tag, "O", n, a))

            no = lambda h: False
            maxima("m0", 0, no)
            maxima("m0", 1, no)
            normalise("m0", 0, PB0, no)
            normalise("m0", 1, PB0, no)
            for n in range(6):
                read_out(dve, ("glu", n))
                tt(CT[:, n], SIG[:, n % 2], GT6[:, n], ALU.mult).then_inc(S("ct0"), 1)
            o_out("m0", 0, M0_HEADS)
            o_out("m0", 1, M0_HEADS)

            def residual(keys):
                for h, m, key in keys:
                    p = got(dve, key)
                    x = XS[:, m, h * 512:(h + 1) * 512]
                    free(tt(x, x, p[:, :], ALU.add), key)

            def cols_out(tag, outs):
                for q in (0, 2):
                    p = got(dve, ("T" + tag, q))
                    for dst, row in outs:
                        for a in range(2):
                            k = 2 * q + a
                            last = tsc(dst[:, k], p[:, a * T:(a + 1) * T], gT[:, row + k:row + k + 1], None, ALU.mult)
                    free(last, ("T" + tag, q))

            residual([(h, m, ("wout0", h, m)) for h in range(2) for m in range(TM)])
            cols_out("f0", [(HT, G_FFN0)])
            n = 0
            for c in range(len(FCH)):
                for f in range(FCH[c] // P):
                    dve.wait_ge(S("sg0"), n + 1)
                    free(tt(HID0[:, c % 2, f], SG0[:, n % 4], PS[units[("h", c, f)][0]][:, T:2 * T], ALU.mult), ("h", c, f))
                    n += 1
            residual([(h, m, ("ffn", 2 * h + m)) for h in range(2) for m in range(TM)])
            cols_out("kv", [(CT, G_KV), (HT, G_MIX1)])
            for m in range(TM):
                read_out(dve, ("kv", m))
            head_norm([(heads_of(KVR.rearrange("p a b -> p (a b)")), 8)], 8, "kvh", 0, sq1, "kv_rows")
            for h in range(2):
                for m in range(TM):
                    read_out(dve, ("win1", h, m))
            head_norm([(heads_of(HS.rearrange("p a b -> p (a b)")), 32)], 32, "q1", 8, sq1, "q1_rows")
            for n in range(0, 8, 2):
                p = got(dve, ("q1T", n))
                free(v.tensor_copy(QT1[:, (n // 2) * 4:(n // 2) * 4 + 4, (n % 2) * P:(n % 2 + 1) * P],
                                   p[0:HD, :].rearrange("p (h t) -> p h t", h=4)), ("q1T", n))
            dve.wait_ge(S("tri"), 3)
            ca = lambda h: h < 12
            for n in range(9):
                if n < 8:
                    maxima("a1", n, ca)
                    normalise("a1", n, PB1, ca)
                if n >= 1:
                    o_out("a1", n - 1, A1_HEADS)
            residual([(h, m, ("wout1", h, m)) for h in range(2) for m in range(TM)])
            cols_out("f1", [(HT, G_FFN1)])
            link(v.memset(LOWER, 0.0))
            for e in range(1, NE):
                last = v.memset(LOWER[:, e, 0:e], 1.0)
            link(last)
            p = got(dve, "router")
            free(v.tensor_copy(LG, p[:, 0:TM * NE].rearrange("p (m e) -> p m e", m=TM)), "router")
            read_out(dve, "router")
            for m in range(TM):
                me = LG[:, m].unsqueeze(2).to_broadcast([P, NE, NE])
                ot = LG[:, m].unsqueeze(1).to_broadcast([P, NE, NE])
                tt(CMP, ot, me, ALU.is_gt)
                link(tt(CMP2, ot, me, ALU.is_equal))
                link(tt(CMP2, CMP2, LOWER, ALU.mult))
                link(tt(CMP, CMP, CMP2, ALU.add))
                link(v.tensor_reduce(out=RNK[:, m], in_=CMP, axis=AX.X, op=ALU.add))
            tsc(SEL, RNK, 1.5, None, ALU.is_lt).then_inc(S("sel"), 1)
            link(v.tensor_reduce(out=vt[:, 0:2], in_=LG, axis=AX.X, op=ALU.max))
            tt(LG, LG, vt[:, 0:2].unsqueeze(2).to_broadcast([P, TM, NE]), ALU.subtract).then_inc(S("rt_d"), 1)
            dve.wait_ge(S("rt_e"), 1)
            link(tt(EX, EX, SEL, ALU.mult))
            link(v.tensor_reduce(out=vt[:, 2:4], in_=EX, axis=AX.X, op=ALU.add))
            link(v.reciprocal(vt[:, 4:6], vt[:, 2:4]))
            for r in range(PASSES):
                last = tt(GW[:, :, r * NE:(r + 1) * NE], EX, vt[:, 4:6].unsqueeze(2).to_broadcast([P, TM, NE]), ALU.mult)
            link(last)
            p = got(dve, "place")
            link(tsc(POS0, p[:, 0:TM * NE].rearrange("p (m e) -> p m e", m=TM), 1.0, None, ALU.add))
            link(tt(POS0, POS0, SEL, ALU.mult))
            link(v.memset(POS, -1.0))
            for r in range(PASSES):
                last = tsc(POS[:, :, r * NE:(r + 1) * NE], POS0, -1.0 - CAP * r, None, ALU.add)
            link(last)
            free(v.tensor_reduce(out=vt[:, 6:7], in_=p[:, 2 * NE:3 * NE], axis=AX.X, op=ALU.max), "place")
            read_out(dve, "place")
            tsc(flag, vt[:, 6:7], CAP + 0.5, None, ALU.is_gt).then_inc(S("flag"), 1)

            def pick(i):
                for m in range(TM):
                    last = tsc(PICK[:, m], iota, POS[:, m, bass.ds(i, 1)], None, ALU.is_equal)
                last.then_inc(S("pick"), 1)

            def xg_out(turn, key):
                p = got(dve, (key, "xg", 0), turn)
                for a in range(4):
                    last = tsc(XG[:, a], p[:, a * CAP:(a + 1) * CAP], gT[:, G_FFN1 + a:G_FFN1 + a + 1], None, ALU.mult)
                free(last, (key, "xg", 0))

            def yr_out(turn, key, bt):
                p = got(dve, (key, "yt", 0), bt)
                free(v.tensor_copy(YR[0:CAP, 0:512], p[0:CAP, :]), (key, "yt", 0))

            def x_add(turn, key, bt):
                for n in range(2):
                    for m in range(TM):
                        p = got(dve, (key, "sc", n, m), bt)
                        x = XS[:, m, n * 512:(n + 1) * 512]
                        last = tt(x, x, p[:, :], ALU.add)
                        free(last, (key, "sc", n, m))

            def expert(turn, key):
                for c in range(NC_E):
                    p = got(dve, (key, "gu", c, 1), turn)
                    read_out(dve, (key, "gu", c, 0), turn)
                    free(tt(HID[:, c % 2].rearrange("p f t -> p (f t)"), SG1[:, c % 2], p[:, 0:4 * CAP], ALU.mult), (key, "gu", c, 1))
                    if c == 0:
                        yr_out(turn, key, turn)
                    if c == 1:
                        x_add(turn, key, turn)
                    if c == 2:
                        dve.wait_ge(S("pick"), turn.count("pick", 0))
                        for m in range(TM):
                            last = tsc(PG[:, m], PICK[:, m], GW[:, m, bass.ds(turn.i, 1)], None, ALU.mult)
                        last.then_inc(S("pgate"), 1)
                    if c == 4:
                        pick(turn.i + 1)
                xg_out(turn, key)
                p = got(dve, (key, "y", 0), turn)
                free(v.tensor_copy(YT[:, 0:4], p[:, 0:4 * CAP].rearrange("p (a t) -> p a t", a=4)),
                     (key, "y", 0))

            dve.wait_ge(S("iota"), 1)
            v.memset(YT, 0.0)
            v.memset(GATE, 0.0)
            pick(0)
            xg_out(None, "first")

            def passes(key, first, end):
                with dve.Fori(first, end) as i:
                    expert(Turn(i, first), key)
                yr_out(Turn(end, first), (key, "end"), None)
                x_add(Turn(end, first), (key, "end"), None)

            passes("main", 0, NE)
            dve.wait_ge(S("flag"), 1)
            over = dve.value_load(flag[0:1, 0:1], min_val=0, max_val=1)
            with dve.If(over > 0):
                v.memset(GATE, 0.0).then_inc(S("gate_zero"), 1)
                passes("over", NE, PASSES * NE)
            v.memset(vt[:, 8:9], 0.0).then_inc(S("x_final"), 1)


_INS = ['x', 'mem', 'l0_mix_norm', 'l0_w_in', 'l0_s5_lam_re', 'l0_s5_lam_im', 'l0_s5_log_dt', 'l0_s5_b_re', 'l0_s5_b_im',
        'l0_s5_c_re', 'l0_s5_c_im', 'l0_s5_d', 'l0_s5_w_glu', 'l0_s5_b_glu', 'l0_mem_norm', 'l0_w_mem_k', 'l0_w_mem_v',
        'l0_mem_q_gain', 'l0_mem_k_gain', 'l0_w_out', 'l0_ffn_norm', 'l0_ffn_w_gate', 'l0_ffn_w_up', 'l0_ffn_w_down',
        'kv_norm', 'kv_w_k', 'kv_w_v', 'kv_k_gain', 'l1_mix_norm', 'l1_w_in', 'l1_moba_q_gain', 'l1_mem_norm',
        'l1_w_mem_k', 'l1_w_mem_v', 'l1_mem_q_gain', 'l1_mem_k_gain', 'l1_w_out', 'l1_ffn_norm', 'l1_moe_router',
        'l1_moe_w_gate', 'l1_moe_w_up', 'l1_moe_w_down']


def kernel(**inputs):
    import numpy as _np
    import concourse.bacc as _bacc
    from concourse import mybir as _mybir
    from concourse.bass_utils import run_bass_kernel_spmd as _run

    nc = _bacc.Bacc("TRN2", target_bir_lowering=False, num_devices=1)
    arrays, w = {}, {}
    for name in _INS:
        a = _np.ascontiguousarray(inputs[name])
        arrays["in_" + name] = a
        w[name] = nc.dram_tensor("in_" + name, a.shape, _mybir.dt.from_np(a.dtype), kind="ExternalInput").ap()
    out = nc.dram_tensor("out_x", (1, T, D), _mybir.dt.float32, kind="ExternalOutput").ap()
    trunk(nc, w, out)
    r = _run(nc, [arrays], core_ids=[0])
    return r.results[0]["out_x"]
```

```python
import math

import numpy as np
import concourse.bass as bass
from concourse import mybir
from contextlib import ExitStack

P = 128
T = 256
TM = T // P
D = 1024
KT = D // P
HD = 64
GROUPS, GDIM, NSTATE = 48, 16, 64
MAIN = GROUPS * GDIM
PAIRS = GROUPS // 2
STEPS = 8
CHUNKS = T // STEPS
FF0 = 2816
NE, FFE = 8, 3584
CAP = 128
PASSES = -(-T // CAP)
NC_E = FFE // 512
EPS = 1e-6
SCALE = HD ** -0.5
NEG = -1e30
SLOT = 4096
NSLOT = 7
PART = SLOT // 4
NPART = 6

G_MIX0, G_MEM0, G_FFN0, G_KV, G_MIX1, G_MEM1, G_FFN1, G_BGLU = (8 * n for n in range(8))
G_ROWS = 8 * 7 + 6


def trunk(nc, w, out):
    fp, f32r, i32 = mybir.dt.float32, mybir.dt.float32r, mybir.dt.int32
    ALU, ACT, AX = mybir.AluOpType, mybir.ActivationFunctionType, mybir.AxisListType
    ctx = ExitStack()
    with ctx:
        ctx.enter_context(nc.allow_non_contiguous_dma(reason="short head gain vectors"))
        sems = {}

        def S(name):
            if name not in sems:
                sems[name] = ctx.enter_context(nc.semaphore(name))
            return sems[name]

        BASE, RING_END, END = -(-nc.sbuf_base // 64) * 64, NSLOT * SLOT, 53200
        ring = nc.alloc_sbuf_tensor_at("ring", [P, RING_END], fp, offset=BASE)
        work = nc.alloc_sbuf_tensor_at("work", [P, END - RING_END], fp, offset=BASE + 4 * RING_END)
        PS = [ctx.enter_context(nc.psum_tensor(f"bank{b}", [P, 512], fp)) for b in range(8)]

        def at(off, *shape, rows=P, row0=0):
            n = int(np.prod(shape))
            assert off >= RING_END or off + n <= RING_END
            v = ring[row0:row0 + rows, off:off + n] if off < RING_END else work[row0:row0 + rows, off - RING_END:off - RING_END + n]
            if len(shape) == 2:
                v = v.rearrange("p (a b) -> p a b", a=shape[0])
            if len(shape) == 3:
                v = v.rearrange("p (a b c) -> p a b c", a=shape[0], b=shape[1])
            return v

        def cut(off, end):
            cur = [off]

            def take(*shape, rows=P):
                n = int(np.prod(shape))
                v = at(cur[0], *shape, rows=rows)
                cur[0] += n
                assert cur[0] <= end, (cur[0], end)
                return v
            return take

        RING = 0
        XS = at(28672, TM, D)
        HS0 = 30720
        HS = at(HS0, TM, D)
        HT0 = 32768
        HT = at(HT0, KT, T)
        CT = at(34816, KT, T)
        A0, B0, C0 = 36864, 43008, 49152
        take_c = cut(C0, 53200)
        kT = [take_c(4, T, rows=HD), take_c(4, T, rows=HD)]
        vM = [take_c(TM, 256), take_c(TM, 256)]
        ident = take_c(P)
        iota = take_c(CAP)
        gT = take_c(G_ROWS)
        hg = take_c(5, rows=HD)
        hgk = take_c(1, rows=HD)
        gp = take_c(3, rows=HD)
        mh = take_c(32)
        ss = take_c(4)
        rs = take_c(4)
        hss = take_c(64)
        hrs = take_c(64)
        smx = take_c(4)
        snm = take_c(2, 4)
        ssum = take_c(2, 4)
        srec = take_c(2, 4)
        A8 = take_c(2, 2, PAIRS)
        ROUT = take_c(KT, NE)
        flag = take_c(1).bitcast(i32)

        Tm = at(12288, GROUPS, P)
        Bm = at(18432, 2, PAIRS, P)
        KX = 24576
        W0bd = at(KX, 2, PAIRS, 32)
        prod = at(KX + 1536, 2, 4, 2 * P)
        MD = at(KX + 3584, PAIRS, GDIM, rows=32)
        Ug = at(KX, GROUPS, CHUNKS)
        VX = at(KX + 1536, 2, PAIRS, CHUNKS)
        stp = at(KX + 3072, 2, 2, PAIRS)
        sq0 = at(KX + 3584, 512)
        CA = at(A0, 2, PAIRS, P)
        Wt = at(B0, 2, PAIRS, P)
        Kst = at(B0, PAIRS, P, rows=32)
        U4 = at(B0, STEPS, MAIN, rows=CHUNKS)
        U5 = at(RING, GROUPS, P, rows=CHUNKS)
        Ysb = at(B0, STEPS, PAIRS * GDIM, rows=64)
        Xbd = at(B0 + 3072, 2, PAIRS, 64)
        GT6 = at(32768, 6, T)
        misc = cut(8192, 12288)
        braw = misc(2, PAIRS, GDIM)
        cT = misc(2, PAIRS, GDIM)
        cnat = misc(2, 3, P)
        Dbc = misc(PAIRS, GDIM, rows=32)
        mask16 = misc(GDIM, rows=32)
        grow = misc(P, rows=G_ROWS)
        tr = cut(18432, 24576)
        lam_r, lam_i, ldt, edt = tr(P, rows=PAIRS), tr(P, rows=PAIRS), tr(2, rows=PAIRS), tr(2, rows=PAIRS)
        zr, zi, er, kk, rr, sn, cs, ebase = (tr(P, rows=PAIRS) for _ in range(8))
        fr, fi, t0, t1, t2 = (tr(P, rows=PAIRS) for _ in range(5))
        pw = tr(2, 8, P, rows=PAIRS)
        cm = tr(2, 8, P, rows=PAIRS)
        u0 = at(8192 + 3000, 4 * P, rows=PAIRS)
        u1 = at(8192 + 3000 + 512, 4 * P, rows=PAIRS)
        assert 3000 + 1024 <= SLOT
        MKR = at(12288, 4, 256)
        sqk = at(12288 + 1024, 1024)
        PB0, PT0, QT0 = at(HS0, 4, 2 * T), at(A0, 4, 2 * T), at(34816, 4, T, rows=HD)
        SIG = at(A0 + 4608, 2, T)
        HID0 = at(B0, 2, 4, T)
        SG0 = at(B0 + 2048, 4, T)
        PT1, KVR, VKV, kTkv = at(A0, 4, 2 * T), at(A0 + 2048, TM, 256), at(A0 + 2560, TM, 256), at(A0 + 3072, 4, T, rows=HD)
        TRI, ONES = at(A0 + 4096, P), at(A0 + 4224, P)
        MSK = at(A0 + 5120, P)
        QT1, PB1 = at(B0, 16, T, rows=HD), at(B0 + 4096, 4, 2 * T)
        sq1 = at(B0 + 4096, 2 * D)
        PART_HL = nc.alloc_sbuf_tensor_at("part_hl", [P, NPART, 2, PART], f32r, offset=BASE + 4 * HT0)
        XG = nc.alloc_sbuf_tensor_at("xg_hl", [P, 2, KT, CAP], f32r, offset=BASE + 4 * C0)
        AT = nc.alloc_sbuf_tensor_at("at_hl", [P, 2, 4, CAP], f32r, offset=BASE + 4 * C0 + 4 * 2 * KT * CAP)
        mo = cut(HT0 + NPART * 2 * PART, B0 + 6144)
        PICK, PG, HID, YR, GATE, SG1 = mo(TM, CAP), mo(TM, CAP), mo(512), mo(D), mo(T), mo(512)
        LG, SEL, RNK, EX, GT_, POS0 = (mo(TM, NE) for _ in range(6))
        CMP, CMP2, LOWER = mo(NE, NE), mo(NE, NE), mo(NE, NE)
        POS, GW = mo(TM, PASSES * NE + 1), mo(TM, PASSES * NE)
        vt = mo(16)

        def mkrow(l, m):
            return MKR[:, 2 * l + m]

        M0_HEADS = [(h, kT[0][:, h], vM[0][:, :, h * HD:(h + 1) * HD], 6 + h // 2, h % 2) for h in range(4)]
        A1_HEADS = [(h, kTkv[:, h // 3], VKV[:, :, (h // 3) * HD:(h // 3 + 1) * HD], h // 2, h % 2) for h in range(12)] \
            + [(h, kT[1][:, h - 12], vM[1][:, :, (h - 12) * HD:(h - 11) * HD], h // 2, h % 2) for h in range(12, 16)]

        def cols(name, n0, n, kt=KT):
            return [(lambda s: s[:, 0:kt * n].rearrange("p (k n) -> p k n", k=kt),
                     w[name][:, n0:n0 + n].rearrange("(k p) n -> p k n", p=P))]

        def kv_pair(a, b):
            return [(lambda s: s[:, 0:2048].rearrange("p (k n) -> p k n", k=KT), w[a].rearrange("(k p) n -> p k n", p=P)),
                    (lambda s: s[:, 2048:4096].rearrange("p (k n) -> p k n", k=KT), w[b].rearrange("(k p) n -> p k n", p=P))]

        def rows_of(name, r0, r):
            return [(lambda s: s[:, 0:r // P * D].rearrange("p (k n) -> p k n", n=D),
                     w[name][r0:r0 + r, :].rearrange("(k p) n -> p k n", p=P))]

        FCH = [512] * 5 + [256]
        stream = [("memkv1", kv_pair("l1_w_mem_k", "l1_w_mem_v")), ("memkv0", kv_pair("l0_w_mem_k", "l0_w_mem_v")),
                  ("win0a", cols("l0_w_in", 0, 512)), ("win0b", cols("l0_w_in", 512, 512)),
                  ("glua", cols("l0_s5_w_glu", 0, 512, 6)), ("glub", cols("l0_s5_w_glu", 512, 256, 6)),
                  ("wout0a", cols("l0_w_out", 0, 512)), ("wout0b", cols("l0_w_out", 512, 512))]
        for c in range(len(FCH) + 1):
            if c < len(FCH):
                stream.append((f"g{c}", cols("l0_ffn_w_gate", 512 * c, FCH[c])))
                stream.append((f"u{c}", cols("l0_ffn_w_up", 512 * c, FCH[c])))
            if c >= 1:
                stream.append((f"d{c - 1}", rows_of("l0_ffn_w_down", 512 * (c - 1), FCH[c - 1])))
        stream += [("kv", kv_pair("kv_w_k", "kv_w_v")),
                   ("win1a", cols("l1_w_in", 0, 512)), ("win1b", cols("l1_w_in", 512, 512)),
                   ("wout1a", cols("l1_w_out", 0, 512)), ("wout1b", cols("l1_w_out", 512, 512))]
        NA = len(stream)
        NAMES = [n for n, _ in stream]

        def slot_of(n):
            return n % 2 if n < 6 else (n - 4) % NSLOT

        filled, need = [0] * NSLOT, []
        for n, (_, dmas) in enumerate(stream):
            filled[slot_of(n)] += 16 * len(dmas)
            need.append(filled[slot_of(n)])
        items = [("g", 0), ("u", 0)]
        for c in range(1, NC_E):
            items += [("g", c), ("u", c), ("d", c - 1)]
        items += [("d", NC_E - 1)]
        NI = len(items)
        assert NI == 3 * NSLOT
        full = [S(f"slot_full{s}") for s in range(NSLOT)]

        def e_slot(q):
            return slot_of(NA + q)

        def e_need(q):
            s = e_slot(q)
            return filled[s] + 16 * (sum(e_slot(r) == s for r in range(q + 1)))

        bank_full = [S(f"bank_full{b}") for b in range(8)]
        bank_free = [S(f"bank_free{b}") for b in range(8)]
        uses, units = [0] * 8, {}
        PER = [4, 4, 3, 3, 1, 1, NC_E + 1, 6]
        NPT = 4 * NI
        ends_bank = {4 * q + 3: items[q] for q in range(NI) if items[q][0] != "d" or items[q][1] == NC_E - 1}
        TALLY = {"pick": (1, 1), "pgate": (0, 1), "hi": (0, NPT), "lo_dve": (0, 3 * NI), "lo_pool": (0, NI),
                 "part_used": (0, NPT - len(ends_bank)), "hi_small": (2, NC_E + 2)}

        class Turn:
            def __init__(self, i, start):
                self.i, self.start = i, start

            def value(self, base, per):
                return self.i * per + (base - self.start * per)

            def count(self, name, k):
                pre, per = TALLY[name]
                return self.i * per + (pre + k)

            def weights(self, base):
                return self.i * (3 * 16) + base

        def unit(pe, key, b, turn=None):
            n = uses[b]
            uses[b] += 1
            units[key] = (b, n)
            if turn is not None:
                pe.wait_ge(bank_free[b], turn.value(n, PER[b]))
            elif n:
                pe.wait_ge(bank_free[b], n)
            return PS[b]

        def ready(ins, key):
            ins.then_inc(bank_full[units[key][0]], 1)

        def got(eng, key, turn=None):
            b, n = units[key]
            eng.wait_ge(bank_full[b], n + 1 if turn is None else turn.value(n + 1, PER[b]))
            return PS[b]

        def free(ins, key):
            ins.then_inc(bank_free[units[key][0]], 1)

        def read_out(eng, key, turn=None):
            b, n = units[key]
            eng.wait_ge(bank_free[b], n + 1 if turn is None else turn.value(n + 1, PER[b]))

        FLIP_AT = {4 * items.index(("g", c + 1)): c for c in range(NC_E - 1)}
        FLIP_AT[4 * items.index(("d", NC_E - 2)) + 3] = NC_E - 1
        SC_AT = {8 + 2 * r: (r // TM, r % TM) for r in range(2 * TM)}
        GT_AT = 4 * items.index(("g", 3)) + 1
        XG_AT = 4 * items.index(("d", NC_E - 2)) + 3
        LEAD = 3

        def part_free(eng, n, turn, key):
            if n in ends_bank:
                kind, c = ends_bank[n]
                got(eng, (key, "y", 1) if kind == "d" else (key, "gu", c, "gu".index(kind)), turn)
            else:
                eng.wait_ge(S("part_used"), turn.count("part_used", sum(r not in ends_bank for r in range(n + 1))))

        item_done = {}

        block = ctx.enter_context(nc.Block())

        @block.tensor
        def _(pe):
            mm = nc.tensor.matmul
            st = [0]

            def item(name):
                n = st[0]
                assert NAMES[n] == name, (NAMES[n], name)
                st[0] += 1
                pe.wait_ge(full[slot_of(n)], need[n])
                return at(slot_of(n) * SLOT, SLOT)

            def transpose(o, i, rows=P):
                return nc.tensor.transpose(o, i, ident[0:rows, 0:rows])

            pe.wait_ge(S("ident"), 2)
            pe.wait_ge(S("ld_gains"), 16 * 8)
            p = unit(pe, "gT", 4)
            ready(transpose(p[:, 0:G_ROWS], grow, G_ROWS), "gT")
            for q in range(4):
                p = unit(pe, ("memT", q), q)
                for k in (2 * q, 2 * q + 1):
                    for m in range(TM):
                        if q == 0 and k == 0:
                            pe.wait_ge(S("mem_rows"), m + 1)
                        last = transpose(p[:, (k % 2) * T + m * P:(k % 2) * T + (m + 1) * P], HS[:, m, k * P:(k + 1) * P])
                ready(last, ("memT", q))
            pe.wait_ge(S("ld_c"), 64)
            for ri in range(2):
                p = unit(pe, ("cT", ri), 4 + ri)
                for a in range(3):
                    last = transpose(p[:, a * P:(a + 1) * P], cnat[:, ri, a])
                ready(last, ("cT", ri))

            def proj_kv(name, src, tag, banks):
                s = item(name)
                for m in range(TM):
                    p = unit(pe, (tag, m), banks[m])
                    for h in range(2):
                        for k in range(KT):
                            last = mm(p[:, h * 256:(h + 1) * 256], lhsT=src[:, k, m * P:(m + 1) * P],
                                      rhs=s[:, h * 2048 + k * 256:h * 2048 + (k + 1) * 256],
                                      start=(k == 0 and h == 0), stop=(k == KT - 1), skip_group_check=True)
                    ready(last, (tag, m))
                item_done[name] = units[(tag, TM - 1)]

            for q in range(4):
                read_out(pe, ("memT", q))
            proj_kv("memkv1", HT, "mkv1", (0, 1))
            for b, src, key in ((6, cm, "cm"), (7, pw, "pw")):
                pe.wait_ge(S("s5_" + key), 1)
                p = unit(pe, "q_" + key, b)
                for ri in range(2):
                    for n in range(8):
                        last = transpose(p[:, (ri * 8 + n) * PAIRS:(ri * 8 + n + 1) * PAIRS], src[:, ri, n], PAIRS)
                ready(last, "q_" + key)
            pe.wait_ge(S("x_rows0"), TM)
            for q in range(4):
                p = unit(pe, ("xT0", q), q)
                for k in (2 * q, 2 * q + 1):
                    for m in range(TM):
                        last = transpose(p[:, (k % 2) * T + m * P:(k % 2) * T + (m + 1) * P], HS[:, m, k * P:(k + 1) * P])
                ready(last, ("xT0", q))
            proj_kv("memkv0", CT, "mkv0", (4, 5))

            def proj_rows(names, src, tag, banks):
                for h, name in enumerate(names):
                    s = item(name)
                    for m in range(TM):
                        p = unit(pe, (tag, h, m), banks[2 * h + m])
                        for k in range(KT):
                            last = mm(p[:, :], lhsT=src[:, k, m * P:(m + 1) * P], rhs=s[:, k * 512:(k + 1) * 512],
                                      start=(k == 0), stop=(k == KT - 1))
                        ready(last, (tag, h, m))
                    item_done[name] = units[(tag, h, TM - 1)]

            for q in range(4):
                read_out(pe, ("xT0", q))
            proj_rows(("win0a", "win0b"), HT, "win0", (0, 1, 2, 3))
            pe.wait_ge(S("mk_rows"), 1)
            for l in (1, 0):
                for m in range(TM):
                    p = unit(pe, ("mkT", l, m), 4 + m)
                    for h in range(4):
                        last = transpose(p[0:HD, h * P:(h + 1) * P], mkrow(l, m)[:, h * HD:(h + 1) * HD])
                    ready(last, ("mkT", l, m))
            pe.wait_ge(S("s5_w"), 12)
            for n in range(12):
                ri, jq = n // 6, n % 6
                p = unit(pe, ("Bm", n), 4 + n % 2)
                for a in range(4):
                    last = transpose(p[:, a * P:(a + 1) * P], Wt[:, ri, jq * 4 + a])
                ready(last, ("Bm", n))
            pe.wait_ge(S("s5_w0"), 4)
            pe.wait_ge(S("s5_ca"), 12)
            for ri in range(2):
                read_out(pe, ("cT", ri))
            for jq in range(6):
                p = unit(pe, ("K", jq), 4 + jq % 2)
                for a in range(4):
                    j = jq * 4 + a
                    for ri in range(2):
                        mm(p[0:32, a * P:a * P + GDIM], lhsT=W0bd[:, ri, j], rhs=cT[:, ri, j],
                           start=(a == 0 and ri == 0), stop=(ri == 1), skip_group_check=True)
                    for ri in range(2):
                        last = mm(p[0:32, a * P + GDIM:(a + 1) * P], lhsT=W0bd[:, ri, j], rhs=CA[:, ri, j, 0:7 * GDIM],
                                  start=False, stop=(ri == 1), skip_group_check=True)
                ready(last, ("K", jq))
            pe.wait_ge(S("u5_act"), 3)
            pe.wait_ge(S("u5_dve"), 3)
            pe.wait_ge(S("u5_pool"), 2)
            for n in range(3):
                p = unit(pe, ("Ug", n), n)
                for a in range(16):
                    g = n * 16 + a
                    last = transpose(p[:, a * CHUNKS:(a + 1) * CHUNKS], U5[:, g], CHUNKS)
                ready(last, ("Ug", n))
            for n in range(12):
                read_out(pe, ("Bm", n))
            for n in range(3):
                read_out(pe, ("Ug", n))
            vb = [unit(pe, ("V", n), 3 + n) for n in range(3)]
            for j in range(PAIRS):
                for ri in range(2):
                    b, c0 = (vb[ri], j * CHUNKS) if j < 16 else (vb[2], (ri * 8 + j - 16) * CHUNKS)
                    for g2 in range(2):
                        last = mm(b[g2 * 64:(g2 + 1) * 64, c0:c0 + CHUNKS], lhsT=Bm[:, ri, j, g2 * 64:(g2 + 1) * 64],
                                  rhs=Ug[:, g2 * PAIRS + j], start=True, stop=True, skip_group_check=True)
                        if j == 15 and g2 == 1:
                            ready(last, ("V", ri))
            ready(last, ("V", 2))
            pe.wait_ge(S("q0_rows"), 1)
            for m in range(TM):
                p = unit(pe, ("q0T", m), 6 + m)
                for h in range(4):
                    last = transpose(p[0:HD, h * P:(h + 1) * P], HS[:, m, MAIN + h * HD:MAIN + (h + 1) * HD])
                ready(last, ("q0T", m))
            pe.wait_ge(S("tm"), 16 * 16)
            yb = [unit(pe, ("Y", n), n) for n in range(6)]
            for j in range(PAIRS):
                for g2 in range(2):
                    mm(yb[j // 4][g2 * 32:(g2 + 1) * 32, (j % 4) * P:(j % 4 + 1) * P], lhsT=Ug[:, g2 * PAIRS + j],
                       rhs=Tm[:, g2 * PAIRS + j], start=(j % 4 == 0), stop=False, skip_group_check=True)
            pe.wait_ge(S("xbd"), 4)
            for j in range(PAIRS):
                for ri in range(2):
                    last = mm(yb[j // 4][0:64, (j % 4) * P:(j % 4 + 1) * P], lhsT=Xbd[:, ri, j], rhs=CA[:, ri, j],
                              start=False, stop=(ri == 1), skip_group_check=True)
                if j % 4 == 3:
                    ready(last, ("Y", j // 4))
            for n in range(6):
                read_out(pe, ("Y", n))
            for n in range(3):
                p = unit(pe, ("yT", n), 6 + n % 2)
                for k in range(STEPS):
                    last = transpose(p[:, k * 64:(k + 1) * 64], Ysb[:, k, n * P:(n + 1) * P], 64)
                ready(last, ("yT", n))

            def attention(tag, heads, qT, masked, pbuf, pt_sb, banks):
                LB, PB = banks
                ng = len(heads) // 2

                def logits(n):
                    for a in range(2):
                        qh, kt_, _, _, _ = heads[2 * n + a]
                        p = unit(pe, (tag, "L", n, a), LB[2 * (n % 2) + a])
                        for m in range(TM):
                            nk = P * (m + 1) if masked(2 * n + a) else T
                            last = mm(p[:, m * T:m * T + nk], lhsT=qT[:, qh, m * P:(m + 1) * P], rhs=kt_[:, 0:nk],
                                      start=True, stop=True, skip_group_check=True)
                        ready(last, (tag, "L", n, a))

                def flip(n):
                    for a in range(2):
                        pe.wait_ge(S(tag + "_p"), 2 * n + a + 1)
                        p = unit(pe, (tag, "PT", n, a), PB[a])
                        for kt_ in range(TM):
                            for m in range(TM):
                                if masked(2 * n + a) and kt_ > m:
                                    continue
                                last = transpose(p[:, kt_ * T + m * P:kt_ * T + (m + 1) * P],
                                                 pbuf[:, (n % 2) * 2 + a, m * T + kt_ * P:m * T + (kt_ + 1) * P])
                        ready(last, (tag, "PT", n, a))

                def outs(n):
                    for a in range(2):
                        _, _, v, _, half = heads[2 * n + a]
                        read_out(pe, (tag, "PT", n, a))
                        p = unit(pe, (tag, "O", n, a), PB[a])
                        o = p[64 * half:64 * half + 64, 0:T]
                        mm(o, lhsT=v[:, 0], rhs=pt_sb[:, (n % 2) * 2 + a, 0:T], start=True, stop=False,
                           skip_group_check=True)
                        m0 = P if masked(2 * n + a) else 0
                        last = mm(o[:, m0:T], lhsT=v[:, 1], rhs=pt_sb[:, (n % 2) * 2 + a, T + m0:2 * T],
                                  start=False, stop=True, skip_group_check=True)
                        ready(last, (tag, "O", n, a))

                return logits, flip, outs, ng

            lg, fl, ou, ng = attention("m0", M0_HEADS, QT0, lambda h: False, PB0, PT0, ((2, 3, 4, 5), (6, 7)))
            for m in range(TM):
                read_out(pe, ("q0T", m))
                read_out(pe, ("mkT", 0, m))
            lg(0)
            lg(1)
            for n in range(3):
                read_out(pe, ("yT", n))
            sa = item("glua")
            sb_ = item("glub")
            for n in range(6):
                s, n0, wn = (sa, n * P, 512) if n < 4 else (sb_, (n - 4) * P, 256)
                p = unit(pe, ("glu", n), n % 2)
                for k in range(6):
                    last = mm(p[:, 0:T], lhsT=s[:, k * wn + n0:k * wn + n0 + P], rhs=GT6[:, k], start=(k == 0), stop=(k == 5))
                ready(last, ("glu", n))
                if n == 3 or n == 5:
                    item_done["glua" if n == 3 else "glub"] = units[("glu", n)]
            fl(0)
            ou(0)
            fl(1)
            ou(1)

            def proj_out(names, tag, banks, wait):
                for h, name in enumerate(names):
                    s = item(name)
                    for m in range(TM):
                        p = unit(pe, (tag, h, m), banks[2 * h + m])
                        for k in range(KT):
                            last = mm(p[:, :], lhsT=CT[:, k, m * P:(m + 1) * P], rhs=s[:, k * 512:(k + 1) * 512],
                                      start=(k == 0), stop=(k == KT - 1))
                        ready(last, (tag, h, m))
                    item_done[name] = units[(tag, h, TM - 1)]

            pe.wait_ge(S("ct0"), 6)
            for n in range(2):
                for a in range(2):
                    read_out(pe, ("m0", "O", n, a))
            proj_out(("wout0a", "wout0b"), "wout0", (0, 1, 2, 3), None)

            def rows_to_cols(tag):
                pe.wait_ge(S("rows_" + tag), TM)
                for q in range(4):
                    p = unit(pe, ("T" + tag, q), q)
                    for k in (2 * q, 2 * q + 1):
                        for m in range(TM):
                            last = transpose(p[:, (k % 2) * T + m * P:(k % 2) * T + (m + 1) * P],
                                             HS[:, m, k * P:(k + 1) * P])
                    ready(last, ("T" + tag, q))

            rows_to_cols("f0")
            for q in range(4):
                read_out(pe, ("Tf0", q))
            for c in range(len(FCH) + 1):
                if c < len(FCH):
                    sg_, su_ = item(f"g{c}"), item(f"u{c}")
                    nf = FCH[c] // P
                    for f in range(nf):
                        p = unit(pe, ("h", c, f), (4 * c + f) % 4)
                        for h, s in enumerate((sg_, su_)):
                            for k in range(KT):
                                last = mm(p[:, h * T:(h + 1) * T], lhsT=s[:, k * FCH[c] + f * P:k * FCH[c] + (f + 1) * P],
                                          rhs=HT[:, k], start=(k == 0 and h == 0), stop=(k == KT - 1),
                                          skip_group_check=True)
                        ready(last, ("h", c, f))
                    item_done[f"g{c}"] = item_done[f"u{c}"] = units[("h", c, nf - 1)]
                if c >= 1:
                    s = item(f"d{c - 1}")
                    nf = FCH[c - 1] // P
                    if c == 1:
                        acc = [unit(pe, ("ffn", b), 4 + b) for b in range(4)]
                    for f in range(nf):
                        read_out(pe, ("h", c - 1, f))
                    for f in range(nf):
                        for m in range(TM):
                            for n in range(2):
                                last = mm(acc[2 * n + m][:, :], lhsT=HID0[:, (c - 1) % 2, f, m * P:(m + 1) * P],
                                          rhs=s[:, f * D + n * 512:f * D + (n + 1) * 512],
                                          start=(c == 1 and f == 0), stop=(c == len(FCH) and f == nf - 1))
                                if c == len(FCH) and f == nf - 1:
                                    ready(last, ("ffn", 2 * n + m))
                    if c < len(FCH):
                        last.then_inc(S("down0"), 1)
                        item_done[f"d{c - 1}"] = c
                    else:
                        item_done[f"d{c - 1}"] = units[("ffn", 3)]
            rows_to_cols("kv")
            for q in range(4):
                read_out(pe, ("Tkv", q))
            proj_kv("kv", CT, "kv", (4, 5))
            proj_rows(("win1a", "win1b"), HT, "win1", (0, 1, 2, 3))
            pe.wait_ge(S("kv_rows"), 1)
            for m in range(TM):
                p = unit(pe, ("kvT", m), 4 + m)
                for h in range(4):
                    last = transpose(p[0:HD, h * P:(h + 1) * P], KVR[:, m, h * HD:(h + 1) * HD])
                ready(last, ("kvT", m))
            pe.wait_ge(S("q1_rows"), 1)
            for n in range(8):
                m, hq = n % 2, n // 2
                p = unit(pe, ("q1T", n), 4 + n % 4)
                for a in range(4):
                    h = hq * 4 + a
                    last = transpose(p[0:HD, a * P:(a + 1) * P], HS[:, m, h * HD:(h + 1) * HD])
                ready(last, ("q1T", n))
            for m in range(TM):
                read_out(pe, ("kvT", m))
                read_out(pe, ("mkT", 1, m))
            for n in range(8):
                read_out(pe, ("q1T", n))
            lg, fl, ou, ng = attention("a1", A1_HEADS, QT1, lambda h: h < 12, PB1, PT1, ((0, 1, 2, 3), (6, 7)))
            for n in range(ng + 2):
                if n < ng:
                    lg(n)
                if 1 <= n <= ng:
                    fl(n - 1)
                    ou(n - 1)
            for n in range(ng):
                for a in range(2):
                    read_out(pe, ("a1", "O", n, a))
            proj_out(("wout1a", "wout1b"), "wout1", (0, 1, 2, 3), None)
            rows_to_cols("f1")
            for q in range(4):
                read_out(pe, ("Tf1", q))
            pe.wait_ge(S("ld_router"), 16)
            p = unit(pe, "router", 4)
            for m in range(TM):
                for k in range(KT):
                    last = mm(p[:, m * NE:(m + 1) * NE], lhsT=HT[:, k, m * P:(m + 1) * P], rhs=ROUT[:, k],
                              start=(k == 0), stop=(k == KT - 1), skip_group_check=True)
            ready(last, "router")
            pe.wait_ge(S("sel"), 1)
            pe.wait_ge(S("tri"), 3)
            p = unit(pe, "place", 5)
            for col, terms in ((0, ((TRI, 0),)), (1, ((ONES, 0), (TRI, 1))), (2, ((ONES, 0), (ONES, 1)))):
                for q, (mat, m) in enumerate(terms):
                    last = mm(p[:, col * NE:(col + 1) * NE], lhsT=mat, rhs=SEL[:, m],
                              start=(q == 0), stop=(q == len(terms) - 1), skip_group_check=True)
            ready(last, "place")

            y_base = [0, 0]

            def three(p, xs, ws, start, stop):
                for q, (a, b) in enumerate(((0, 0), (1, 0), (0, 1))):
                    last = mm(p, lhsT=xs[a], rhs=ws[b], start=start and q == 0, stop=stop and q == 2)
                return last

            def gather(turn, key):
                for b in range(2):
                    p = unit(pe, (key, "xg", b), 7 - b, turn)
                    for kk_ in range(4):
                        k = 4 * b + kk_
                        for m in range(TM):
                            last = mm(p[:, kk_ * CAP:(kk_ + 1) * CAP], lhsT=HS[:, m, k * P:(k + 1) * P],
                                      rhs=PICK[:, m], start=(kk_ == 0 and m == 0), stop=(m == TM - 1),
                                      skip_group_check=True)
                    ready(last, (key, "xg", b))

            def scatter(turn, key, bt, n, m):
                if n == 0 and m == 0:
                    for b in range(2):
                        pe.wait_ge(bank_free[4 + b], uses[4 + b] if bt is None else bt.value(y_base[b], 1))
                p = unit(pe, (key, "sc", n, m), 7, bt)
                ready(mm(p[:, :], lhsT=GATE[0:CAP, m * P:(m + 1) * P], rhs=YR[0:CAP, n * 512:(n + 1) * 512],
                         start=True, stop=True), (key, "sc", n, m))

            def expert(turn, key):
                def part(n):
                    q, j = n // 4, n % 4
                    if j < 3:
                        pe.wait_ge(S("lo_dve"), turn.count("lo_dve", 3 * q + j + 1))
                    else:
                        pe.wait_ge(S("lo_pool"), turn.count("lo_pool", q + 1))
                    return PART_HL[:, n % NPART, 0], PART_HL[:, n % NPART, 1]

                def flip(c):
                    read_out(pe, (key, "gu", c, 1), turn)
                    p = unit(pe, (key, "aT", c), 6, turn)
                    for f in range(4):
                        last = transpose(p[:, f * CAP:(f + 1) * CAP], HID[0:CAP, f * P:(f + 1) * P], CAP)
                    ready(last, (key, "aT", c))

                for b in range(2):
                    pe.wait_ge(bank_free[6 + b], turn.value(uses[6 + b], PER[6 + b]))
                for n in range(NPT):
                    (kind, c), j = items[n // 4], n % 4
                    if kind == "d":
                        if j == 0:
                            read_out(pe, (key, "aT", c), turn)
                            if c == 0:
                                acc = [unit(pe, (key, "y", b), 4 + b, turn) for b in range(2)]
                        hl = part(n)
                        for b in range(2):
                            last = three(acc[b][0:CAP, :], (AT[:, 0, j], AT[:, 1, j]),
                                         [w_[:, b * 512:(b + 1) * 512] for w_ in hl],
                                         c == 0 and j == 0, c == NC_E - 1 and j == 3)
                            if c == NC_E - 1 and j == 3:
                                ready(last, (key, "y", b))
                    else:
                        if j == 0:
                            p = unit(pe, (key, "gu", c, "gu".index(kind)), 2 * (c % 2) + "gu".index(kind), turn)
                        hl = part(n)
                        for a in range(2):
                            k = 2 * j + a
                            last = three(p[0:CAP, :], (XG[:, 0, k], XG[:, 1, k]),
                                         [w_[:, a * 512:(a + 1) * 512] for w_ in hl], k == 0, k == KT - 1)
                        if j == 3:
                            ready(last, (key, "gu", c, "gu".index(kind)))
                    if n not in ends_bank:
                        last.then_inc(S("part_used"), 1)
                    if n in SC_AT:
                        scatter(turn, key, turn, *SC_AT[n])
                    if n in FLIP_AT:
                        flip(FLIP_AT[n])
                    if n == GT_AT:
                        pe.wait_ge(S("pgate"), turn.count("pgate", 1))
                        p2 = unit(pe, (key, "gt"), 7, turn)
                        for m in range(TM):
                            last = transpose(p2[0:CAP, m * P:(m + 1) * P], PG[:, m])
                        ready(last, (key, "gt"))
                    if n == XG_AT:
                        pe.wait_ge(S("pick"), turn.count("pick", 1))
                        gather(turn, key)

            pe.wait_ge(S("pick"), 1)
            gather(None, "first")

            def passes(key, first, end):
                base = list(uses)
                y_base[:] = uses[4:6]
                with pe.Fori(first, end) as i:
                    expert(Turn(i, first), key)
                for b in range(8):
                    assert uses[b] - base[b] == PER[b], (b, uses[b] - base[b])
                    uses[b] = base[b] + PER[b] * (end - first)
                for n, m in SC_AT.values():
                    scatter(Turn(end, first), (key, "end"), None, n, m)

            passes("main", 0, NE)
            pe.wait_ge(S("flag"), 1)
            over = pe.value_load(flag[0:1, 0:1], min_val=0, max_val=1)
            with pe.If(over > 0):
                pe.wait_ge(S("gate_zero"), 1)
                passes("over", NE, PASSES * NE)

        @block.sync
        def _(sp):
            def used(n):
                d = item_done[NAMES[n]]
                if isinstance(d, int):
                    sp.wait_ge(S("down0"), d)
                else:
                    sp.wait_ge(bank_full[d[0]], d[1] + 1)

            def e_used(turn, q, key):
                part_free(sp, 4 * q + 3, turn, key)

            def load_static(n):
                for dst, src in stream[n][1]:
                    sp.dma_start(dst(at(slot_of(n) * SLOT, SLOT)), src).then_inc(full[slot_of(n)], 16)

            for n in range(NA):
                s = slot_of(n)
                prev = [q for q in range(n) if slot_of(q) == s]
                if prev:
                    used(prev[-1])
                    if NAMES[n] in ("glua", "glub"):
                        got(sp, ("Ug", 2))
                else:
                    if n >= 6:
                        got(sp, ("yT", 2))
                load_static(n)

            def load_expert(e, q):
                kind, c = items[q]
                slot = at(e_slot(q) * SLOT, SLOT)
                if kind == "d":
                    src = w["l1_moe_w_down"][bass.ds(e, 1), c * 512:(c + 1) * 512, :].rearrange("e (k p) n -> p (e k) n", p=P)
                    sp.dma_start(slot.rearrange("p (k n) -> p k n", n=D), src).then_inc(full[e_slot(q)], 16)
                else:
                    src = w["l1_moe_w_gate" if kind == "g" else "l1_moe_w_up"][bass.ds(e, 1), :, c * 512:(c + 1) * 512] \
                        .rearrange("e (k p) n -> p (e k) n", p=P)
                    sp.dma_start(slot.rearrange("p (k n) -> p k n", n=512), src).then_inc(full[e_slot(q)], 16)

            EARLY = 2
            for q in range(NSLOT):
                used(max(n for n in range(NA) if slot_of(n) == e_slot(q)))
                load_expert(0, q)

            def rest(turn, i, key):
                for q in range(NSLOT, NI):
                    e_used(turn, q - NSLOT, key)
                    load_expert(i % NE, q)

            def first_items(turn, i, lo, hi, key):
                for q in range(lo, hi):
                    e_used(turn, NI - NSLOT + q, key)
                    load_expert((i + 1) % NE, q)

            def passes(key, first, end):
                with sp.Fori(first, end - 1) as i:
                    rest(Turn(i, first), i, key)
                    first_items(Turn(i, first), i, 0, NSLOT, key)
                rest(Turn(end - 1, first), end - 1, key)
                first_items(Turn(end - 1, first), end - 1, 0, EARLY, key)

            passes("main", 0, NE)
            sp.wait_ge(S("flag"), 1)
            over = sp.value_load(flag[0:1, 0:1], min_val=0, max_val=1)
            with sp.If(over > 0):
                first_items(Turn(NE - 1, 0), NE - 1, EARLY, NSLOT, "main")
                passes("over", NE, PASSES * NE)
            sp.wait_ge(S("x_final"), 1)
            sp.dma_start(out[0].rearrange("(m p) n -> p m n", p=P), XS).then_inc(S("stored"), 16)
            sp.wait_ge(S("stored"), 16)

        @block.gpsimd
        def _(pool):
            g = nc.gpsimd
            n_chain = [0]

            def link(ins):
                n_chain[0] += 1
                ins.then_inc(S("pool_chain"), 1)
                pool.wait_ge(S("pool_chain"), n_chain[0])

            g.iota(iota, pattern=[[1, CAP]], base=0, channel_multiplier=0, allow_small_or_imprecise_dtypes=True).then_inc(S("iota"), 1)
            link(g.memset(ident, 0.0))
            link(g.affine_select(out=ident, in_=ident, compare_op=ALU.not_equal, fill=1.0, base=0,
                                 pattern=[[-1, P]], channel_multiplier=1))
            g.memset(mh, -0.5).then_inc(S("ident"), 1)
            g.memset(ebase, math.e).then_inc(S("ident"), 1)
            pool.wait_ge(S("ident"), 2)

            def root(tag, n, src, dst, width):
                pool.wait_ge(S("ss_" + tag), n)
                link(g.tensor_scalar(src, src, 1.0 / width, EPS, ALU.mult, ALU.add))
                g.tensor_tensor(dst, src, mh[:, 0:src.shape[-1]], ALU.pow).then_inc(S("rs_" + tag), 1)

            root("mem", 2, ss[:, 0:2], rs[:, 0:2], D)
            pool.wait_ge(S("ld_lam"), 48)
            g.tensor_tensor(edt, ebase[:, 0:2], ldt, ALU.pow).then_inc(S("dt"), 1)
            pool.wait_ge(S("zr"), 1)
            g.tensor_tensor(er, ebase, zr, ALU.pow).then_inc(S("er"), 1)
            root("x0", 2, ss[:, 2:4], rs[:, 2:4], D)
            pool.wait_ge(S("ld_d"), 32)
            link(g.tensor_tensor(mask16, ident[0:32, 0:GDIM], ident[0:32, GDIM:32], ALU.add))
            g.tensor_tensor(MD, Dbc, mask16.unsqueeze(1).to_broadcast([32, PAIRS, GDIM]), ALU.mult).then_inc(S("skip"), 1)
            link(g.memset(W0bd, 0.0))

            def complex_sums(dst, tag, n0, ops):
                for n in range(PAIRS // 2):
                    pool.wait_ge(S("prods"), 4 * (n0 + n + 1))
                    b = (n0 + n) % 2
                    for ri in range(2):
                        last = g.tensor_tensor(dst[:, ri, 2 * n:2 * n + 2], prod[:, b, 2 * ri].rearrange("p (j c) -> p j c", j=2),
                                               prod[:, b, 2 * ri + 1].rearrange("p (j c) -> p j c", j=2), ops[ri])
                        if ri:
                            last.then_inc(S("s5_" + tag), 1)

            complex_sums(Wt, "w", 0, (ALU.subtract, ALU.add))
            pool.wait_ge(S("s5_w"), 12)
            for ri in range(2):
                for g2 in range(2):
                    g.tensor_copy(W0bd[g2 * 64:(g2 + 1) * 64, ri, :, g2 * GDIM:(g2 + 1) * GDIM],
                                  Wt[g2 * 64:(g2 + 1) * 64, ri, :, 7 * GDIM:8 * GDIM]).then_inc(S("s5_w0"), 1)
                    pool.wait_ge(S("s5_w0"), 2 * ri + g2 + 1)
            complex_sums(CA, "ca", 12, (ALU.add, ALU.subtract))
            root("mk", 1, hss[:, 0:16], hrs[:, 0:16], HD)
            for l in range(2):
                for m in range(TM):
                    read_out(pool, ("mkT", l, m))
            g.memset(Tm, 0.0).then_inc(S("tm_zero"), 1)
            root("q0", 1, hss[:, 16:24], hrs[:, 16:24], HD)
            for s in (2, 5):
                pool.wait_ge(S(f"u_step{s}"), 32)
                g.tensor_copy(U5[:, :, s * GDIM:(s + 1) * GDIM], U4[:, s].rearrange("p (g i) -> p g i", i=GDIM)).then_inc(S("u5_pool"), 1)
            for n in range(3):
                read_out(pool, ("Ug", n))
            g.memset(Xbd, 0.0).then_inc(S("xbd_zero"), 1)
            root("f0", 2, ss[:, 0:2], rs[:, 0:2], D)
            got(pool, ("yT", 2))
            link(g.memset(TRI, 1.0))
            g.memset(ONES, 1.0).then_inc(S("tri"), 1)
            link(g.memset(MSK, 0.0))
            g.affine_select(out=TRI, in_=TRI, compare_op=ALU.is_gt, fill=0.0, base=0,
                            pattern=[[1, P]], channel_multiplier=-1).then_inc(S("tri"), 1)
            g.affine_select(out=MSK, in_=MSK, compare_op=ALU.is_ge, fill=NEG, base=0,
                            pattern=[[-1, P]], channel_multiplier=1).then_inc(S("tri"), 1)
            root("kv", 2, ss[:, 2:4], rs[:, 2:4], D)
            root("kvh", 1, hss[:, 0:8], hrs[:, 0:8], HD)
            root("q1", 1, hss[:, 8:40], hrs[:, 8:40], HD)
            root("f1", 2, ss[:, 0:2], rs[:, 0:2], D)

            def lo(turn, q):
                n = 4 * q + 3
                pool.wait_ge(S("hi"), turn.count("hi", n + 1))
                b = n % NPART
                g.tensor_tensor(PART_HL[:, b, 1], at(e_slot(q) * SLOT + 3 * PART, PART), PART_HL[:, b, 0].bitcast(fp),
                                ALU.subtract).then_inc(S("lo_pool"), 1)

            lo(Turn(0, 0), 0)

            def passes(first, end):
                with pool.Fori(first, end) as i:
                    for q in range(1, NI):
                        lo(Turn(i, first), q)
                    lo(Turn(i + 1, first), 0)

            passes(0, NE)
            pool.wait_ge(S("flag"), 1)
            over = pool.value_load(flag[0:1, 0:1], min_val=0, max_val=1)
            with pool.If(over > 0):
                passes(NE, PASSES * NE)

        @block.scalar
        def _(act):
            ac = nc.scalar.activation

            def load(dst, src, sem):
                act.dma_start(dst, src).then_inc(S(sem), 16)

            for m in range(TM):
                load(HS[:, m], w["mem"][0, m * P:(m + 1) * P, :], f"ld_mem{m}")
            load(lam_r.rearrange("j (g p) -> j g p", g=2), w["l0_s5_lam_re"].rearrange("(g j) p -> j g p", g=2), "ld_lam")
            load(lam_i.rearrange("j (g p) -> j g p", g=2), w["l0_s5_lam_im"].rearrange("(g j) p -> j g p", g=2), "ld_lam")
            load(ldt, w["l0_s5_log_dt"].rearrange("(g j) -> j g", g=2), "ld_lam")
            for r, name in ((G_MIX0, "l0_mix_norm"), (G_MEM0, "l0_mem_norm"), (G_FFN0, "l0_ffn_norm"), (G_KV, "kv_norm"),
                            (G_MIX1, "l1_mix_norm"), (G_MEM1, "l1_mem_norm"), (G_FFN1, "l1_ffn_norm")):
                load(grow[r:r + 8, :], w[name].rearrange("(r p) -> r p", p=P), "ld_gains")
            load(grow[G_BGLU:G_BGLU + 6, :], w["l0_s5_b_glu"].rearrange("(r p) -> r p", p=P), "ld_gains")
            for m in range(TM):
                load(XS[:, m], w["x"][0, m * P:(m + 1) * P, :], f"ld_x{m}")
            for ri, name in enumerate(("l0_s5_b_re", "l0_s5_b_im")):
                for g2 in range(2):
                    load(braw[g2 * 64:(g2 + 1) * 64, ri], w[name][g2 * PAIRS:(g2 + 1) * PAIRS].rearrange("j p i -> p j i"), "ld_b")
            for ri, name in enumerate(("l0_s5_c_re", "l0_s5_c_im")):
                for g2 in range(2):
                    load(cnat[:, ri, :, g2 * 64:(g2 + 1) * 64],
                         w[name][g2 * PAIRS:(g2 + 1) * PAIRS].rearrange("(a jj) o p -> (jj o) a p", a=3), "ld_c")
            for g2 in range(2):
                load(Dbc[g2 * GDIM:(g2 + 1) * GDIM], w["l0_s5_d"][g2 * PAIRS * GDIM:(g2 + 1) * PAIRS * GDIM]
                     .rearrange("(a j o) -> a j o", a=1, o=GDIM).to_broadcast([GDIM, PAIRS, GDIM]), "ld_d")
            for n, name in enumerate(("l0_mem_q_gain", "l0_mem_k_gain", "l1_mem_q_gain", "l1_mem_k_gain", "l1_moba_q_gain")):
                load(hg[:, n:n + 1], w[name].rearrange("(p a) -> p a", a=1), "ld_hg")
            load(hgk, w["kv_k_gain"].rearrange("(p a) -> p a", a=1), "ld_hg")
            load(ROUT, w["l1_moe_router"].rearrange("(k p) e -> p k e", p=P), "ld_router")

            def square(src, tag, col, ld=None):
                for m in range(TM):
                    if ld:
                        act.wait_ge(S(f"{ld}{m}"), 16)
                    ac((at(32768, TM, D) if src is HS else HS)[:, m], src[:, m], ACT.Square,
                       accum_out=ss[:, col + m:col + m + 1]).then_inc(S("ss_" + tag), 1)

            def scale_rows(src, tag, col, done):
                act.wait_ge(S("rs_" + tag), 1)
                for m in range(TM):
                    ac(HS[:, m], src[:, m], ACT.Copy, scale=rs[:, col + m:col + m + 1]).then_inc(S(done), 1)

            square(HS, "mem", 0, "ld_mem")
            p = got(act, "gT")
            free(ac(gT, p[:, 0:G_ROWS], ACT.Copy), "gT")
            scale_rows(HS, "mem", 0, "mem_rows")
            act.wait_ge(S("ang"), 1)
            ac(sn, rr, ACT.Sin).then_inc(S("sin"), 1)
            act.wait_ge(S("ang"), 2)
            ac(cs, kk, ACT.Sin).then_inc(S("sin"), 1)

            def gains_out(key, q, outs):
                p = got(act, (key, q))
                for dst, row in outs:
                    for a in range(2):
                        k = 2 * q + a
                        last = ac(dst[:, k], p[:, a * T:(a + 1) * T], ACT.Copy, scale=gT[:, row + k:row + k + 1])
                free(last, (key, q))

            read_out(act, "gT")
            for q in range(4):
                gains_out("memT", q, [(CT, G_MEM0), (HT, G_MEM1)])
            for ri in range(2):
                p = got(act, ("cT", ri))
                free(ac(cT[:, ri], p[:, 0:PAIRS * GDIM], ACT.Copy, scale=1.0 if ri == 0 else -1.0), ("cT", ri))
            square(XS, "x0", 2, "ld_x")
            scale_rows(XS, "x0", 2, "x_rows0")

            def kv_out(tag, rows, vals):
                for m in range(TM):
                    p = got(act, (tag, m))
                    ac(rows(m), p[:, 0:256], ACT.Copy)
                    free(ac(vals(m), p[:, 256:512], ACT.Copy), (tag, m))

            kv_out("mkv1", lambda m: mkrow(1, m), lambda m: vM[1][:, m])
            for q in range(4):
                gains_out("xT0", q, [(HT, G_MIX0)])
            kv_out("mkv0", lambda m: mkrow(0, m), lambda m: vM[0][:, m])
            for h in range(2):
                for m in range(TM):
                    p = got(act, ("win0", h, m))
                    free(ac(HS[:, m, h * 512:(h + 1) * 512], p[:, :], ACT.Copy), ("win0", h, m))
            act.wait_ge(S("gp"), 3)
            for l in (1, 0):
                for m in range(TM):
                    p = got(act, ("mkT", l, m))
                    free(ac(kT[l][:, :, m * P:(m + 1) * P], p[0:HD, :].rearrange("p (h t) -> p h t", h=4), ACT.Copy,
                            scale=gp[:, l:l + 1]), ("mkT", l, m))
            for n in range(12):
                p = got(act, ("Bm", n))
                ri, jq = n // 6, n % 6
                free(ac(Bm[:, ri, jq * 4:jq * 4 + 4], p[:, :].rearrange("p (a c) -> p a c", a=4), ACT.Copy), ("Bm", n))
            for jq in range(6):
                p = got(act, ("K", jq))
                free(ac(Kst[:, jq * 4:jq * 4 + 4], p[0:32, :].rearrange("p (a c) -> p a c", a=4), ACT.Copy), ("K", jq))
            act.wait_ge(S("kst_d"), 1)
            act.wait_ge(S("tm_zero"), 1)
            Tv = Tm.rearrange("p (g j) c -> p g j c", g=2)
            for s in range(STEPS):
                for g2 in range(2):
                    act.dma_start(Tv[s * GDIM:(s + 1) * GDIM, g2, :, s * GDIM:P],
                                  Kst[g2 * GDIM:(g2 + 1) * GDIM, :, 0:P - s * GDIM]).then_inc(S("tm"), 16)
            for h in range(2):
                for m in range(TM):
                    read_out(act, ("win0", h, m))
            act.wait_ge(S("tm"), 16 * 16)
            for s in range(STEPS):
                for m in range(TM):
                    act.dma_start(U4[m * 16:(m + 1) * 16, s], HS[s:P:STEPS, m, 0:MAIN]).then_inc(S(f"u_step{s}"), 16)
            for s in (0, 3, 6):
                act.wait_ge(S(f"u_step{s}"), 32)
                ac(U5[:, :, s * GDIM:(s + 1) * GDIM], U4[:, s].rearrange("p (g i) -> p g i", i=GDIM), ACT.Copy).then_inc(S("u5_act"), 1)
            for n in range(3):
                p = got(act, ("Ug", n))
                free(ac(Ug[:, n * 16:(n + 1) * 16], p[:, :].rearrange("p (a c) -> p a c", a=16), ACT.Copy), ("Ug", n))
            for n in range(3):
                p = got(act, ("V", n))
                dst, src = (VX[:, n, 0:16], p[:, :].rearrange("p (j c) -> p j c", c=CHUNKS)) if n < 2 else \
                    (VX[:, :, 16:24], p[:, :].rearrange("p (r j c) -> p r j c", r=2, c=CHUNKS))
                free(ac(dst, src, ACT.Copy), ("V", n))
            for m in range(TM):
                p = got(act, ("q0T", m))
                free(ac(QT0[:, :, m * P:(m + 1) * P], p[0:HD, :].rearrange("p (h t) -> p h t", h=4), ACT.Copy), ("q0T", m))
            act.wait_ge(S("scan"), 1)
            act.wait_ge(S("xbd_zero"), 1)
            for g2 in range(2):
                ac(Xbd[g2 * 64:(g2 + 1) * 64, 1, :, g2 * 32 + 1:g2 * 32 + 32], VX[g2 * 64:(g2 + 1) * 64, 1, :, 0:31],
                   ACT.Copy).then_inc(S("xbd"), 1)
            for n in range(1, 6, 2):
                p = got(act, ("Y", n))
                free(ac(Ysb[:, :, n * 64:(n + 1) * 64].rearrange("p k (a o) -> p k a o", a=4),
                        p[0:64, :].rearrange("p (a k o) -> p k a o", a=4, k=STEPS), ACT.Copy), ("Y", n))
            for n in range(3):
                p = got(act, ("yT", n))
                for g2 in range(2):
                    last = ac(GT6[:, g2 * 3 + n].rearrange("p (c k) -> p c k", k=STEPS),
                              p[:, :].rearrange("p (k g c) -> p g c k", k=STEPS, g=2)[:, g2], ACT.Gelu_apprx_tanh)
                free(last, ("yT", n))

            def softmax(tag, n, pbuf, masked):
                for a in range(2):
                    act.wait_ge(S(tag + "_max"), 2 * n + a + 1)
                    p = PS_OF(tag, n, a)
                    for m in range(TM):
                        nk = P * (m + 1) if masked(2 * n + a) else T
                        c = 2 * a + m
                        last = ac(pbuf[:, (n % 2) * 2 + a, m * T:m * T + nk], p[:, m * T:m * T + nk], ACT.Exp,
                                  bias=snm[:, n % 2, c:c + 1], accum_out=ssum[:, n % 2, c:c + 1])
                    free(last, (tag, "L", n, a))

            def PS_OF(tag, n, a):
                return PS[units[(tag, "L", n, a)][0]]

            def pt_out(tag, n, pt, masked):
                for a in range(2):
                    p = got(act, (tag, "PT", n, a))
                    d = pt[:, (n % 2) * 2 + a]
                    if masked(2 * n + a):
                        ac(d[:, 0:T], p[:, 0:T], ACT.Copy)
                        last = ac(d[:, T + P:2 * T], p[:, T + P:2 * T], ACT.Copy)
                    else:
                        last = ac(d, p[:, :], ACT.Copy)
                    free(last, (tag, "PT", n, a))

            for n in range(2):
                softmax("m0", n, PB0, lambda h: False)
            for n in range(6):
                if n >= 2:
                    act.wait_ge(S("ct0"), n - 1)
                p = got(act, ("glu", n))
                free(ac(SIG[:, n % 2], p[:, 0:T], ACT.Sigmoid, bias=gT[:, G_BGLU + n:G_BGLU + n + 1]), ("glu", n))
            for n in range(2):
                pt_out("m0", n, PT0, lambda h: False)

            def cols_out(tag, outs):
                for q in (1, 3):
                    gains_out("T" + tag, q, outs)

            def norm(tag, col, parts):
                for key in parts:
                    read_out(act, key)
                square(XS, tag, col)
                scale_rows(XS, tag, col, "rows_" + tag)

            norm("f0", 0, [("wout0", h, m) for h in range(2) for m in range(TM)])
            cols_out("f0", [(HT, G_FFN0)])
            n = 0
            for c in range(len(FCH)):
                for f in range(FCH[c] // P):
                    p = got(act, ("h", c, f))
                    ac(SG0[:, n % 4], p[:, 0:T], ACT.Silu).then_inc(S("sg0"), 1)
                    n += 1
            norm("kv", 2, [("ffn", b) for b in range(4)])
            cols_out("kv", [(CT, G_KV), (HT, G_MIX1)])
            kv_out("kv", lambda m: KVR[:, m], lambda m: VKV[:, m])
            for h in range(2):
                for m in range(TM):
                    p = got(act, ("win1", h, m))
                    free(ac(HS[:, m, h * 512:(h + 1) * 512], p[:, :], ACT.Copy), ("win1", h, m))
            for m in range(TM):
                p = got(act, ("kvT", m))
                free(ac(kTkv[:, :, m * P:(m + 1) * P], p[0:HD, :].rearrange("p (h t) -> p h t", h=4), ACT.Copy,
                        scale=gp[:, 2:3]), ("kvT", m))
            for n in range(1, 8, 2):
                p = got(act, ("q1T", n))
                free(ac(QT1[:, (n // 2) * 4:(n // 2) * 4 + 4, (n % 2) * P:(n % 2 + 1) * P],
                        p[0:HD, :].rearrange("p (h t) -> p h t", h=4), ACT.Copy), ("q1T", n))
            for n in range(9):
                if n < 8:
                    softmax("a1", n, PB1, lambda h: h < 12)
                if n >= 1:
                    pt_out("a1", n - 1, PT1, lambda h: h < 12)
            norm("f1", 0, [("wout1", h, m) for h in range(2) for m in range(TM)])
            cols_out("f1", [(HT, G_FFN1)])
            act.wait_ge(S("rt_d"), 1)
            ac(EX, LG, ACT.Exp).then_inc(S("rt_e"), 1)

            def hi(turn, n, q_turn):
                q, j = n // 4, n % 4
                if j == 0:
                    act.wait_ge(full[e_slot(q)], q_turn.weights(e_need(q)))
                ac(PART_HL[:, n % NPART, 0], at(e_slot(q) * SLOT + j * PART, PART), ACT.Copy).then_inc(S("hi"), 1)

            def xg_out(turn, key):
                for b in range(2):
                    p = got(act, (key, "xg", b), turn)
                    for a in range(4):
                        k = 4 * b + a
                        last = ac(XG[:, 0, k], p[:, a * CAP:(a + 1) * CAP], ACT.Copy, scale=gT[:, G_FFN1 + k:G_FFN1 + k + 1])
                    last.then_inc(S("hi_small"), 1)

            def expert(turn, key):
                later = Turn(turn.i + 1, turn.start)
                for s in range(NPT):
                    n = s + NPART
                    part_free(act, s, turn, key)
                    hi(turn, n % NPT, turn if n < NPT else later)
                    k = n - LEAD
                    if k < NPT and k % 4 == 3 and items[k // 4][0] == "g":
                        c = items[k // 4][1]
                        p = got(act, (key, "gu", c, 0), turn)
                        free(ac(SG1[0:CAP], p[0:CAP, :], ACT.Silu), (key, "gu", c, 0))
                    if k in FLIP_AT:
                        p = got(act, (key, "aT", FLIP_AT[k]), turn)
                        ac(AT[:, 0].rearrange("p f t -> p (f t)"), p[:, 0:4 * CAP], ACT.Copy).then_inc(S("hi_small"), 1)
                    if k == GT_AT:
                        p = got(act, (key, "gt"), turn)
                        free(ac(GATE[0:CAP], p[0:CAP, 0:T], ACT.Copy), (key, "gt"))
                    if k == XG_AT:
                        xg_out(turn, key)
                    if k == NPT - 1:
                        p = got(act, (key, "y", 1), turn)
                        free(ac(YR[0:CAP, 512:1024], p[0:CAP, :], ACT.Copy), (key, "y", 1))

            got(act, "place")
            for n in range(NPART):
                hi(None, n, Turn(0, 0))
            xg_out(None, "first")

            def passes(key, first, end):
                with act.Fori(first, end) as i:
                    expert(Turn(i, first), key)

            passes("main", 0, NE)
            act.wait_ge(S("flag"), 1)
            over = act.value_load(flag[0:1, 0:1], min_val=0, max_val=1)
            with act.If(over > 0):
                passes("over", NE, PASSES * NE)

        @block.vector
        def _(dve):
            v = nc.vector
            n_chain = [0]

            def link(ins):
                n_chain[0] += 1
                ins.then_inc(S("dve_chain"), 1)
                dve.wait_ge(S("dve_chain"), n_chain[0])
                return ins

            tt, tsc = v.tensor_tensor, v.tensor_scalar

            def bc2(x):
                return x.unsqueeze(2).to_broadcast([PAIRS, 2, NSTATE])

            def v2(x):
                return x.rearrange("p (g s) -> p g s", g=2)

            dve.wait_ge(S("ld_lam"), 48)
            dve.wait_ge(S("dt"), 1)
            tt(v2(zr), v2(lam_r), bc2(edt), ALU.mult).then_inc(S("zr"), 1)
            link(tt(v2(zi), v2(lam_i), bc2(edt), ALU.mult))
            link(tsc(kk, zi, 1.0 / (2 * math.pi), None, ALU.mult))
            link(tsc(kk, kk, 12582912.0, None, ALU.add))
            link(tsc(kk, kk, -12582912.0, None, ALU.add))
            c1 = 6.28125
            c2 = 0.0019350051879882812
            c3 = 2 * math.pi - c1 - c2
            link(v.scalar_tensor_tensor(out=rr, in0=kk, scalar=-c1, in1=zi, op0=ALU.mult, op1=ALU.add))
            link(v.scalar_tensor_tensor(out=rr, in0=kk, scalar=-c2, in1=rr, op0=ALU.mult, op1=ALU.add))
            link(v.scalar_tensor_tensor(out=rr, in0=kk, scalar=-c3, in1=rr, op0=ALU.mult, op1=ALU.add))
            pi = 3.1415925
            link(tsc(rr, rr, -pi, pi, ALU.max, ALU.min))
            tsc(t0, rr, -1.0, None, ALU.mult).then_inc(S("ang"), 1)
            dve.wait_ge(S("ang"), 1)
            link(tt(t0, t0, rr, ALU.max))
            tsc(kk, t0, -1.0, math.pi / 2, ALU.mult, ALU.add).then_inc(S("ang"), 1)
            link(tt(t1, lam_r, lam_r, ALU.mult))
            link(tt(t2, lam_i, lam_i, ALU.mult))
            link(tt(t1, t1, t2, ALU.add))
            link(v.reciprocal(zi, t1))
            dve.wait_ge(S("er"), 1)
            dve.wait_ge(S("sin"), 2)
            link(tt(pw[:, 0, 0], er, cs, ALU.mult))
            link(tt(pw[:, 1, 0], er, sn, ALU.mult))
            link(tsc(t0, pw[:, 0, 0], -1.0, None, ALU.add))
            ai = pw[:, 1, 0]
            link(tt(t1, t0, lam_r, ALU.mult))
            link(tt(t2, ai, lam_i, ALU.mult))
            link(tt(t1, t1, t2, ALU.add))
            link(tt(fr, t1, zi, ALU.mult))
            link(tt(t1, ai, lam_r, ALU.mult))
            link(tt(t2, t0, lam_i, ALU.mult))
            link(tt(t1, t1, t2, ALU.subtract))
            link(tt(fi, t1, zi, ALU.mult))

            def cmul(dr, di, ar, ai_, br, bi, n):
                w0, w1 = (x[:, 0:n * P].rearrange("p (n c) -> p n c", n=n) for x in (u0, u1))
                b_ = lambda x: x.unsqueeze(1).to_broadcast([PAIRS, n, P])
                tt(w0, ar, b_(br), ALU.mult)
                link(tt(w1, ai_, b_(bi), ALU.mult))
                link(tt(dr, w0, w1, ALU.subtract))
                tt(w0, ar, b_(bi), ALU.mult)
                link(tt(w1, ai_, b_(br), ALU.mult))
                return link(tt(di, w0, w1, ALU.add))

            cmul(pw[:, 0, 1:2], pw[:, 1, 1:2], pw[:, 0, 0:1], pw[:, 1, 0:1], pw[:, 0, 0], pw[:, 1, 0], 1)
            cmul(pw[:, 0, 2:4], pw[:, 1, 2:4], pw[:, 0, 0:2], pw[:, 1, 0:2], pw[:, 0, 1], pw[:, 1, 1], 2)
            cmul(pw[:, 0, 4:8], pw[:, 1, 4:8], pw[:, 0, 0:4], pw[:, 1, 0:4], pw[:, 0, 3], pw[:, 1, 3], 4)
            v.tensor_copy(cm[:, 0, 7], fr)
            link(v.tensor_copy(cm[:, 1, 7], fi))
            for s0, n in ((3, 4), (0, 3)):
                for s in range(s0, s0 + n):
                    m = 7 - s
                    cmul(cm[:, 0, s:s + 1], cm[:, 1, s:s + 1], pw[:, 0, m - 1:m], pw[:, 1, m - 1:m], fr, fi, 1)
            tsc(t0[0:1, 0:1], t0[0:1, 0:1], 1.0, None, ALU.mult).then_inc(S("s5_cm"), 1)
            tsc(t1[0:1, 0:1], t1[0:1, 0:1], 1.0, None, ALU.mult).then_inc(S("s5_pw"), 1)

            def products(bank, key, x, n0, combos, tag):
                p = got(dve, key)
                fac = p[:, 0:16 * PAIRS].rearrange("p (r n j) -> p r j n", r=2, n=8)
                for n in range(PAIRS // 2):
                    t = n0 + n
                    if t >= 2:
                        dve.wait_ge(S("s5_w") if t - 2 < 12 else S("s5_ca"), t - 1 if t - 2 < 12 else t - 13)
                    for q, (fri, xri) in enumerate(combos):
                        last = tt(prod[:, t % 2, q].rearrange("p (j n i) -> p j n i", j=2, n=8),
                                  fac[:, fri, 2 * n:2 * n + 2].unsqueeze(3).to_broadcast([P, 2, 8, GDIM]),
                                  x[:, xri, 2 * n:2 * n + 2].unsqueeze(2).to_broadcast([P, 2, 8, GDIM]), ALU.mult)
                        last.then_inc(S("prods"), 1)
                return p, last

            dve.wait_ge(S("ld_b"), 64)
            p, last = products(6, "q_cm", braw, 0, ((0, 0), (1, 1), (0, 1), (1, 0)), "w")
            for ri in range(2):
                read_out(dve, ("cT", ri))
            read_out(dve, "gT")
            p, last = products(7, "q_pw", cT, 12, ((0, 0), (1, 1), (0, 1), (1, 0)), "ca")
            for o, (a, b) in enumerate(((0, 1), (1, 0))):
                re = p[:, 7 * PAIRS:8 * PAIRS]
                im = p[:, 15 * PAIRS:16 * PAIRS]
                cp = v.tensor_copy(A8[:, o, o], re)
                if o == 0:
                    free(cp, "q_cm")
                last = tsc(A8[:, o, 1 - o], im, -1.0 if o == 0 else 1.0, None, ALU.mult)
            free(last, "q_pw")
            dve.wait_ge(S("ld_hg"), 96)
            for n, (a, b) in enumerate(((hg[:, 0:1], hg[:, 1:2]), (hg[:, 2:3], hg[:, 3:4]), (hg[:, 4:5], hgk))):
                tsc(gp[:, n:n + 1], a, b, SCALE, ALU.mult, ALU.mult).then_inc(S("gp"), 1)

            def head_norm(rows, nh, tag, c0, sq, done):
                sqv = sq.rearrange("p (h d) -> p h d", d=HD)
                k = 0
                for r, n in rows:
                    last = tt(sqv[:, k:k + n], r, r, ALU.mult)
                    k += n
                link(last)
                v.tensor_reduce(out=hss[:, c0:c0 + nh], in_=sqv[:, 0:nh], axis=AX.X, op=ALU.add).then_inc(S("ss_" + tag), 1)
                dve.wait_ge(S("rs_" + tag), 1)
                k = c0
                for r, n in rows:
                    last = tt(r, r, hrs[:, k:k + n].unsqueeze(2).to_broadcast([P, n, HD]), ALU.mult)
                    k += n
                last.then_inc(S(done), 1)

            def heads_of(x):
                return x.rearrange("p (h d) -> p h d", d=HD)

            for m in range(TM):
                read_out(dve, ("mkv1", m))
                read_out(dve, ("mkv0", m))
            head_norm([(heads_of(MKR.rearrange("p a b -> p (a b)")), 16)], 16, "mk", 0, sqk, "mk_rows")
            for jq in range(6):
                read_out(dve, ("K", jq))
            dve.wait_ge(S("skip"), 1)
            tt(Kst[:, :, 0:GDIM], Kst[:, :, 0:GDIM], MD, ALU.add).then_inc(S("kst_d"), 1)
            dve.wait_ge(S("kst_d"), 1)
            for h in range(2):
                for m in range(TM):
                    read_out(dve, ("win0", h, m))
            head_norm([(heads_of(HS[:, m, MAIN:D]), 4) for m in range(TM)], 8, "q0", 16, sq0, "q0_rows")
            for s in (1, 4, 7):
                dve.wait_ge(S(f"u_step{s}"), 32)
                v.tensor_copy(U5[:, :, s * GDIM:(s + 1) * GDIM], U4[:, s].rearrange("p (g i) -> p g i", i=GDIM)).then_inc(S("u5_dve"), 1)
            for n in range(3):
                read_out(dve, ("V", n))
            for c in range(1, CHUNKS - 1):
                link(tt(stp, A8, VX[:, :, :, c - 1].unsqueeze(1).to_broadcast([P, 2, 2, PAIRS]), ALU.mult))
                link(tt(stp[:, :, 0], stp[:, :, 0], stp[:, :, 1], ALU.add))
                link(tt(VX[:, :, :, c], VX[:, :, :, c], stp[:, :, 0], ALU.add))
            v.memset(stp[:, 0, 0, 0:1], 0.0).then_inc(S("scan"), 1)
            dve.wait_ge(S("xbd_zero"), 1)
            for g2 in range(2):
                v.tensor_copy(Xbd[g2 * 64:(g2 + 1) * 64, 0, :, g2 * 32 + 1:g2 * 32 + 32],
                              VX[g2 * 64:(g2 + 1) * 64, 0, :, 0:31]).then_inc(S("xbd"), 1)
            for n in range(0, 6, 2):
                p = got(dve, ("Y", n))
                free(v.tensor_copy(Ysb[:, :, n * 64:(n + 1) * 64].rearrange("p k (a o) -> p k a o", a=4),
                                   p[0:64, :].rearrange("p (a k o) -> p k a o", a=4, k=STEPS)), ("Y", n))

            def maxima(tag, n, masked):
                for a in range(2):
                    p = got(dve, (tag, "L", n, a))
                    c = 2 * a
                    if masked(2 * n + a):
                        tt(p[:, 0:P], p[:, 0:P], MSK, ALU.add)
                        link(tt(p[:, T + P:2 * T], p[:, T + P:2 * T], MSK, ALU.add))
                        v.tensor_reduce(out=snm[:, n % 2, c:c + 1], in_=p[:, 0:P], axis=AX.X, op=ALU.max, negate=True)
                        last = v.tensor_reduce(out=snm[:, n % 2, c + 1:c + 2], in_=p[:, T:2 * T], axis=AX.X, op=ALU.max,
                                               negate=True)
                    else:
                        last = v.tensor_reduce(out=snm[:, n % 2, c:c + 2], in_=p[:, :].rearrange("p (m k) -> p m k", m=2),
                                               axis=AX.X, op=ALU.max, negate=True)
                    last.then_inc(S(tag + "_max"), 1)

            def normalise(tag, n, pbuf, masked):
                for a in range(2):
                    read_out(dve, (tag, "L", n, a))
                link(v.reciprocal(srec[:, n % 2], ssum[:, n % 2]))
                for a in range(2):
                    for m in range(TM):
                        nk = P * (m + 1) if masked(2 * n + a) else T
                        x = pbuf[:, (n % 2) * 2 + a, m * T:m * T + nk]
                        last = tsc(x, x, srec[:, n % 2, 2 * a + m:2 * a + m + 1], None, ALU.mult)
                    last.then_inc(S(tag + "_p"), 1)

            def o_out(tag, n, heads):
                for a in range(2):
                    _, _, _, tile, half = heads[2 * n + a]
                    p = got(dve, (tag, "O", n, a))
                    free(v.tensor_copy(CT[64 * half:64 * half + 64, tile], p[64 * half:64 * half + 64, 0:T])
                         , (tag, "O", n, a))

            no = lambda h: False
            maxima("m0", 0, no)
            maxima("m0", 1, no)
            normalise("m0", 0, PB0, no)
            normalise("m0", 1, PB0, no)
            for n in range(6):
                read_out(dve, ("glu", n))
                tt(CT[:, n], SIG[:, n % 2], GT6[:, n], ALU.mult).then_inc(S("ct0"), 1)
            o_out("m0", 0, M0_HEADS)
            o_out("m0", 1, M0_HEADS)

            def residual(keys):
                for h, m, key in keys:
                    p = got(dve, key)
                    x = XS[:, m, h * 512:(h + 1) * 512]
                    free(tt(x, x, p[:, :], ALU.add), key)

            def cols_out(tag, outs):
                for q in (0, 2):
                    p = got(dve, ("T" + tag, q))
                    for dst, row in outs:
                        for a in range(2):
                            k = 2 * q + a
                            last = tsc(dst[:, k], p[:, a * T:(a + 1) * T], gT[:, row + k:row + k + 1], None, ALU.mult)
                    free(last, ("T" + tag, q))

            residual([(h, m, ("wout0", h, m)) for h in range(2) for m in range(TM)])
            cols_out("f0", [(HT, G_FFN0)])
            n = 0
            for c in range(len(FCH)):
                for f in range(FCH[c] // P):
                    dve.wait_ge(S("sg0"), n + 1)
                    free(tt(HID0[:, c % 2, f], SG0[:, n % 4], PS[units[("h", c, f)][0]][:, T:2 * T], ALU.mult), ("h", c, f))
                    n += 1
            residual([(h, m, ("ffn", 2 * h + m)) for h in range(2) for m in range(TM)])
            cols_out("kv", [(CT, G_KV), (HT, G_MIX1)])
            for m in range(TM):
                read_out(dve, ("kv", m))
            head_norm([(heads_of(KVR.rearrange("p a b -> p (a b)")), 8)], 8, "kvh", 0, sq1, "kv_rows")
            for h in range(2):
                for m in range(TM):
                    read_out(dve, ("win1", h, m))
            head_norm([(heads_of(HS.rearrange("p a b -> p (a b)")), 32)], 32, "q1", 8, sq1, "q1_rows")
            for n in range(0, 8, 2):
                p = got(dve, ("q1T", n))
                free(v.tensor_copy(QT1[:, (n // 2) * 4:(n // 2) * 4 + 4, (n % 2) * P:(n % 2 + 1) * P],
                                   p[0:HD, :].rearrange("p (h t) -> p h t", h=4)), ("q1T", n))
            dve.wait_ge(S("tri"), 3)
            ca = lambda h: h < 12
            for n in range(9):
                if n < 8:
                    maxima("a1", n, ca)
                    normalise("a1", n, PB1, ca)
                if n >= 1:
                    o_out("a1", n - 1, A1_HEADS)
            residual([(h, m, ("wout1", h, m)) for h in range(2) for m in range(TM)])
            cols_out("f1", [(HT, G_FFN1)])
            link(v.memset(LOWER, 0.0))
            for e in range(1, NE):
                last = v.memset(LOWER[:, e, 0:e], 1.0)
            link(last)
            p = got(dve, "router")
            free(v.tensor_copy(LG, p[:, 0:TM * NE].rearrange("p (m e) -> p m e", m=TM)), "router")
            read_out(dve, "router")
            for m in range(TM):
                me = LG[:, m].unsqueeze(2).to_broadcast([P, NE, NE])
                ot = LG[:, m].unsqueeze(1).to_broadcast([P, NE, NE])
                tt(CMP, ot, me, ALU.is_gt)
                link(tt(CMP2, ot, me, ALU.is_equal))
                link(tt(CMP2, CMP2, LOWER, ALU.mult))
                link(tt(CMP, CMP, CMP2, ALU.add))
                link(v.tensor_reduce(out=RNK[:, m], in_=CMP, axis=AX.X, op=ALU.add))
            tsc(SEL, RNK, 1.5, None, ALU.is_lt).then_inc(S("sel"), 1)
            link(v.tensor_reduce(out=vt[:, 0:2], in_=LG, axis=AX.X, op=ALU.max))
            tt(LG, LG, vt[:, 0:2].unsqueeze(2).to_broadcast([P, TM, NE]), ALU.subtract).then_inc(S("rt_d"), 1)
            dve.wait_ge(S("rt_e"), 1)
            link(tt(EX, EX, SEL, ALU.mult))
            link(v.tensor_reduce(out=vt[:, 2:4], in_=EX, axis=AX.X, op=ALU.add))
            link(v.reciprocal(vt[:, 4:6], vt[:, 2:4]))
            for r in range(PASSES):
                last = tt(GW[:, :, r * NE:(r + 1) * NE], EX, vt[:, 4:6].unsqueeze(2).to_broadcast([P, TM, NE]), ALU.mult)
            link(last)
            p = got(dve, "place")
            link(tsc(POS0, p[:, 0:TM * NE].rearrange("p (m e) -> p m e", m=TM), 1.0, None, ALU.add))
            link(tt(POS0, POS0, SEL, ALU.mult))
            link(v.memset(POS, -1.0))
            for r in range(PASSES):
                last = tsc(POS[:, :, r * NE:(r + 1) * NE], POS0, -1.0 - CAP * r, None, ALU.add)
            link(last)
            free(v.tensor_reduce(out=vt[:, 6:7], in_=p[:, 2 * NE:3 * NE], axis=AX.X, op=ALU.max), "place")
            read_out(dve, "place")
            tsc(flag, vt[:, 6:7], CAP + 0.5, None, ALU.is_gt).then_inc(S("flag"), 1)

            def pick(i):
                for m in range(TM):
                    last = tsc(PICK[:, m], iota, POS[:, m, bass.ds(i, 1)], None, ALU.is_equal)
                last.then_inc(S("pick"), 1)

            def lo(turn, n):
                q, j, b = n // 4, n % 4, n % NPART
                dve.wait_ge(S("hi"), turn.count("hi", n + 1))
                tt(PART_HL[:, b, 1], at(e_slot(q) * SLOT + j * PART, PART), PART_HL[:, b, 0].bitcast(fp),
                   ALU.subtract).then_inc(S("lo_dve"), 1)

            def xg_out(turn, key):
                for b in range(2):
                    dve.wait_ge(S("hi_small"), b + 1 if turn is None else turn.count("hi_small", NC_E + b + 1))
                    p = PS[7 - b]
                    for a in range(4):
                        k = 4 * b + a
                        last = v.scalar_tensor_tensor(XG[:, 1, k], p[:, a * CAP:(a + 1) * CAP], gT[:, G_FFN1 + k:G_FFN1 + k + 1],
                                                      XG[:, 0, k].bitcast(fp), ALU.mult, ALU.subtract)
                    free(last, (key, "xg", b))

            def x_add(turn, key, bt, n, m):
                p = got(dve, (key, "sc", n, m), bt)
                x = XS[:, m, n * 512:(n + 1) * 512]
                free(tt(x, x, p[:, :], ALU.add), (key, "sc", n, m))

            def expert(turn, key):
                later = Turn(turn.i + 1, turn.start)
                for s in range(NPT):
                    n = s + NPART
                    if n % 4 < 3:
                        lo(turn if n < NPT else later, n % NPT)
                    k = n - LEAD
                    if k < NPT and k % 4 == 3 and items[k // 4][0] == "u":
                        c = items[k // 4][1]
                        p = got(dve, (key, "gu", c, 1), turn)
                        read_out(dve, (key, "gu", c, 0), turn)
                        free(tt(HID[0:CAP], SG1[0:CAP], p[0:CAP, :], ALU.mult), (key, "gu", c, 1))
                    if k in SC_AT:
                        x_add(turn, key, turn, *SC_AT[k])
                    if k in FLIP_AT:
                        dve.wait_ge(S("hi_small"), turn.count("hi_small", FLIP_AT[k] + 1))
                        free(tt(AT[:, 1].rearrange("p f t -> p (f t)"), PS[6][:, 0:4 * CAP],
                                AT[:, 0].rearrange("p f t -> p (f t)").bitcast(fp), ALU.subtract), (key, "aT", FLIP_AT[k]))
                    if k == GT_AT - 8:
                        dve.wait_ge(S("pick"), turn.count("pick", 0))
                        for m in range(TM):
                            last = tsc(PG[:, m], PICK[:, m], GW[:, m, bass.ds(turn.i, 1)], None, ALU.mult)
                        last.then_inc(S("pgate"), 1)
                    if k == GT_AT + 8:
                        pick(turn.i + 1)
                    if k == XG_AT:
                        xg_out(turn, key)
                    if k == NPT - 1:
                        p = got(dve, (key, "y", 0), turn)
                        free(v.tensor_copy(YR[0:CAP, 0:512], p[0:CAP, :]), (key, "y", 0))

            dve.wait_ge(S("iota"), 1)
            v.memset(YR, 0.0)
            v.memset(GATE, 0.0)
            pick(0)
            for n in range(NPART):
                if n % 4 < 3:
                    lo(Turn(0, 0), n)
            xg_out(None, "first")

            def passes(key, first, end):
                with dve.Fori(first, end) as i:
                    expert(Turn(i, first), key)
                for n, m in SC_AT.values():
                    x_add(Turn(end, first), (key, "end"), None, n, m)

            passes("main", 0, NE)
            dve.wait_ge(S("flag"), 1)
            over = dve.value_load(flag[0:1, 0:1], min_val=0, max_val=1)
            with dve.If(over > 0):
                v.memset(GATE, 0.0).then_inc(S("gate_zero"), 1)
                passes("over", NE, PASSES * NE)
            v.memset(vt[:, 8:9], 0.0).then_inc(S("x_final"), 1)


_INS = ['x', 'mem', 'l0_mix_norm', 'l0_w_in', 'l0_s5_lam_re', 'l0_s5_lam_im', 'l0_s5_log_dt', 'l0_s5_b_re', 'l0_s5_b_im',
        'l0_s5_c_re', 'l0_s5_c_im', 'l0_s5_d', 'l0_s5_w_glu', 'l0_s5_b_glu', 'l0_mem_norm', 'l0_w_mem_k', 'l0_w_mem_v',
        'l0_mem_q_gain', 'l0_mem_k_gain', 'l0_w_out', 'l0_ffn_norm', 'l0_ffn_w_gate', 'l0_ffn_w_up', 'l0_ffn_w_down',
        'kv_norm', 'kv_w_k', 'kv_w_v', 'kv_k_gain', 'l1_mix_norm', 'l1_w_in', 'l1_moba_q_gain', 'l1_mem_norm',
        'l1_w_mem_k', 'l1_w_mem_v', 'l1_mem_q_gain', 'l1_mem_k_gain', 'l1_w_out', 'l1_ffn_norm', 'l1_moe_router',
        'l1_moe_w_gate', 'l1_moe_w_up', 'l1_moe_w_down']


def kernel(**inputs):
    import numpy as _np
    import concourse.bacc as _bacc
    from concourse import mybir as _mybir
    from concourse.bass_utils import run_bass_kernel_spmd as _run

    nc = _bacc.Bacc("TRN2", target_bir_lowering=False, num_devices=1)
    arrays, w = {}, {}
    for name in _INS:
        a = _np.ascontiguousarray(inputs[name])
        arrays["in_" + name] = a
        w[name] = nc.dram_tensor("in_" + name, a.shape, _mybir.dt.from_np(a.dtype), kind="ExternalInput").ap()
    out = nc.dram_tensor("out_x", (1, T, D), _mybir.dt.float32, kind="ExternalOutput").ap()
    trunk(nc, w, out)
    r = _run(nc, [arrays], core_ids=[0])
    return r.results[0]["out_x"]
```

```python
import math

import numpy as np
import concourse.bass as bass
from concourse import mybir
from contextlib import ExitStack

P = 128
T = 256
TM = T // P
D = 1024
KT = D // P
HD = 64
GROUPS, GDIM, NSTATE = 48, 16, 64
MAIN = GROUPS * GDIM
PAIRS = GROUPS // 2
STEPS = 8
CHUNKS = T // STEPS
NE, FFE = 8, 3584
CAP = 128
PASSES = -(-T // CAP)
NC_E = FFE // 512
EPS = 1e-6
SCALE = HD ** -0.5
NEG = -1e30
SLOT = 4096
NSLOT = 7
PART = SLOT // 4
NFP = 3
NPART = 6

G_MIX0, G_MEM0, G_FFN0, G_KV, G_MIX1, G_MEM1, G_FFN1, G_BGLU = (8 * n for n in range(8))
G_ROWS = 8 * 7 + 6


def trunk(nc, w, out):
    fp, f32r, i32 = mybir.dt.float32, mybir.dt.float32r, mybir.dt.int32
    ALU, ACT, AX = mybir.AluOpType, mybir.ActivationFunctionType, mybir.AxisListType
    ctx = ExitStack()
    with ctx:
        ctx.enter_context(nc.allow_non_contiguous_dma(reason="short head gain vectors"))
        sems = {}

        def S(name):
            if name not in sems:
                sems[name] = ctx.enter_context(nc.semaphore(name))
            return sems[name]

        BASE, RING_END, END = -(-nc.sbuf_base // 64) * 64, NSLOT * SLOT, 53200
        ring = nc.alloc_sbuf_tensor_at("ring", [P, RING_END], fp, offset=BASE)
        work = nc.alloc_sbuf_tensor_at("work", [P, END - RING_END], fp, offset=BASE + 4 * RING_END)
        PS = [ctx.enter_context(nc.psum_tensor(f"bank{b}", [P, 512], fp)) for b in range(8)]

        def at(off, *shape, rows=P, row0=0):
            n = int(np.prod(shape))
            assert off >= RING_END or off + n <= RING_END
            v = ring[row0:row0 + rows, off:off + n] if off < RING_END else work[row0:row0 + rows, off - RING_END:off - RING_END + n]
            if len(shape) == 2:
                v = v.rearrange("p (a b) -> p a b", a=shape[0])
            if len(shape) == 3:
                v = v.rearrange("p (a b c) -> p a b c", a=shape[0], b=shape[1])
            return v

        def cut(off, end):
            cur = [off]

            def take(*shape, rows=P):
                n = int(np.prod(shape))
                v = at(cur[0], *shape, rows=rows)
                cur[0] += n
                assert cur[0] <= end, (cur[0], end)
                return v
            return take

        XS = at(28672, TM, D)
        HS0 = 30720
        HS = at(HS0, TM, D)
        HT0 = 32768
        HT = at(HT0, KT, T)
        CT0 = 34816
        CT = at(CT0, KT, T)
        A0, B0, C0 = 36864, 43008, 49152
        take_c = cut(C0, 53200)
        kT = [take_c(4, T, rows=HD), take_c(4, T, rows=HD)]
        vM = [take_c(TM, 256), take_c(TM, 256)]
        ident = take_c(P)
        iota = take_c(CAP)
        gT = take_c(G_ROWS)
        hg = take_c(5, rows=HD)
        hgk = take_c(1, rows=HD)
        gp = take_c(3, rows=HD)
        mh = take_c(32)
        ss = take_c(4)
        rs = take_c(4)
        hss = take_c(64)
        hrs = take_c(64)
        snm = take_c(2, 4)
        ssum = take_c(2, 4)
        srec = take_c(2, 4)
        A8 = take_c(2, 2, PAIRS)
        ROUT = take_c(KT, NE)
        flag = take_c(1).bitcast(i32)

        Tm = at(12288, GROUPS, P)
        Bm = at(18432, 2, PAIRS, P)
        KX = 24576
        W0bd = at(KX, 2, PAIRS, 32)
        prod = at(KX + 1536, 2, 4, 2 * P)
        MD = at(KX + 3584, PAIRS, GDIM, rows=32)
        Ug = at(HT0, GROUPS, CHUNKS)
        VX = at(CT0, 2, PAIRS, CHUNKS)
        stp = at(HT0 + 1536, 2, 2, PAIRS)
        sq0 = at(CT0 + 1536, 512)
        CA = at(A0, 2, PAIRS, P)
        Wt = at(B0, 2, PAIRS, P)
        Kst = at(B0, PAIRS, P, rows=32)
        U4 = at(A0, STEPS, MAIN, rows=CHUNKS)
        U5 = at(A0, GROUPS, P, rows=CHUNKS, row0=CHUNKS)
        Ysb = at(B0, STEPS, PAIRS * GDIM, rows=64)
        Xbd = at(B0 + 3072, 2, PAIRS, 64)
        GT6 = at(32768, 6, T)
        misc = cut(8192, 12288)
        braw = misc(2, PAIRS, GDIM)
        cT = misc(2, PAIRS, GDIM)
        cnat = misc(2, 3, P)
        Dbc = misc(PAIRS, GDIM, rows=32)
        mask16 = misc(GDIM, rows=32)
        grow = misc(P, rows=G_ROWS)
        tr = cut(18432, 24576)
        lam_r, lam_i, ldt, edt = tr(P, rows=PAIRS), tr(P, rows=PAIRS), tr(2, rows=PAIRS), tr(2, rows=PAIRS)
        zr, zi, er, kk, rr, sn, cs = (tr(P, rows=PAIRS) for _ in range(7))
        fr, fi, t0, t1, t2 = (tr(P, rows=PAIRS) for _ in range(5))
        pw = tr(2, 8, P, rows=PAIRS)
        cm = tr(2, 8, P, rows=PAIRS)
        u0 = at(8192 + 3000, 4 * P, rows=PAIRS)
        u1 = at(8192 + 3000 + 512, 4 * P, rows=PAIRS)
        assert 3000 + 1024 <= SLOT
        MEMR = at(CT0, TM, D)
        MT = [at(12288, KT, T), at(14336, KT, T)]
        MKR = at(8192 + 3000, 4, 256)
        sqk = at(KX + 1536, 1024)
        PB0, PT0, QT0 = at(HS0, 4, 2 * T), at(A0, 4, 2 * T), at(KX, 4, T, rows=HD)
        SIG = at(A0 + 4608, 2, T)
        def hi_lo(name, off, *shape):
            return nc.alloc_sbuf_tensor_at(name, [P, *shape], f32r, offset=BASE + 4 * off)

        HTHL = hi_lo("ht_hl", HT0, 2, KT, T)
        FPART = hi_lo("fpart_hl", A0, NFP, 2, PART)
        HIDHL = hi_lo("hid_hl", B0, 2, 2, 4, T)
        SG0 = at(B0 + 4096, 4, T)
        HID0 = at(B0 + 5120, 4, T)
        PT1, KVR, VKV, kTkv = at(A0, 4, 2 * T), at(A0 + 2048, TM, 256), at(A0 + 2560, TM, 256), at(A0 + 3072, 4, T, rows=HD)
        TRI, ONES = at(A0 + 4096, P), at(A0 + 4224, P)
        MSK = at(A0 + 5120, P)
        QT1, PB1 = at(B0, 16, T, rows=HD), at(B0 + 4096, 4, 2 * T)
        sq1 = at(B0 + 4096, 2 * D)
        PART_HL = hi_lo("part_hl", HT0, NPART, 2, PART)
        XG = hi_lo("xg_hl", C0, 2, KT, CAP)
        AT = hi_lo("at_hl", C0 + 2 * KT * CAP, 2, 4, CAP)
        mo = cut(HT0 + NPART * 2 * PART, B0 + 6144)
        PICK, PG, HID, YR, GATE, SG1 = mo(TM, CAP), mo(TM, CAP), mo(512), mo(D), mo(T), mo(512)
        LG, SEL, RNK, EX, POS0 = (mo(TM, NE) for _ in range(5))
        CMP, CMP2, LOWER = mo(NE, NE), mo(NE, NE), mo(NE, NE)
        POS, GW = mo(TM, PASSES * NE + 1), mo(TM, PASSES * NE)
        vt = mo(16)

        def q_scale(tag, h):
            return hrs[:, 16:24].rearrange("p (m h) -> p m h", m=TM)[:, :, h] if tag == "m0" else \
                hrs[:, 8:40].rearrange("p (m h) -> p m h", m=TM)[:, :, h]

        def mkrow(l, m):
            return MKR[:, 2 * l + m]

        M0_HEADS = [(h, kT[0][:, h], vM[0][:, :, h * HD:(h + 1) * HD], 6 + h // 2, h % 2) for h in range(4)]
        A1_HEADS = [(h, kTkv[:, h // 3], VKV[:, :, (h // 3) * HD:(h // 3 + 1) * HD], h // 2, h % 2) for h in range(12)] \
            + [(h, kT[1][:, h - 12], vM[1][:, :, (h - 12) * HD:(h - 11) * HD], h // 2, h % 2) for h in range(12, 16)]

        def cols(name, n0, n, kt=KT):
            return [(lambda s: s[:, 0:kt * n].rearrange("p (k n) -> p k n", k=kt),
                     w[name][:, n0:n0 + n].rearrange("(k p) n -> p k n", p=P))]

        def kv_pair(a, b):
            return [(lambda s: s[:, 0:2048].rearrange("p (k n) -> p k n", k=KT), w[a].rearrange("(k p) n -> p k n", p=P)),
                    (lambda s: s[:, 2048:4096].rearrange("p (k n) -> p k n", k=KT), w[b].rearrange("(k p) n -> p k n", p=P))]

        def rows_of(name, r0, r):
            return [(lambda s: s[:, 0:r // P * D].rearrange("p (k n) -> p k n", n=D),
                     w[name][r0:r0 + r, :].rearrange("(k p) n -> p k n", p=P))]

        FCH = [512] * 5 + [256]
        stream = [("win0a", cols("l0_w_in", 0, 512)), ("win0b", cols("l0_w_in", 512, 512)),
                  ("memkv0", kv_pair("l0_w_mem_k", "l0_w_mem_v")), ("memkv1", kv_pair("l1_w_mem_k", "l1_w_mem_v")),
                  ("glua", cols("l0_s5_w_glu", 0, 512, 6)), ("glub", cols("l0_s5_w_glu", 512, 256, 6)),
                  ("wout0a", cols("l0_w_out", 0, 512)), ("wout0b", cols("l0_w_out", 512, 512))]
        for c in range(len(FCH) + 1):
            if c < len(FCH):
                stream.append((f"g{c}", cols("l0_ffn_w_gate", 512 * c, FCH[c])))
                stream.append((f"u{c}", cols("l0_ffn_w_up", 512 * c, FCH[c])))
            if c >= 1:
                stream.append((f"d{c - 1}", rows_of("l0_ffn_w_down", 512 * (c - 1), FCH[c - 1])))
        stream += [("kv", kv_pair("kv_w_k", "kv_w_v")),
                   ("win1a", cols("l1_w_in", 0, 512)), ("win1b", cols("l1_w_in", 512, 512)),
                   ("wout1a", cols("l1_w_out", 0, 512)), ("wout1b", cols("l1_w_out", 512, 512))]
        NA = len(stream)
        NAMES = [n for n, _ in stream]

        def slot_of(n):
            return n % 2 if n < 6 else (n - 4) % NSLOT

        filled, need = [0] * NSLOT, []
        for n, (_, dmas) in enumerate(stream):
            filled[slot_of(n)] += 16 * len(dmas)
            need.append(filled[slot_of(n)])
        items = [("g", 0), ("u", 0)]
        for c in range(1, NC_E):
            items += [("g", c), ("u", c), ("d", c - 1)]
        items += [("d", NC_E - 1)]
        NI = len(items)
        assert NI == 3 * NSLOT
        full = [S(f"slot_full{s}") for s in range(NSLOT)]

        def e_slot(q):
            return slot_of(NA + q)

        def e_need(q):
            s = e_slot(q)
            return filled[s] + 16 * (sum(e_slot(r) == s for r in range(q + 1)))

        bank_full = [S(f"bank_full{b}") for b in range(8)]
        bank_free = [S(f"bank_free{b}") for b in range(8)]
        uses, units = [0] * 8, {}
        PER = [4, 4, 3, 3, 1, 1, NC_E + 1, 6]
        NPT = 4 * NI
        ends_bank = {4 * q + 3: items[q] for q in range(NI) if items[q][0] != "d" or items[q][1] == NC_E - 1}
        TALLY = {"pick": (1, 1), "pgate": (0, 1), "hi": (0, NPT), "lo_dve": (0, 3 * NI), "lo_pool": (0, NI),
                 "part_used": (0, NPT - len(ends_bank)), "hi_small": (2, NC_E + 2)}

        class Turn:
            def __init__(self, i, start):
                self.i, self.start = i, start

            def value(self, base, per):
                return self.i * per + (base - self.start * per)

            def count(self, name, k):
                pre, per = TALLY[name]
                return self.i * per + (pre + k)

            def weights(self, base):
                return self.i * (3 * 16) + base

        def unit(pe, key, b, turn=None):
            n = uses[b]
            uses[b] += 1
            units[key] = (b, n)
            if turn is not None:
                pe.wait_ge(bank_free[b], turn.value(n, PER[b]))
            elif n:
                pe.wait_ge(bank_free[b], n)
            return PS[b]

        def ready(ins, key):
            ins.then_inc(bank_full[units[key][0]], 1)

        def got(eng, key, turn=None):
            b, n = units[key]
            eng.wait_ge(bank_full[b], n + 1 if turn is None else turn.value(n + 1, PER[b]))
            return PS[b]

        def free(ins, key):
            ins.then_inc(bank_free[units[key][0]], 1)

        def read_out(eng, key, turn=None):
            b, n = units[key]
            eng.wait_ge(bank_free[b], n + 1 if turn is None else turn.value(n + 1, PER[b]))

        FLIP_AT = {4 * items.index(("g", c + 1)): c for c in range(NC_E - 1)}
        FLIP_AT[4 * items.index(("d", NC_E - 2)) + 3] = NC_E - 1
        SC_AT = {8 + 2 * r: (r // TM, r % TM) for r in range(2 * TM)}
        GT_AT = 4 * items.index(("g", 3)) + 1
        XG_AT = 4 * items.index(("d", NC_E - 2)) + 3
        LEAD = 3

        def part_free(eng, n, turn, key):
            if n in ends_bank:
                kind, c = ends_bank[n]
                got(eng, (key, "y", 1) if kind == "d" else (key, "gu", c, "gu".index(kind)), turn)
            else:
                eng.wait_ge(S("part_used"), turn.count("part_used", sum(r not in ends_bank for r in range(n + 1))))

        fparts, f_last = [], {}
        for name in NAMES:
            if name[0] in "gud" and name[1:].isdigit():
                c = int(name[1:])
                for j in range(KT * FCH[c] // PART):
                    fparts.append((name[0], c, j))
                f_last[name] = len(fparts) - 1
        f_bank = {f_last[f"u{c}"]: ("h", c, FCH[c] // P - 1) for c in range(len(FCH))}
        f_bank[f_last[f"d{len(FCH) - 1}"]] = ("ffn", 3)

        def f_free(eng, n):
            if n in f_bank:
                got(eng, f_bank[n])
            else:
                eng.wait_ge(S("f_used"), sum(r not in f_bank for r in range(n + 1)))

        item_done = {}

        block = ctx.enter_context(nc.Block())

        @block.tensor
        def _(pe):
            mm = nc.tensor.matmul
            st = [0]

            def item(name):
                n = st[0]
                assert NAMES[n] == name, (NAMES[n], name)
                st[0] += 1
                pe.wait_ge(full[slot_of(n)], need[n])
                return at(slot_of(n) * SLOT, SLOT)

            def transpose(o, i, rows=P):
                return nc.tensor.transpose(o, i, ident[0:rows, 0:rows])

            pe.wait_ge(S("ident"), 1)
            pe.wait_ge(S("ld_gains"), 16 * 8)
            p = unit(pe, "gT", 4)
            ready(transpose(p[:, 0:G_ROWS], grow, G_ROWS), "gT")
            for m in range(TM):
                pe.wait_ge(S(f"ld_x{m}"), 16)
            for q in range(4):
                p = unit(pe, ("xT0", q), q)
                for k in (2 * q, 2 * q + 1):
                    for m in range(TM):
                        last = transpose(p[:, (k % 2) * T + m * P:(k % 2) * T + (m + 1) * P], XS[:, m, k * P:(k + 1) * P])
                ready(last, ("xT0", q))

            def proj_half(name, src, tag, h, banks):
                s = item(name)
                for m in range(TM):
                    p = unit(pe, (tag, h, m), banks[2 * h + m])
                    for k in range(KT):
                        last = mm(p[:, :], lhsT=src[:, k, m * P:(m + 1) * P], rhs=s[:, k * 512:(k + 1) * 512],
                                  start=(k == 0), stop=(k == KT - 1))
                    ready(last, (tag, h, m))
                item_done[name] = units[(tag, h, TM - 1)]

            def proj_rows(names, src, tag, banks):
                for h, name in enumerate(names):
                    proj_half(name, src, tag, h, banks)

            for q in range(4):
                read_out(pe, ("xT0", q))
            proj_half("win0a", HT, "win0", 0, (0, 1, 2, 3))
            for m in range(TM):
                pe.wait_ge(S(f"ld_mem{m}"), 16)
            for q in range(4):
                p = unit(pe, ("memT", q), 2 + q)
                for k in (2 * q, 2 * q + 1):
                    for m in range(TM):
                        last = transpose(p[:, (k % 2) * T + m * P:(k % 2) * T + (m + 1) * P], MEMR[:, m, k * P:(k + 1) * P])
                ready(last, ("memT", q))

            for b, src, key in ((6, cm, "cm"), (7, pw, "pw")):
                pe.wait_ge(S("s5_" + key), 1)
                p = unit(pe, "q_" + key, b)
                for ri in range(2):
                    for n in range(8):
                        last = transpose(p[:, (ri * 8 + n) * PAIRS:(ri * 8 + n + 1) * PAIRS],
                                         src[:, ri, 7 - n if key == "cm" else n], PAIRS)
                ready(last, "q_" + key)
            proj_half("win0b", HT, "win0", 1, (0, 1, 2, 3))
            pe.wait_ge(S("ld_c"), 64)
            for ri in range(2):
                p = unit(pe, ("cT", ri), 4 + ri)
                for a in range(3):
                    last = transpose(p[:, a * P:(a + 1) * P], cnat[:, ri, a])
                ready(last, ("cT", ri))
            def proj_kv(name, src, tag, banks):
                s = item(name)
                for m in range(TM):
                    p = unit(pe, (tag, m), banks[m])
                    for h in range(2):
                        for k in range(KT):
                            last = mm(p[:, h * 256:(h + 1) * 256], lhsT=src[:, k, m * P:(m + 1) * P],
                                      rhs=s[:, h * 2048 + k * 256:h * 2048 + (k + 1) * 256],
                                      start=(k == 0 and h == 0), stop=(k == KT - 1), skip_group_check=True)
                    ready(last, (tag, m))
                item_done[name] = units[(tag, TM - 1)]

            for q in range(4):
                read_out(pe, ("memT", q))
            proj_kv("memkv0", MT[0], "mkv0", (4, 5))
            pe.wait_ge(S("u5_act"), STEPS // 2)
            pe.wait_ge(S("u5_dve"), STEPS // 2)
            for n in range(3):
                p = unit(pe, ("Ug", n), n)
                for a in range(16):
                    g = n * 16 + a
                    last = nc.tensor.transpose(p[:, a * CHUNKS:(a + 1) * CHUNKS], U5[:, g], ident[CHUNKS:2 * CHUNKS, CHUNKS:2 * CHUNKS])
                ready(last, ("Ug", n))
            proj_kv("memkv1", MT[1], "mkv1", (4, 5))
            pe.wait_ge(S("s5_w"), 12)
            for n in range(12):
                ri, jq = n // 6, n % 6
                p = unit(pe, ("Bm", n), 4 + n % 2)
                for a in range(4):
                    last = transpose(p[:, a * P:(a + 1) * P], Wt[:, ri, jq * 4 + a])
                ready(last, ("Bm", n))
            for n in range(12):
                read_out(pe, ("Bm", n))
            for n in range(3):
                read_out(pe, ("Ug", n))
            vb = [unit(pe, ("V", n), n) for n in range(3)]
            for j in range(PAIRS):
                for ri in range(2):
                    b, c0 = (vb[ri], j * CHUNKS) if j < 16 else (vb[2], (ri * 8 + j - 16) * CHUNKS)
                    for g2 in range(2):
                        last = mm(b[g2 * 64:(g2 + 1) * 64, c0:c0 + CHUNKS], lhsT=Bm[:, ri, j, g2 * 64:(g2 + 1) * 64],
                                  rhs=Ug[:, g2 * PAIRS + j], start=True, stop=True, skip_group_check=True)
                        if j == 15 and g2 == 1:
                            ready(last, ("V", ri))
            ready(last, ("V", 2))
            pe.wait_ge(S("s5_w0"), 4)
            pe.wait_ge(S("s5_ca"), 12)
            for ri in range(2):
                read_out(pe, ("cT", ri))
            for jq in range(6):
                p = unit(pe, ("K", jq), 4 + jq % 2)
                for a in range(4):
                    j = jq * 4 + a
                    for ri in range(2):
                        mm(p[0:32, a * P:a * P + GDIM], lhsT=W0bd[:, ri, j], rhs=cT[:, ri, j],
                           start=(a == 0 and ri == 0), stop=(ri == 1), skip_group_check=True)
                    for ri in range(2):
                        last = mm(p[0:32, a * P + GDIM:(a + 1) * P], lhsT=W0bd[:, ri, j], rhs=CA[:, ri, j, 0:7 * GDIM],
                                  start=False, stop=(ri == 1), skip_group_check=True)
                ready(last, ("K", jq))
            pe.wait_ge(S("mk_rows"), 1)
            for l in (1, 0):
                for m in range(TM):
                    p = unit(pe, ("mkT", l, m), 4 + m)
                    for h in range(4):
                        last = transpose(p[0:HD, h * P:(h + 1) * P], mkrow(l, m)[:, h * HD:(h + 1) * HD])
                    ready(last, ("mkT", l, m))
            for m in range(TM):
                p = unit(pe, ("q0T", m), 6 + m)
                for h in range(4):
                    last = transpose(p[0:HD, h * P:(h + 1) * P], HS[:, m, MAIN + h * HD:MAIN + (h + 1) * HD])
                ready(last, ("q0T", m))
            def attention(tag, heads, qT, masked, pbuf, pt_sb, banks):
                LB, PB = banks
                ng = len(heads) // 2

                def logits(n):
                    for a in range(2):
                        qh, kt_, _, _, _ = heads[2 * n + a]
                        p = unit(pe, (tag, "L", n, a), LB[2 * (n % 2) + a])
                        for m in range(TM):
                            nk = P * (m + 1) if masked(2 * n + a) else T
                            last = mm(p[:, m * T:m * T + nk], lhsT=qT[:, qh, m * P:(m + 1) * P], rhs=kt_[:, 0:nk],
                                      start=True, stop=True, skip_group_check=True)
                        ready(last, (tag, "L", n, a))

                def flip(n):
                    for a in range(2):
                        pe.wait_ge(S(tag + "_p"), 2 * n + a + 1)
                        p = unit(pe, (tag, "PT", n, a), PB[(2 * n + a) % len(PB)])
                        for kt_ in range(TM):
                            for m in range(TM):
                                if masked(2 * n + a) and kt_ > m:
                                    continue
                                last = transpose(p[:, kt_ * T + m * P:kt_ * T + (m + 1) * P],
                                                 pbuf[:, (n % 2) * 2 + a, m * T + kt_ * P:m * T + (kt_ + 1) * P])
                        ready(last, (tag, "PT", n, a))

                def outs(n):
                    for a in range(2):
                        _, _, v, _, half = heads[2 * n + a]
                        read_out(pe, (tag, "PT", n, a))
                        p = unit(pe, (tag, "O", n, a), PB[(2 * n + a) % len(PB)])
                        o = p[64 * half:64 * half + 64, 0:T]
                        mm(o, lhsT=v[:, 0], rhs=pt_sb[:, (n % 2) * 2 + a, 0:T], start=True, stop=False,
                           skip_group_check=True)
                        m0 = P if masked(2 * n + a) else 0
                        last = mm(o[:, m0:T], lhsT=v[:, 1], rhs=pt_sb[:, (n % 2) * 2 + a, T + m0:2 * T],
                                  start=False, stop=True, skip_group_check=True)
                        ready(last, (tag, "O", n, a))

                return logits, flip, outs, ng

            lg, fl, ou, ng = attention("m0", M0_HEADS, QT0, lambda h: False, PB0, PT0, ((0, 1, 2, 3), (6, 7)))
            for m in range(TM):
                read_out(pe, ("q0T", m))
                read_out(pe, ("mkT", 0, m))
            lg(0)
            lg(1)
            pe.wait_ge(S("tm"), 16 * 16)
            yb = [unit(pe, ("Y", n), n) for n in range(6)]
            for j in range(PAIRS):
                for g2 in range(2):
                    mm(yb[j // 4][g2 * 32:(g2 + 1) * 32, (j % 4) * P:(j % 4 + 1) * P], lhsT=Ug[:, g2 * PAIRS + j],
                       rhs=Tm[:, g2 * PAIRS + j], start=(j % 4 == 0), stop=False, skip_group_check=True)
            pe.wait_ge(S("xbd"), 4)
            for j in range(PAIRS):
                for ri in range(2):
                    last = mm(yb[j // 4][0:64, (j % 4) * P:(j % 4 + 1) * P], lhsT=Xbd[:, ri, j], rhs=CA[:, ri, j],
                              start=False, stop=(ri == 1), skip_group_check=True)
                if j % 4 == 3:
                    ready(last, ("Y", j // 4))
            for n in range(6):
                read_out(pe, ("Y", n))
            for n in range(3):
                p = unit(pe, ("yT", n), 6 + n % 2)
                for k in range(STEPS):
                    last = transpose(p[:, k * 64:(k + 1) * 64], Ysb[:, k, n * P:(n + 1) * P], 64)
                ready(last, ("yT", n))

            for n in range(3):
                read_out(pe, ("yT", n))
            sa = item("glua")
            sb_ = item("glub")
            for n in range(6):
                s, n0, wn = (sa, n * P, 512) if n < 4 else (sb_, (n - 4) * P, 256)
                p = unit(pe, ("glu", n), n % 2)
                for k in range(6):
                    last = mm(p[:, 0:T], lhsT=s[:, k * wn + n0:k * wn + n0 + P], rhs=GT6[:, k], start=(k == 0), stop=(k == 5))
                ready(last, ("glu", n))
                if n == 3 or n == 5:
                    item_done["glua" if n == 3 else "glub"] = units[("glu", n)]
            fl(0)
            ou(0)
            fl(1)
            ou(1)

            def proj_out(names, tag, banks):
                for h, name in enumerate(names):
                    s = item(name)
                    for m in range(TM):
                        p = unit(pe, (tag, h, m), banks[2 * h + m])
                        for k in range(KT):
                            last = mm(p[:, :], lhsT=CT[:, k, m * P:(m + 1) * P], rhs=s[:, k * 512:(k + 1) * 512],
                                      start=(k == 0), stop=(k == KT - 1))
                        ready(last, (tag, h, m))
                    item_done[name] = units[(tag, h, TM - 1)]

            pe.wait_ge(S("ct0"), 6)
            for n in range(2):
                for a in range(2):
                    read_out(pe, ("m0", "O", n, a))
            proj_out(("wout0a", "wout0b"), "wout0", (0, 1, 2, 3))

            def rows_to_cols(tag, src=None, parts=()):
                if src is None:
                    src = HS
                    pe.wait_ge(S("rows_" + tag), TM)
                for key in parts:
                    read_out(pe, key)
                for q in range(4):
                    p = unit(pe, ("T" + tag, q), q)
                    for k in (2 * q, 2 * q + 1):
                        for m in range(TM):
                            last = transpose(p[:, (k % 2) * T + m * P:(k % 2) * T + (m + 1) * P],
                                             src[:, m, k * P:(k + 1) * P])
                    ready(last, ("T" + tag, q))

            rows_to_cols("f0")
            for q in range(4):
                read_out(pe, ("Tf0", q))
            def three(p, xs, ws, start, stop, **kw):
                for q, (a, b) in enumerate(((0, 0), (1, 0), (0, 1))):
                    last = mm(p, lhsT=xs[a], rhs=ws[b], start=start and q == 0, stop=stop and q == 2, **kw)
                return last

            st[0] += len(f_last)
            for n, (kind, c, j) in enumerate(fparts):
                nf = FCH[c] // P
                if kind == "g" and j == 0:
                    hp = [unit(pe, ("h", c, f), f) for f in range(nf)]
                if kind == "d" and j == 0:
                    pe.wait_ge(S("hid_lo"), c + 1)
                    if c == 0:
                        acc = [unit(pe, ("ffn", b), 4 + b) for b in range(4)]
                pe.wait_ge(S("f_lo"), n + 1)
                hl = FPART[:, n % NFP, 0], FPART[:, n % NFP, 1]
                if kind == "d":
                    for m in range(TM):
                        for b in range(2):
                            end = c == len(FCH) - 1 and j == nf - 1
                            last = three(acc[2 * b + m][:, :], [HIDHL[:, c % 2, x, j, m * P:(m + 1) * P] for x in range(2)],
                                         [w_[:, b * 512:(b + 1) * 512] for w_ in hl], c == 0 and j == 0, end)
                            if end:
                                ready(last, ("ffn", 2 * b + m))
                else:
                    h, kpp = "gu".index(kind), PART // FCH[c]
                    for kk_ in range(kpp):
                        k = j * kpp + kk_
                        for f in range(nf):
                            o = kk_ * FCH[c] + f * P
                            last = three(hp[f][:, h * T:(h + 1) * T], [w_[:, o:o + P] for w_ in hl],
                                         [HTHL[:, x, k] for x in range(2)], h == 0 and k == 0, k == KT - 1,
                                         skip_group_check=True)
                            if h == 1 and k == KT - 1:
                                ready(last, ("h", c, f))
                if n not in f_bank:
                    last.then_inc(S("f_used"), 1)
            rows_to_cols("kv", XS, [("ffn", b) for b in range(4)])
            for q in range(4):
                read_out(pe, ("Tkv", q))
            proj_kv("kv", CT, "kv", (4, 5))
            proj_rows(("win1a", "win1b"), HT, "win1", (0, 1, 2, 3))
            pe.wait_ge(S("kv_rows"), 1)
            for m in range(TM):
                p = unit(pe, ("kvT", m), 4 + m)
                for h in range(4):
                    last = transpose(p[0:HD, h * P:(h + 1) * P], KVR[:, m, h * HD:(h + 1) * HD])
                ready(last, ("kvT", m))
            for h in range(2):
                for m in range(TM):
                    read_out(pe, ("win1", h, m))
            for n in range(8):
                m, hq = n % 2, n // 2
                p = unit(pe, ("q1T", n), 4 + n % 4)
                for a in range(4):
                    h = hq * 4 + a
                    last = transpose(p[0:HD, a * P:(a + 1) * P], HS[:, m, h * HD:(h + 1) * HD])
                ready(last, ("q1T", n))
            for m in range(TM):
                read_out(pe, ("kvT", m))
                read_out(pe, ("mkT", 1, m))
            for n in range(8):
                read_out(pe, ("q1T", n))
            lg, fl, ou, ng = attention("a1", A1_HEADS, QT1, lambda h: h < 12, PB1, PT1, ((0, 1, 2, 3), (6, 7, 4, 5)))
            lg(0)
            lg(1)
            for n in range(ng):
                fl(n)
                if n + 2 < ng:
                    lg(n + 2)
                ou(n)
            for n in range(ng):
                for a in range(2):
                    read_out(pe, ("a1", "O", n, a))
            proj_out(("wout1a", "wout1b"), "wout1", (0, 1, 2, 3))
            rows_to_cols("f1", XS, [("wout1", h, m) for h in range(2) for m in range(TM)])
            for q in range(4):
                read_out(pe, ("Tf1", q))
            pe.wait_ge(S("ld_router"), 16)
            p = unit(pe, "router", 4)
            for m in range(TM):
                for k in range(KT):
                    last = mm(p[:, m * NE:(m + 1) * NE], lhsT=HT[:, k, m * P:(m + 1) * P], rhs=ROUT[:, k],
                              start=(k == 0), stop=(k == KT - 1), skip_group_check=True)
            ready(last, "router")
            pe.wait_ge(S("sel"), 1)
            pe.wait_ge(S("tri"), 3)
            p = unit(pe, "place", 5)
            for col, terms in ((0, ((TRI, 0),)), (1, ((ONES, 0), (TRI, 1))), (2, ((ONES, 0), (ONES, 1)))):
                for q, (mat, m) in enumerate(terms):
                    last = mm(p[:, col * NE:(col + 1) * NE], lhsT=mat, rhs=SEL[:, m],
                              start=(q == 0), stop=(q == len(terms) - 1), skip_group_check=True)
            ready(last, "place")

            y_base = [0, 0]

            def gather(turn, key):
                for b in range(2):
                    p = unit(pe, (key, "xg", b), 7 - b, turn)
                    for kk_ in range(4):
                        k = 4 * b + kk_
                        for m in range(TM):
                            last = mm(p[:, kk_ * CAP:(kk_ + 1) * CAP], lhsT=HS[:, m, k * P:(k + 1) * P],
                                      rhs=PICK[:, m], start=(kk_ == 0 and m == 0), stop=(m == TM - 1),
                                      skip_group_check=True)
                    ready(last, (key, "xg", b))

            def scatter(turn, key, bt, n, m):
                if n == 0 and m == 0:
                    for b in range(2):
                        pe.wait_ge(bank_free[4 + b], uses[4 + b] if bt is None else bt.value(y_base[b], 1))
                p = unit(pe, (key, "sc", n, m), 7, bt)
                ready(mm(p[:, :], lhsT=GATE[0:CAP, m * P:(m + 1) * P], rhs=YR[0:CAP, n * 512:(n + 1) * 512],
                         start=True, stop=True), (key, "sc", n, m))

            def expert(turn, key):
                def part(n):
                    q, j = n // 4, n % 4
                    if j < 3:
                        pe.wait_ge(S("lo_dve"), turn.count("lo_dve", 3 * q + j + 1))
                    else:
                        pe.wait_ge(S("lo_pool"), turn.count("lo_pool", q + 1))
                    return PART_HL[:, n % NPART, 0], PART_HL[:, n % NPART, 1]

                def flip(c):
                    read_out(pe, (key, "gu", c, 1), turn)
                    p = unit(pe, (key, "aT", c), 6, turn)
                    for f in range(4):
                        last = transpose(p[:, f * CAP:(f + 1) * CAP], HID[0:CAP, f * P:(f + 1) * P], CAP)
                    ready(last, (key, "aT", c))

                for b in range(2):
                    pe.wait_ge(bank_free[6 + b], turn.value(uses[6 + b], PER[6 + b]))
                for n in range(NPT):
                    (kind, c), j = items[n // 4], n % 4
                    if kind == "d":
                        if j == 0:
                            read_out(pe, (key, "aT", c), turn)
                            if c == 0:
                                acc = [unit(pe, (key, "y", b), 4 + b, turn) for b in range(2)]
                        hl = part(n)
                        for b in range(2):
                            last = three(acc[b][0:CAP, :], (AT[:, 0, j], AT[:, 1, j]),
                                         [w_[:, b * 512:(b + 1) * 512] for w_ in hl],
                                         c == 0 and j == 0, c == NC_E - 1 and j == 3)
                            if c == NC_E - 1 and j == 3:
                                ready(last, (key, "y", b))
                    else:
                        if j == 0:
                            p = unit(pe, (key, "gu", c, "gu".index(kind)), 2 * (c % 2) + "gu".index(kind), turn)
                        hl = part(n)
                        for a in range(2):
                            k = 2 * j + a
                            last = three(p[0:CAP, :], (XG[:, 0, k], XG[:, 1, k]),
                                         [w_[:, a * 512:(a + 1) * 512] for w_ in hl], k == 0, k == KT - 1)
                        if j == 3:
                            ready(last, (key, "gu", c, "gu".index(kind)))
                    if n not in ends_bank:
                        last.then_inc(S("part_used"), 1)
                    if n in SC_AT:
                        scatter(turn, key, turn, *SC_AT[n])
                    if n in FLIP_AT:
                        flip(FLIP_AT[n])
                    if n == GT_AT:
                        pe.wait_ge(S("pgate"), turn.count("pgate", 1))
                        p2 = unit(pe, (key, "gt"), 7, turn)
                        for m in range(TM):
                            last = transpose(p2[0:CAP, m * P:(m + 1) * P], PG[:, m])
                        ready(last, (key, "gt"))
                    if n == XG_AT:
                        pe.wait_ge(S("pick"), turn.count("pick", 1))
                        gather(turn, key)

            pe.wait_ge(S("pick"), 1)
            pe.wait_ge(S("rows_f1"), TM)
            gather(None, "first")

            def passes(key, first, end):
                base = list(uses)
                y_base[:] = uses[4:6]
                with pe.Fori(first, end) as i:
                    expert(Turn(i, first), key)
                for b in range(8):
                    assert uses[b] - base[b] == PER[b], (b, uses[b] - base[b])
                    uses[b] = base[b] + PER[b] * (end - first)
                for n, m in SC_AT.values():
                    scatter(Turn(end, first), (key, "end"), None, n, m)

            passes("main", 0, NE)
            pe.wait_ge(S("flag"), 1)
            over = pe.value_load(flag[0:1, 0:1], min_val=0, max_val=1)
            with pe.If(over > 0):
                pe.wait_ge(S("gate_zero"), 1)
                passes("over", NE, PASSES * NE)

        @block.sync
        def _(sp):
            def used(n):
                if NAMES[n] in f_last:
                    f_free(sp, f_last[NAMES[n]])
                else:
                    b, use = item_done[NAMES[n]]
                    sp.wait_ge(bank_full[b], use + 1)

            def e_used(turn, q, key):
                part_free(sp, 4 * q + 3, turn, key)

            def load_static(n):
                for dst, src in stream[n][1]:
                    sp.dma_start(dst(at(slot_of(n) * SLOT, SLOT)), src).then_inc(full[slot_of(n)], 16)

            for m in range(TM):
                sp.dma_start(XS[:, m], w["x"][0, m * P:(m + 1) * P, :]).then_inc(S(f"ld_x{m}"), 16)
            sp.wait_ge(S("ld_gains"), 16 * 8)
            def load(dst, src, sem):
                sp.dma_start(dst, src).then_inc(S(sem), 16)

            for n in range(NA):
                s = slot_of(n)
                prev = [q for q in range(n) if slot_of(q) == s]
                if prev:
                    used(prev[-1])
                else:
                    if n >= 6:
                        got(sp, ("yT", 2))
                load_static(n)
                if n == 0:
                    for ri, name in enumerate(("l0_s5_b_re", "l0_s5_b_im")):
                        for g2 in range(2):
                            load(braw[g2 * 64:(g2 + 1) * 64, ri], w[name][g2 * PAIRS:(g2 + 1) * PAIRS].rearrange("j p i -> p j i"), "ld_b")
                if n == 1:
                    for m in range(TM):
                        sp.dma_start(MEMR[:, m], w["mem"][0, m * P:(m + 1) * P, :]).then_inc(S(f"ld_mem{m}"), 16)
                    for ri, name in enumerate(("l0_s5_c_re", "l0_s5_c_im")):
                        for g2 in range(2):
                            load(cnat[:, ri, :, g2 * 64:(g2 + 1) * 64],
                                 w[name][g2 * PAIRS:(g2 + 1) * PAIRS].rearrange("(a jj) o p -> (jj o) a p", a=3), "ld_c")
                    for g2 in range(2):
                        load(Dbc[g2 * GDIM:(g2 + 1) * GDIM], w["l0_s5_d"][g2 * PAIRS * GDIM:(g2 + 1) * PAIRS * GDIM]
                             .rearrange("(a j o) -> a j o", a=1, o=GDIM).to_broadcast([GDIM, PAIRS, GDIM]), "ld_d")
                    for n, name in enumerate(("l0_mem_q_gain", "l0_mem_k_gain", "l1_mem_q_gain", "l1_mem_k_gain", "l1_moba_q_gain")):
                        load(hg[:, n:n + 1], w[name].rearrange("(p a) -> p a", a=1), "ld_hg")
                    load(hgk, w["kv_k_gain"].rearrange("(p a) -> p a", a=1), "ld_hg")
                    load(ROUT, w["l1_moe_router"].rearrange("(k p) e -> p k e", p=P), "ld_router")
                if NAMES[n] == "memkv1":
                    for h in range(2):
                        for m in range(TM):
                            read_out(sp, ("win0", h, m))
                    for s in range(STEPS):
                        for m in range(TM):
                            sp.dma_start(U4[m * 16:(m + 1) * 16, s], HS[s:P:STEPS, m, 0:MAIN]).then_inc(S(f"u_step{s}"), 16)
                if NAMES[n] == "glub":
                    sp.wait_ge(S("kst_d"), 1)
                    sp.wait_ge(S("tm_zero"), 1)
                    Tv = Tm.rearrange("p (g j) c -> p g j c", g=2)
                    for s in range(STEPS):
                        for g2 in range(2):
                            sp.dma_start(Tv[s * GDIM:(s + 1) * GDIM, g2, :, s * GDIM:P],
                                          Kst[g2 * GDIM:(g2 + 1) * GDIM, :, 0:P - s * GDIM]).then_inc(S("tm"), 16)

            def load_expert(e, q):
                kind, c = items[q]
                slot = at(e_slot(q) * SLOT, SLOT)
                if kind == "d":
                    src = w["l1_moe_w_down"][bass.ds(e, 1), c * 512:(c + 1) * 512, :].rearrange("e (k p) n -> p (e k) n", p=P)
                    sp.dma_start(slot.rearrange("p (k n) -> p k n", n=D), src).then_inc(full[e_slot(q)], 16)
                else:
                    src = w["l1_moe_w_gate" if kind == "g" else "l1_moe_w_up"][bass.ds(e, 1), :, c * 512:(c + 1) * 512] \
                        .rearrange("e (k p) n -> p (e k) n", p=P)
                    sp.dma_start(slot.rearrange("p (k n) -> p k n", n=512), src).then_inc(full[e_slot(q)], 16)

            EARLY = 2
            for q in range(NSLOT):
                used(max(n for n in range(NA) if slot_of(n) == e_slot(q)))
                load_expert(0, q)

            def rest(turn, i, key):
                for q in range(NSLOT, NI):
                    e_used(turn, q - NSLOT, key)
                    load_expert(i % NE, q)

            def first_items(turn, i, lo, hi, key):
                for q in range(lo, hi):
                    e_used(turn, NI - NSLOT + q, key)
                    load_expert((i + 1) % NE, q)

            def passes(key, first, end):
                with sp.Fori(first, end - 1) as i:
                    rest(Turn(i, first), i, key)
                    first_items(Turn(i, first), i, 0, NSLOT, key)
                rest(Turn(end - 1, first), end - 1, key)
                first_items(Turn(end - 1, first), end - 1, 0, EARLY, key)

            passes("main", 0, NE)
            sp.wait_ge(S("flag"), 1)
            over = sp.value_load(flag[0:1, 0:1], min_val=0, max_val=1)
            with sp.If(over > 0):
                first_items(Turn(NE - 1, 0), NE - 1, EARLY, NSLOT, "main")
                passes("over", NE, PASSES * NE)
            sp.wait_ge(S("x_final"), 1)
            sp.dma_start(out[0].rearrange("(m p) n -> p m n", p=P), XS).then_inc(S("stored"), 16)
            sp.wait_ge(S("stored"), 16)

        @block.gpsimd
        def _(pool):
            g = nc.gpsimd
            n_chain = [0]

            def link(ins):
                n_chain[0] += 1
                ins.then_inc(S("pool_chain"), 1)
                pool.wait_ge(S("pool_chain"), n_chain[0])

            g.iota(iota, pattern=[[1, CAP]], base=0, channel_multiplier=0, allow_small_or_imprecise_dtypes=True).then_inc(S("iota"), 1)
            link(g.memset(ident, 0.0))
            link(g.affine_select(out=ident, in_=ident, compare_op=ALU.not_equal, fill=1.0, base=0,
                                 pattern=[[-1, P]], channel_multiplier=1))
            g.memset(mh, -0.5).then_inc(S("ident"), 1)
            pool.wait_ge(S("ident"), 1)

            def root(tag, n, src, dst, width):
                pool.wait_ge(S("ss_" + tag), n)
                link(g.tensor_scalar(src, src, 1.0 / width, EPS, ALU.mult, ALU.add))
                g.tensor_tensor(dst, src, mh[:, 0:src.shape[-1]], ALU.pow).then_inc(S("rs_" + tag), 1)

            root("x0", 2, ss[:, 2:4], rs[:, 2:4], D)
            root("mem", 2, ss[:, 0:2], rs[:, 0:2], D)
            pool.wait_ge(S("ld_d"), 32)
            link(g.tensor_tensor(mask16, ident[0:32, 0:GDIM], ident[0:32, GDIM:32], ALU.add))
            g.tensor_tensor(MD, Dbc, mask16.unsqueeze(1).to_broadcast([32, PAIRS, GDIM]), ALU.mult).then_inc(S("skip"), 1)
            link(g.memset(W0bd, 0.0))

            def complex_sums(dst, tag, n0, ops):
                for n in range(PAIRS // 2):
                    pool.wait_ge(S("prods"), 4 * (n0 + n + 1))
                    b = (n0 + n) % 2
                    for ri in range(2):
                        last = g.tensor_tensor(dst[:, ri, 2 * n:2 * n + 2], prod[:, b, 2 * ri].rearrange("p (j c) -> p j c", j=2),
                                               prod[:, b, 2 * ri + 1].rearrange("p (j c) -> p j c", j=2), ops[ri])
                        if ri:
                            last.then_inc(S("s5_" + tag), 1)

            complex_sums(Wt, "w", 0, (ALU.subtract, ALU.add))
            pool.wait_ge(S("s5_w"), 12)
            for ri in range(2):
                for g2 in range(2):
                    g.tensor_copy(W0bd[g2 * 64:(g2 + 1) * 64, ri, :, g2 * GDIM:(g2 + 1) * GDIM],
                                  Wt[g2 * 64:(g2 + 1) * 64, ri, :, 7 * GDIM:8 * GDIM]).then_inc(S("s5_w0"), 1)
                    pool.wait_ge(S("s5_w0"), 2 * ri + g2 + 1)
            root("q0", 1, hss[:, 16:24], hrs[:, 16:24], HD)
            for n in range(3):
                read_out(pool, ("Ug", n))
            complex_sums(CA, "ca", 12, (ALU.add, ALU.subtract))
            root("mk", 1, hss[:, 0:16], hrs[:, 0:16], HD)
            for m in range(TM):
                got(pool, ("mkv1", m))
            g.memset(Tm, 0.0).then_inc(S("tm_zero"), 1)
            got(pool, ("Bm", 11))
            g.memset(Xbd, 0.0).then_inc(S("xbd_zero"), 1)
            for jq in range(6):
                read_out(pool, ("K", jq))
            g.tensor_tensor(Kst[:, :, 0:GDIM], Kst[:, :, 0:GDIM], MD, ALU.add).then_inc(S("kst_d"), 1)
            root("f0", 2, ss[:, 0:2], rs[:, 0:2], D)
            root("kv", 2, ss[:, 2:4], rs[:, 2:4], D)
            got(pool, ("ffn", 3))
            link(g.memset(TRI, 1.0))
            g.memset(ONES, 1.0).then_inc(S("tri"), 1)
            link(g.memset(MSK, 0.0))
            g.affine_select(out=TRI, in_=TRI, compare_op=ALU.is_gt, fill=0.0, base=0,
                            pattern=[[1, P]], channel_multiplier=-1).then_inc(S("tri"), 1)
            g.affine_select(out=MSK, in_=MSK, compare_op=ALU.is_ge, fill=NEG, base=0,
                            pattern=[[-1, P]], channel_multiplier=1).then_inc(S("tri"), 1)
            root("kvh", 1, hss[:, 0:8], hrs[:, 0:8], HD)
            root("q1", 1, hss[:, 8:40], hrs[:, 8:40], HD)
            root("f1", 2, ss[:, 0:2], rs[:, 0:2], D)

            def lo(turn, q):
                n = 4 * q + 3
                pool.wait_ge(S("hi"), turn.count("hi", n + 1))
                b = n % NPART
                g.tensor_tensor(PART_HL[:, b, 1], at(e_slot(q) * SLOT + 3 * PART, PART), PART_HL[:, b, 0].bitcast(fp),
                                ALU.subtract).then_inc(S("lo_pool"), 1)

            lo(Turn(0, 0), 0)

            def passes(first, end):
                with pool.Fori(first, end) as i:
                    for q in range(1, NI):
                        lo(Turn(i, first), q)
                    lo(Turn(i + 1, first), 0)

            passes(0, NE)
            pool.wait_ge(S("flag"), 1)
            over = pool.value_load(flag[0:1, 0:1], min_val=0, max_val=1)
            with pool.If(over > 0):
                passes(NE, PASSES * NE)

        @block.scalar
        def _(act):
            ac = nc.scalar.activation

            def load(dst, src, sem):
                act.dma_start(dst, src).then_inc(S(sem), 16)

            load(lam_r.rearrange("j (g p) -> j g p", g=2), w["l0_s5_lam_re"].rearrange("(g j) p -> j g p", g=2), "ld_lam")
            load(lam_i.rearrange("j (g p) -> j g p", g=2), w["l0_s5_lam_im"].rearrange("(g j) p -> j g p", g=2), "ld_lam")
            load(ldt, w["l0_s5_log_dt"].rearrange("(g j) -> j g", g=2), "ld_lam")
            for r, name in ((G_MIX0, "l0_mix_norm"), (G_MEM0, "l0_mem_norm"), (G_FFN0, "l0_ffn_norm"), (G_KV, "kv_norm"),
                            (G_MIX1, "l1_mix_norm"), (G_MEM1, "l1_mem_norm"), (G_FFN1, "l1_ffn_norm")):
                load(grow[r:r + 8, :], w[name].rearrange("(r p) -> r p", p=P), "ld_gains")
            load(grow[G_BGLU:G_BGLU + 6, :], w["l0_s5_b_glu"].rearrange("(r p) -> r p", p=P), "ld_gains")
            def square(src, tag, col, ld=None):
                for m in range(TM):
                    if ld:
                        act.wait_ge(S(f"{ld}{m}"), 16)
                    ac((at(12288, TM, D) if src is MEMR else HS)[:, m], src[:, m], ACT.Square,
                       accum_out=ss[:, col + m:col + m + 1]).then_inc(S("ss_" + tag), 1)

            def scale_rows(src, tag, col, done):
                act.wait_ge(S("rs_" + tag), 1)
                for m in range(TM):
                    ac(HS[:, m], src[:, m], ACT.Copy, scale=rs[:, col + m:col + m + 1]).then_inc(S(done), 1)

            square(XS, "x0", 2, "ld_x")
            act.wait_ge(S("ld_lam"), 48)
            ac(edt, ldt, ACT.Exp).then_inc(S("dt"), 1)
            act.wait_ge(S("zr"), 1)
            ac(er, zr, ACT.Exp).then_inc(S("er"), 1)
            act.wait_ge(S("ang"), 1)
            ac(sn, rr, ACT.Sin).then_inc(S("sin"), 1)
            act.wait_ge(S("ang"), 2)
            ac(cs, kk, ACT.Sin).then_inc(S("sin"), 1)
            p = got(act, "gT")
            free(ac(gT, p[:, 0:G_ROWS], ACT.Copy), "gT")
            read_out(act, "gT")

            def gains_out(key, q, outs):
                p = got(act, (key, q))
                for dst, row in outs:
                    for a in range(2):
                        k = 2 * q + a
                        last = ac(dst[:, k], p[:, a * T:(a + 1) * T], ACT.Copy, scale=gT[:, row + k:row + k + 1])
                free(last, (key, q))

            for q in range(4):
                gains_out("xT0", q, [(HT, G_MIX0)])
            square(MEMR, "mem", 0, "ld_mem")

            def kv_out(tag, col, rows, vals):
                for m in range(TM):
                    p = got(act, (tag, m))
                    ac(rows(m), p[:, 0:256], ACT.Copy, scale=rs[:, col + m:col + m + 1])
                    free(ac(vals(m), p[:, 256:512], ACT.Copy, scale=rs[:, col + m:col + m + 1]), (tag, m))

            act.wait_ge(S("rs_mem"), 1)
            act.wait_ge(S("rs_x0"), 1)

            def win0_out(h):
                for m in range(TM):
                    p = got(act, ("win0", h, m))
                    free(ac(HS[:, m, h * 512:(h + 1) * 512], p[:, :], ACT.Copy, scale=rs[:, 2 + m:3 + m]), ("win0", h, m))

            win0_out(0)
            for q in range(4):
                gains_out("memT", q, [(MT[0], G_MEM0), (MT[1], G_MEM1)])
            win0_out(1)
            for ri in range(2):
                p = got(act, ("cT", ri))
                free(ac(cT[:, ri], p[:, 0:PAIRS * GDIM], ACT.Copy, scale=1.0 if ri == 0 else -1.0), ("cT", ri))
            for s in range(0, STEPS, 2):
                act.wait_ge(S(f"u_step{s}"), 32)
                ac(U5[:, :, s * GDIM:(s + 1) * GDIM], U4[:, s].rearrange("p (g i) -> p g i", i=GDIM), ACT.Copy).then_inc(S("u5_act"), 1)
            kv_out("mkv0", 0, lambda m: mkrow(0, m), lambda m: vM[0][:, m])
            for n in range(3):
                p = got(act, ("Ug", n))
                free(ac(Ug[:, n * 16:(n + 1) * 16], p[:, :].rearrange("p (a c) -> p a c", a=16), ACT.Copy), ("Ug", n))
            kv_out("mkv1", 0, lambda m: mkrow(1, m), lambda m: vM[1][:, m])
            for n in range(12):
                p = got(act, ("Bm", n))
                ri, jq = n // 6, n % 6
                free(ac(Bm[:, ri, jq * 4:jq * 4 + 4], p[:, :].rearrange("p (a c) -> p a c", a=4), ACT.Copy), ("Bm", n))
            for n in range(3):
                p = got(act, ("V", n))
                dst, src = (VX[:, n, 0:16], p[:, :].rearrange("p (j c) -> p j c", c=CHUNKS)) if n < 2 else \
                    (VX[:, :, 16:24], p[:, :].rearrange("p (r j c) -> p r j c", r=2, c=CHUNKS))
                free(ac(dst, src, ACT.Copy), ("V", n))
            for jq in range(6):
                p = got(act, ("K", jq))
                free(ac(Kst[:, jq * 4:jq * 4 + 4], p[0:32, :].rearrange("p (a c) -> p a c", a=4), ACT.Copy), ("K", jq))
            act.wait_ge(S("gp"), 3)
            for l in (1, 0):
                for m in range(TM):
                    p = got(act, ("mkT", l, m))
                    free(ac(kT[l][:, :, m * P:(m + 1) * P], p[0:HD, :].rearrange("p (h t) -> p h t", h=4), ACT.Copy,
                            scale=gp[:, l:l + 1]), ("mkT", l, m))
            for m in range(TM):
                p = got(act, ("q0T", m))
                free(ac(QT0[:, :, m * P:(m + 1) * P], p[0:HD, :].rearrange("p (h t) -> p h t", h=4), ACT.Copy), ("q0T", m))
            act.wait_ge(S("scan"), 1)
            act.wait_ge(S("xbd_zero"), 1)
            for g2 in range(2):
                ac(Xbd[g2 * 64:(g2 + 1) * 64, 1, :, g2 * 32 + 1:g2 * 32 + 32], VX[g2 * 64:(g2 + 1) * 64, 1, :, 0:31],
                   ACT.Copy).then_inc(S("xbd"), 1)
            def softmax(tag, n, pbuf, masked, heads):
                for a in range(2):
                    act.wait_ge(S(tag + "_max"), 2 * n + a + 1)
                    p = PS_OF(tag, n, a)
                    for m in range(TM):
                        nk = P * (m + 1) if masked(2 * n + a) else T
                        c = 2 * a + m
                        last = ac(pbuf[:, (n % 2) * 2 + a, m * T:m * T + nk], p[:, m * T:m * T + nk], ACT.Exp,
                                  bias=snm[:, n % 2, c:c + 1], scale=q_scale(tag, heads[2 * n + a][0])[:, m:m + 1], accum_out=ssum[:, n % 2, c:c + 1])
                    free(last, (tag, "L", n, a))

            def PS_OF(tag, n, a):
                return PS[units[(tag, "L", n, a)][0]]

            def pt_out(tag, n, pt, masked):
                for a in range(2):
                    p = got(act, (tag, "PT", n, a))
                    d = pt[:, (n % 2) * 2 + a]
                    if masked(2 * n + a):
                        ac(d[:, 0:T], p[:, 0:T], ACT.Copy)
                        last = ac(d[:, T + P:2 * T], p[:, T + P:2 * T], ACT.Copy)
                    else:
                        last = ac(d, p[:, :], ACT.Copy)
                    free(last, (tag, "PT", n, a))

            for n in range(2):
                softmax("m0", n, PB0, lambda h: False, M0_HEADS)
            for n in range(1, 6, 2):
                p = got(act, ("Y", n))
                free(ac(Ysb[:, :, n * 64:(n + 1) * 64].rearrange("p k (a o) -> p k a o", a=4),
                        p[0:64, :].rearrange("p (a k o) -> p k a o", a=4, k=STEPS), ACT.Copy), ("Y", n))
            for n in range(3):
                p = got(act, ("yT", n))
                for g2 in range(2):
                    last = ac(GT6[:, g2 * 3 + n].rearrange("p (c k) -> p c k", k=STEPS),
                              p[:, :].rearrange("p (k g c) -> p g c k", k=STEPS, g=2)[:, g2], ACT.Gelu_apprx_tanh)
                free(last, ("yT", n))

            for n in range(6):
                if n >= 2:
                    act.wait_ge(S("ct0"), n - 1)
                p = got(act, ("glu", n))
                free(ac(SIG[:, n % 2], p[:, 0:T], ACT.Sigmoid, bias=gT[:, G_BGLU + n:G_BGLU + n + 1]), ("glu", n))
            for n in range(2):
                pt_out("m0", n, PT0, lambda h: False)

            def cols_out(tag, outs):
                for q in (1, 3):
                    gains_out("T" + tag, q, outs)

            def norm(tag, col, parts, rows=True):
                for key in parts:
                    read_out(act, key)
                square(XS, tag, col)
                if rows:
                    scale_rows(XS, tag, col, "rows_" + tag)

            def f_hi(n):
                kind, c, j = fparts[n]
                it = NAMES.index(f"{kind}{c}")
                if j == 0:
                    act.wait_ge(full[slot_of(it)], need[it])
                if n >= NFP:
                    f_free(act, n - NFP)
                ac(FPART[:, n % NFP, 0], at(slot_of(it) * SLOT + j * PART, PART), ACT.Copy).then_inc(S("f_hi"), 1)

            act.wait_ge(S("ct0"), 6)
            for n in range(2):
                for a in range(2):
                    got(act, ("m0", "O", n, a))
            for n in range(NFP):
                f_hi(n)
            norm("f0", 0, [("wout0", h, m) for h in range(2) for m in range(TM)])
            for q in range(4):
                p = got(act, ("Tf0", q))
                for a in range(2):
                    k = 2 * q + a
                    last = ac(HTHL[:, 0, k], p[:, a * T:(a + 1) * T], ACT.Copy, scale=gT[:, G_FFN0 + k:G_FFN0 + k + 1])
                last.then_inc(S("ht_hi"), 1)
            for n in range(NFP, len(fparts) + NFP):
                if n < len(fparts):
                    f_hi(n)
                kind, c, j = fparts[n - NFP + 1] if n - NFP + 1 < len(fparts) else ("", 0, 0)
                if n - NFP + 1 in f_bank and kind == "u":
                    for f in range(FCH[c] // P):
                        p = got(act, ("h", c, f))
                        ac(SG0[:, f], p[:, 0:T], ACT.Silu).then_inc(S("sg0"), 1)
                if n - NFP in f_bank and fparts[n - NFP][0] == "u":
                    c = fparts[n - NFP][1]
                    nf = FCH[c] // P
                    for f in range(nf):
                        read_out(act, ("h", c, f))
                    ac(HIDHL[:, c % 2, 0, 0:nf], HID0[:, 0:nf], ACT.Copy).then_inc(S("hid_hi"), 1)
            norm("kv", 2, [("ffn", b) for b in range(4)], rows=False)
            cols_out("kv", [(CT, G_KV), (HT, G_MIX1)])
            act.wait_ge(S("rs_kv"), 1)
            kv_out("kv", 2, lambda m: KVR[:, m], lambda m: VKV[:, m])
            for h in range(2):
                for m in range(TM):
                    p = got(act, ("win1", h, m))
                    free(ac(HS[:, m, h * 512:(h + 1) * 512], p[:, :], ACT.Copy, scale=rs[:, 2 + m:3 + m]), ("win1", h, m))
            for m in range(TM):
                p = got(act, ("kvT", m))
                free(ac(kTkv[:, :, m * P:(m + 1) * P], p[0:HD, :].rearrange("p (h t) -> p h t", h=4), ACT.Copy,
                        scale=gp[:, 2:3]), ("kvT", m))
            for n in range(1, 8, 2):
                p = got(act, ("q1T", n))
                free(ac(QT1[:, (n // 2) * 4:(n // 2) * 4 + 4, (n % 2) * P:(n % 2 + 1) * P],
                        p[0:HD, :].rearrange("p (h t) -> p h t", h=4), ACT.Copy), ("q1T", n))
            ng = len(A1_HEADS) // 2
            for n in range(2):
                softmax("a1", n, PB1, lambda h: h < 12, A1_HEADS)
            for n in range(ng):
                pt_out("a1", n, PT1, lambda h: h < 12)
                if n + 2 < ng:
                    softmax("a1", n + 2, PB1, lambda h: h < 12, A1_HEADS)
            norm("f1", 0, [("wout1", h, m) for h in range(2) for m in range(TM)], rows=False)
            cols_out("f1", [(HT, G_FFN1)])
            scale_rows(XS, "f1", 0, "rows_f1")
            act.wait_ge(S("rt_d"), 1)
            ac(EX, LG, ACT.Exp).then_inc(S("rt_e"), 1)

            def hi(turn, n, q_turn):
                q, j = n // 4, n % 4
                if j == 0:
                    act.wait_ge(full[e_slot(q)], q_turn.weights(e_need(q)))
                ac(PART_HL[:, n % NPART, 0], at(e_slot(q) * SLOT + j * PART, PART), ACT.Copy).then_inc(S("hi"), 1)

            def xg_out(turn, key):
                for b in range(2):
                    p = got(act, (key, "xg", b), turn)
                    for a in range(4):
                        k = 4 * b + a
                        last = ac(XG[:, 0, k], p[:, a * CAP:(a + 1) * CAP], ACT.Copy, scale=gT[:, G_FFN1 + k:G_FFN1 + k + 1])
                    last.then_inc(S("hi_small"), 1)

            def expert(turn, key):
                later = Turn(turn.i + 1, turn.start)
                for s in range(NPT):
                    n = s + NPART
                    part_free(act, s, turn, key)
                    hi(turn, n % NPT, turn if n < NPT else later)
                    k = n - LEAD
                    if k < NPT and k % 4 == 3 and items[k // 4][0] == "g":
                        c = items[k // 4][1]
                        p = got(act, (key, "gu", c, 0), turn)
                        free(ac(SG1[0:CAP], p[0:CAP, :], ACT.Silu), (key, "gu", c, 0))
                    if k in FLIP_AT:
                        p = got(act, (key, "aT", FLIP_AT[k]), turn)
                        ac(AT[:, 0].rearrange("p f t -> p (f t)"), p[:, 0:4 * CAP], ACT.Copy).then_inc(S("hi_small"), 1)
                    if k == GT_AT:
                        p = got(act, (key, "gt"), turn)
                        free(ac(GATE[0:CAP], p[0:CAP, 0:T], ACT.Copy), (key, "gt"))
                    if k == XG_AT:
                        xg_out(turn, key)
                    if k == NPT - 1:
                        p = got(act, (key, "y", 1), turn)
                        free(ac(YR[0:CAP, 512:1024], p[0:CAP, :], ACT.Copy), (key, "y", 1))

            got(act, "place")
            for n in range(NPART):
                hi(None, n, Turn(0, 0))
            xg_out(None, "first")

            def passes(key, first, end):
                with act.Fori(first, end) as i:
                    expert(Turn(i, first), key)

            passes("main", 0, NE)
            act.wait_ge(S("flag"), 1)
            over = act.value_load(flag[0:1, 0:1], min_val=0, max_val=1)
            with act.If(over > 0):
                passes("over", NE, PASSES * NE)

        @block.vector
        def _(dve):
            v = nc.vector
            n_chain = [0]

            def link(ins):
                n_chain[0] += 1
                ins.then_inc(S("dve_chain"), 1)
                dve.wait_ge(S("dve_chain"), n_chain[0])
                return ins

            tt, tsc = v.tensor_tensor, v.tensor_scalar

            def bc2(x):
                return x.unsqueeze(2).to_broadcast([PAIRS, 2, NSTATE])

            def v2(x):
                return x.rearrange("p (g s) -> p g s", g=2)

            dve.wait_ge(S("ld_lam"), 48)
            dve.wait_ge(S("dt"), 1)
            tt(v2(zr), v2(lam_r), bc2(edt), ALU.mult).then_inc(S("zr"), 1)
            link(tt(v2(zi), v2(lam_i), bc2(edt), ALU.mult))
            link(tsc(kk, zi, 1.0 / (2 * math.pi), None, ALU.mult))
            link(tsc(kk, kk, 12582912.0, None, ALU.add))
            link(tsc(kk, kk, -12582912.0, None, ALU.add))
            c1 = 6.28125
            c2 = 0.0019350051879882812
            c3 = 2 * math.pi - c1 - c2
            link(v.scalar_tensor_tensor(out=rr, in0=kk, scalar=-c1, in1=zi, op0=ALU.mult, op1=ALU.add))
            link(v.scalar_tensor_tensor(out=rr, in0=kk, scalar=-c2, in1=rr, op0=ALU.mult, op1=ALU.add))
            link(v.scalar_tensor_tensor(out=rr, in0=kk, scalar=-c3, in1=rr, op0=ALU.mult, op1=ALU.add))
            pi = 3.1415925
            link(tsc(rr, rr, -pi, pi, ALU.max, ALU.min))
            tsc(t0, rr, -1.0, None, ALU.mult).then_inc(S("ang"), 1)
            dve.wait_ge(S("ang"), 1)
            link(tt(t0, t0, rr, ALU.max))
            tsc(kk, t0, -1.0, math.pi / 2, ALU.mult, ALU.add).then_inc(S("ang"), 1)
            link(tt(t1, lam_r, lam_r, ALU.mult))
            link(tt(t2, lam_i, lam_i, ALU.mult))
            link(tt(t1, t1, t2, ALU.add))
            link(v.reciprocal(zi, t1))
            dve.wait_ge(S("er"), 1)
            dve.wait_ge(S("sin"), 2)
            link(tt(pw[:, 0, 0], er, cs, ALU.mult))
            link(tt(pw[:, 1, 0], er, sn, ALU.mult))
            link(tsc(t0, pw[:, 0, 0], -1.0, None, ALU.add))
            ai = pw[:, 1, 0]
            link(tt(t1, t0, lam_r, ALU.mult))
            link(tt(t2, ai, lam_i, ALU.mult))
            link(tt(t1, t1, t2, ALU.add))
            link(tt(fr, t1, zi, ALU.mult))
            link(tt(t1, ai, lam_r, ALU.mult))
            link(tt(t2, t0, lam_i, ALU.mult))
            link(tt(t1, t1, t2, ALU.subtract))
            link(tt(fi, t1, zi, ALU.mult))

            def cmul(dr, di, ar, ai_, br, bi, n):
                w0, w1 = (x[:, 0:n * P].rearrange("p (n c) -> p n c", n=n) for x in (u0, u1))
                b_ = lambda x: x.unsqueeze(1).to_broadcast([PAIRS, n, P])
                tt(w0, ar, b_(br), ALU.mult)
                link(tt(w1, ai_, b_(bi), ALU.mult))
                link(tt(dr, w0, w1, ALU.subtract))
                tt(w0, ar, b_(bi), ALU.mult)
                link(tt(w1, ai_, b_(br), ALU.mult))
                return link(tt(di, w0, w1, ALU.add))

            cmul(pw[:, 0, 1:2], pw[:, 1, 1:2], pw[:, 0, 0:1], pw[:, 1, 0:1], pw[:, 0, 0], pw[:, 1, 0], 1)
            cmul(pw[:, 0, 2:4], pw[:, 1, 2:4], pw[:, 0, 0:2], pw[:, 1, 0:2], pw[:, 0, 1], pw[:, 1, 1], 2)
            cmul(pw[:, 0, 4:8], pw[:, 1, 4:8], pw[:, 0, 0:4], pw[:, 1, 0:4], pw[:, 0, 3], pw[:, 1, 3], 4)
            v.tensor_copy(cm[:, 0, 0], fr)
            link(v.tensor_copy(cm[:, 1, 0], fi))
            cmul(cm[:, 0, 1:5], cm[:, 1, 1:5], pw[:, 0, 0:4], pw[:, 1, 0:4], fr, fi, 4)
            cmul(cm[:, 0, 5:8], cm[:, 1, 5:8], pw[:, 0, 4:7], pw[:, 1, 4:7], fr, fi, 3)
            tsc(t0[0:1, 0:1], t0[0:1, 0:1], 1.0, None, ALU.mult).then_inc(S("s5_cm"), 1)
            tsc(t1[0:1, 0:1], t1[0:1, 0:1], 1.0, None, ALU.mult).then_inc(S("s5_pw"), 1)

            def products(bank, key, x, n0, combos, tag):
                p = got(dve, key)
                fac = p[:, 0:16 * PAIRS].rearrange("p (r n j) -> p r j n", r=2, n=8)
                for n in range(PAIRS // 2):
                    t = n0 + n
                    if t >= 2:
                        dve.wait_ge(S("s5_w") if t - 2 < 12 else S("s5_ca"), t - 1 if t - 2 < 12 else t - 13)
                    for q, (fri, xri) in enumerate(combos):
                        last = tt(prod[:, t % 2, q].rearrange("p (j n i) -> p j n i", j=2, n=8),
                                  fac[:, fri, 2 * n:2 * n + 2].unsqueeze(3).to_broadcast([P, 2, 8, GDIM]),
                                  x[:, xri, 2 * n:2 * n + 2].unsqueeze(2).to_broadcast([P, 2, 8, GDIM]), ALU.mult)
                        last.then_inc(S("prods"), 1)
                return p, last

            dve.wait_ge(S("ld_b"), 64)
            p, last = products(6, "q_cm", braw, 0, ((0, 0), (1, 1), (0, 1), (1, 0)), "w")
            def head_norm(rows, nh, tag, c0, sq, done):
                sqv = sq.rearrange("p (h d) -> p h d", d=HD)
                k = 0
                for r, n in rows:
                    last = tt(sqv[:, k:k + n], r, r, ALU.mult)
                    k += n
                link(last)
                v.tensor_reduce(out=hss[:, c0:c0 + nh], in_=sqv[:, 0:nh], axis=AX.X, op=ALU.add).then_inc(S("ss_" + tag), 1)
                if done is None:
                    return
                dve.wait_ge(S("rs_" + tag), 1)
                k = c0
                for r, n in rows:
                    last = tt(r, r, hrs[:, k:k + n].unsqueeze(2).to_broadcast([P, n, HD]), ALU.mult)
                    k += n
                last.then_inc(S(done), 1)

            def heads_of(x):
                return x.rearrange("p (h d) -> p h d", d=HD)

            for s in range(1, STEPS, 2):
                dve.wait_ge(S(f"u_step{s}"), 32)
                v.tensor_copy(U5[:, :, s * GDIM:(s + 1) * GDIM], U4[:, s].rearrange("p (g i) -> p g i", i=GDIM)).then_inc(S("u5_dve"), 1)
            for q in range(4):
                read_out(dve, ("memT", q))
            for h in range(2):
                for m in range(TM):
                    read_out(dve, ("win0", h, m))
            head_norm([(heads_of(HS[:, m, MAIN:D]), 4) for m in range(TM)], 8, "q0", 16, sq0, None)
            for ri in range(2):
                read_out(dve, ("cT", ri))
            read_out(dve, "gT")
            p, last = products(7, "q_pw", cT, 12, ((0, 0), (1, 1), (0, 1), (1, 0)), "ca")
            for o, (a, b) in enumerate(((0, 1), (1, 0))):
                re = p[:, 7 * PAIRS:8 * PAIRS]
                im = p[:, 15 * PAIRS:16 * PAIRS]
                cp = v.tensor_copy(A8[:, o, o], re)
                if o == 0:
                    free(cp, "q_cm")
                last = tsc(A8[:, o, 1 - o], im, -1.0 if o == 0 else 1.0, None, ALU.mult)
            free(last, "q_pw")
            dve.wait_ge(S("ld_hg"), 96)
            for n, (a, b) in enumerate(((hg[:, 0:1], hg[:, 1:2]), (hg[:, 2:3], hg[:, 3:4]), (hg[:, 4:5], hgk))):
                tsc(gp[:, n:n + 1], a, b, SCALE, ALU.mult, ALU.mult).then_inc(S("gp"), 1)

            for m in range(TM):
                read_out(dve, ("mkv1", m))
                read_out(dve, ("mkv0", m))
            dve.wait_ge(S("s5_ca"), 12)
            head_norm([(heads_of(MKR.rearrange("p a b -> p (a b)")), 16)], 16, "mk", 0, sqk, "mk_rows")
            for n in range(3):
                read_out(dve, ("V", n))
            for c in range(1, CHUNKS - 1):
                link(tt(stp, A8, VX[:, :, :, c - 1].unsqueeze(1).to_broadcast([P, 2, 2, PAIRS]), ALU.mult))
                link(tt(stp[:, :, 0], stp[:, :, 0], stp[:, :, 1], ALU.add))
                link(tt(VX[:, :, :, c], VX[:, :, :, c], stp[:, :, 0], ALU.add))
            v.memset(stp[:, 0, 0, 0:1], 0.0).then_inc(S("scan"), 1)
            dve.wait_ge(S("xbd_zero"), 1)
            for g2 in range(2):
                v.tensor_copy(Xbd[g2 * 64:(g2 + 1) * 64, 0, :, g2 * 32 + 1:g2 * 32 + 32],
                              VX[g2 * 64:(g2 + 1) * 64, 0, :, 0:31]).then_inc(S("xbd"), 1)
            def maxima(tag, n, masked, heads):
                for a in range(2):
                    p = got(dve, (tag, "L", n, a))
                    c = 2 * a
                    if masked(2 * n + a):
                        tt(p[:, 0:P], p[:, 0:P], MSK, ALU.add)
                        link(tt(p[:, T + P:2 * T], p[:, T + P:2 * T], MSK, ALU.add))
                        v.tensor_reduce(out=snm[:, n % 2, c:c + 1], in_=p[:, 0:P], axis=AX.X, op=ALU.max, negate=True)
                        last = v.tensor_reduce(out=snm[:, n % 2, c + 1:c + 2], in_=p[:, T:2 * T], axis=AX.X, op=ALU.max,
                                               negate=True)
                    else:
                        last = v.tensor_reduce(out=snm[:, n % 2, c:c + 2], in_=p[:, :].rearrange("p (m k) -> p m k", m=2),
                                               axis=AX.X, op=ALU.max, negate=True)
                    link(last)
                    q = q_scale(tag, heads[2 * n + a][0])
                    tt(snm[:, n % 2, c:c + 2], snm[:, n % 2, c:c + 2], q, ALU.mult).then_inc(S(tag + "_max"), 1)

            def normalise(tag, n, pbuf, masked):
                for a in range(2):
                    read_out(dve, (tag, "L", n, a))
                link(v.reciprocal(srec[:, n % 2], ssum[:, n % 2]))
                for a in range(2):
                    for m in range(TM):
                        nk = P * (m + 1) if masked(2 * n + a) else T
                        x = pbuf[:, (n % 2) * 2 + a, m * T:m * T + nk]
                        last = tsc(x, x, srec[:, n % 2, 2 * a + m:2 * a + m + 1], None, ALU.mult)
                    last.then_inc(S(tag + "_p"), 1)

            def o_out(tag, n, heads):
                for a in range(2):
                    _, _, _, tile, half = heads[2 * n + a]
                    p = got(dve, (tag, "O", n, a))
                    free(v.tensor_copy(CT[64 * half:64 * half + 64, tile], p[64 * half:64 * half + 64, 0:T])
                         , (tag, "O", n, a))

            no = lambda h: False
            dve.wait_ge(S("rs_q0"), 1)
            maxima("m0", 0, no, M0_HEADS)
            maxima("m0", 1, no, M0_HEADS)
            normalise("m0", 0, PB0, no)
            normalise("m0", 1, PB0, no)
            for n in range(0, 6, 2):
                p = got(dve, ("Y", n))
                free(v.tensor_copy(Ysb[:, :, n * 64:(n + 1) * 64].rearrange("p k (a o) -> p k a o", a=4),
                                   p[0:64, :].rearrange("p (a k o) -> p k a o", a=4, k=STEPS)), ("Y", n))

            for n in range(6):
                read_out(dve, ("glu", n))
                tt(CT[:, n], SIG[:, n % 2], GT6[:, n], ALU.mult).then_inc(S("ct0"), 1)
            o_out("m0", 0, M0_HEADS)
            o_out("m0", 1, M0_HEADS)

            def residual(keys):
                for h, m, key in keys:
                    p = got(dve, key)
                    x = XS[:, m, h * 512:(h + 1) * 512]
                    free(tt(x, x, p[:, :], ALU.add), key)

            def cols_out(tag, outs):
                for q in (0, 2):
                    p = got(dve, ("T" + tag, q))
                    for dst, row in outs:
                        for a in range(2):
                            k = 2 * q + a
                            last = tsc(dst[:, k], p[:, a * T:(a + 1) * T], gT[:, row + k:row + k + 1], None, ALU.mult)
                    free(last, ("T" + tag, q))

            def f_lo(n):
                kind, c, j = fparts[n]
                it = NAMES.index(f"{kind}{c}")
                dve.wait_ge(S("f_hi"), n + 1)
                tt(FPART[:, n % NFP, 1], at(slot_of(it) * SLOT + j * PART, PART), FPART[:, n % NFP, 0].bitcast(fp),
                   ALU.subtract).then_inc(S("f_lo"), 1)

            for n in range(NFP):
                f_lo(n)
            residual([(h, m, ("wout0", h, m)) for h in range(2) for m in range(TM)])
            for q in range(4):
                dve.wait_ge(S("ht_hi"), q + 1)
                p = PS[units[("Tf0", q)][0]]
                for a in range(2):
                    k = 2 * q + a
                    last = v.scalar_tensor_tensor(HTHL[:, 1, k], p[:, a * T:(a + 1) * T], gT[:, G_FFN0 + k:G_FFN0 + k + 1],
                                                  HTHL[:, 0, k].bitcast(fp), ALU.mult, ALU.subtract)
                free(last, ("Tf0", q))
            n_sg = 0
            for n in range(NFP, len(fparts) + NFP):
                if n < len(fparts):
                    f_lo(n)
                if n - NFP + 1 in f_bank and n - NFP + 1 < len(fparts) and fparts[n - NFP + 1][0] == "u":
                    c = fparts[n - NFP + 1][1]
                    if c:
                        dve.wait_ge(S("hid_lo"), c)
                    for f in range(FCH[c] // P):
                        n_sg += 1
                        dve.wait_ge(S("sg0"), n_sg)
                        free(tt(HID0[:, f], SG0[:, f], PS[units[("h", c, f)][0]][:, T:2 * T], ALU.mult), ("h", c, f))
                if n - NFP in f_bank and fparts[n - NFP][0] == "u":
                    c = fparts[n - NFP][1]
                    nf = FCH[c] // P
                    dve.wait_ge(S("hid_hi"), c + 1)
                    tt(HIDHL[:, c % 2, 1, 0:nf], HID0[:, 0:nf], HIDHL[:, c % 2, 0, 0:nf].bitcast(fp),
                       ALU.subtract).then_inc(S("hid_lo"), 1)
            residual([(h, m, ("ffn", 2 * h + m)) for h in range(2) for m in range(TM)])
            cols_out("kv", [(CT, G_KV), (HT, G_MIX1)])
            for m in range(TM):
                read_out(dve, ("kv", m))
            head_norm([(heads_of(KVR.rearrange("p a b -> p (a b)")), 8)], 8, "kvh", 0, sq1, "kv_rows")
            for h in range(2):
                for m in range(TM):
                    read_out(dve, ("win1", h, m))
            head_norm([(heads_of(HS.rearrange("p a b -> p (a b)")), 32)], 32, "q1", 8, sq1, None)
            for n in range(0, 8, 2):
                p = got(dve, ("q1T", n))
                free(v.tensor_copy(QT1[:, (n // 2) * 4:(n // 2) * 4 + 4, (n % 2) * P:(n % 2 + 1) * P],
                                   p[0:HD, :].rearrange("p (h t) -> p h t", h=4)), ("q1T", n))
            dve.wait_ge(S("tri"), 3)
            ca = lambda h: h < 12
            dve.wait_ge(S("rs_q1"), 1)
            ng = len(A1_HEADS) // 2
            for n in range(2):
                maxima("a1", n, ca, A1_HEADS)
            for n in range(ng):
                normalise("a1", n, PB1, ca)
                if n >= 1:
                    o_out("a1", n - 1, A1_HEADS)
                if n + 2 < ng:
                    maxima("a1", n + 2, ca, A1_HEADS)
            o_out("a1", ng - 1, A1_HEADS)
            for a in range(2):
                got(dve, ("a1", "O", ng - 1, a))
            v.memset(YR, 0.0)
            v.memset(GATE, 0.0)
            link(v.memset(LOWER, 0.0))
            for e in range(1, NE):
                last = v.memset(LOWER[:, e, 0:e], 1.0)
            link(last)
            residual([(h, m, ("wout1", h, m)) for h in range(2) for m in range(TM)])
            cols_out("f1", [(HT, G_FFN1)])
            p = got(dve, "router")
            dve.wait_ge(S("rs_f1"), 1)
            for m in range(TM):
                last = tsc(LG[:, m], p[:, m * NE:(m + 1) * NE], rs[:, m:m + 1], None, ALU.mult)
            free(last, "router")
            read_out(dve, "router")
            for m in range(TM):
                me = LG[:, m].unsqueeze(2).to_broadcast([P, NE, NE])
                ot = LG[:, m].unsqueeze(1).to_broadcast([P, NE, NE])
                tt(CMP, ot, me, ALU.is_gt)
                link(tt(CMP2, ot, me, ALU.is_equal))
                link(tt(CMP2, CMP2, LOWER, ALU.mult))
                link(tt(CMP, CMP, CMP2, ALU.add))
                link(v.tensor_reduce(out=RNK[:, m], in_=CMP, axis=AX.X, op=ALU.add))
            tsc(SEL, RNK, 1.5, None, ALU.is_lt).then_inc(S("sel"), 1)
            link(v.tensor_reduce(out=vt[:, 0:2], in_=LG, axis=AX.X, op=ALU.max))
            tt(LG, LG, vt[:, 0:2].unsqueeze(2).to_broadcast([P, TM, NE]), ALU.subtract).then_inc(S("rt_d"), 1)
            dve.wait_ge(S("rt_e"), 1)
            link(tt(EX, EX, SEL, ALU.mult))
            link(v.tensor_reduce(out=vt[:, 2:4], in_=EX, axis=AX.X, op=ALU.add))
            link(v.reciprocal(vt[:, 4:6], vt[:, 2:4]))
            for r in range(PASSES):
                last = tt(GW[:, :, r * NE:(r + 1) * NE], EX, vt[:, 4:6].unsqueeze(2).to_broadcast([P, TM, NE]), ALU.mult)
            link(last)
            p = got(dve, "place")
            link(tsc(POS0, p[:, 0:TM * NE].rearrange("p (m e) -> p m e", m=TM), 1.0, None, ALU.add))
            link(tt(POS0, POS0, SEL, ALU.mult))
            link(v.memset(POS, -1.0))
            for r in range(PASSES):
                last = tsc(POS[:, :, r * NE:(r + 1) * NE], POS0, -1.0 - CAP * r, None, ALU.add)
            link(last)
            free(v.tensor_reduce(out=vt[:, 6:7], in_=p[:, 2 * NE:3 * NE], axis=AX.X, op=ALU.max), "place")
            read_out(dve, "place")
            tsc(flag, vt[:, 6:7], CAP + 0.5, None, ALU.is_gt).then_inc(S("flag"), 1)

            def pick(i):
                for m in range(TM):
                    last = tsc(PICK[:, m], iota, POS[:, m, bass.ds(i, 1)], None, ALU.is_equal)
                last.then_inc(S("pick"), 1)

            def lo(turn, n):
                q, j, b = n // 4, n % 4, n % NPART
                dve.wait_ge(S("hi"), turn.count("hi", n + 1))
                tt(PART_HL[:, b, 1], at(e_slot(q) * SLOT + j * PART, PART), PART_HL[:, b, 0].bitcast(fp),
                   ALU.subtract).then_inc(S("lo_dve"), 1)

            def xg_out(turn, key):
                for b in range(2):
                    dve.wait_ge(S("hi_small"), b + 1 if turn is None else turn.count("hi_small", NC_E + b + 1))
                    p = PS[7 - b]
                    for a in range(4):
                        k = 4 * b + a
                        last = v.scalar_tensor_tensor(XG[:, 1, k], p[:, a * CAP:(a + 1) * CAP], gT[:, G_FFN1 + k:G_FFN1 + k + 1],
                                                      XG[:, 0, k].bitcast(fp), ALU.mult, ALU.subtract)
                    free(last, (key, "xg", b))

            def x_add(turn, key, bt, n, m):
                p = got(dve, (key, "sc", n, m), bt)
                x = XS[:, m, n * 512:(n + 1) * 512]
                free(tt(x, x, p[:, :], ALU.add), (key, "sc", n, m))

            def expert(turn, key):
                later = Turn(turn.i + 1, turn.start)
                for s in range(NPT):
                    n = s + NPART
                    if n % 4 < 3:
                        lo(turn if n < NPT else later, n % NPT)
                    k = n - LEAD
                    if k < NPT and k % 4 == 3 and items[k // 4][0] == "u":
                        c = items[k // 4][1]
                        p = got(dve, (key, "gu", c, 1), turn)
                        read_out(dve, (key, "gu", c, 0), turn)
                        free(tt(HID[0:CAP], SG1[0:CAP], p[0:CAP, :], ALU.mult), (key, "gu", c, 1))
                    if k in SC_AT:
                        x_add(turn, key, turn, *SC_AT[k])
                    if k in FLIP_AT:
                        dve.wait_ge(S("hi_small"), turn.count("hi_small", FLIP_AT[k] + 1))
                        free(tt(AT[:, 1].rearrange("p f t -> p (f t)"), PS[6][:, 0:4 * CAP],
                                AT[:, 0].rearrange("p f t -> p (f t)").bitcast(fp), ALU.subtract), (key, "aT", FLIP_AT[k]))
                    if k == GT_AT - 8:
                        dve.wait_ge(S("pick"), turn.count("pick", 0))
                        for m in range(TM):
                            last = tsc(PG[:, m], PICK[:, m], GW[:, m, bass.ds(turn.i, 1)], None, ALU.mult)
                        last.then_inc(S("pgate"), 1)
                    if k == GT_AT + 8:
                        pick(turn.i + 1)
                    if k == XG_AT:
                        xg_out(turn, key)
                    if k == NPT - 1:
                        p = got(dve, (key, "y", 0), turn)
                        free(v.tensor_copy(YR[0:CAP, 0:512], p[0:CAP, :]), (key, "y", 0))

            dve.wait_ge(S("iota"), 1)
            pick(0)
            for n in range(NPART):
                if n % 4 < 3:
                    lo(Turn(0, 0), n)
                if n == 2:
                    xg_out(None, "first")

            def passes(key, first, end):
                with dve.Fori(first, end) as i:
                    expert(Turn(i, first), key)
                for n, m in SC_AT.values():
                    x_add(Turn(end, first), (key, "end"), None, n, m)

            passes("main", 0, NE)
            dve.wait_ge(S("flag"), 1)
            over = dve.value_load(flag[0:1, 0:1], min_val=0, max_val=1)
            with dve.If(over > 0):
                v.memset(GATE, 0.0).then_inc(S("gate_zero"), 1)
                passes("over", NE, PASSES * NE)
            v.memset(vt[:, 8:9], 0.0).then_inc(S("x_final"), 1)


_INS = ['x', 'mem', 'l0_mix_norm', 'l0_w_in', 'l0_s5_lam_re', 'l0_s5_lam_im', 'l0_s5_log_dt', 'l0_s5_b_re', 'l0_s5_b_im',
        'l0_s5_c_re', 'l0_s5_c_im', 'l0_s5_d', 'l0_s5_w_glu', 'l0_s5_b_glu', 'l0_mem_norm', 'l0_w_mem_k', 'l0_w_mem_v',
        'l0_mem_q_gain', 'l0_mem_k_gain', 'l0_w_out', 'l0_ffn_norm', 'l0_ffn_w_gate', 'l0_ffn_w_up', 'l0_ffn_w_down',
        'kv_norm', 'kv_w_k', 'kv_w_v', 'kv_k_gain', 'l1_mix_norm', 'l1_w_in', 'l1_moba_q_gain', 'l1_mem_norm',
        'l1_w_mem_k', 'l1_w_mem_v', 'l1_mem_q_gain', 'l1_mem_k_gain', 'l1_w_out', 'l1_ffn_norm', 'l1_moe_router',
        'l1_moe_w_gate', 'l1_moe_w_up', 'l1_moe_w_down']


def kernel(**inputs):
    import numpy as _np
    import concourse.bacc as _bacc
    from concourse import mybir as _mybir
    from concourse.bass_utils import run_bass_kernel_spmd as _run

    nc = _bacc.Bacc("TRN2", target_bir_lowering=False, num_devices=1)
    arrays, w = {}, {}
    for name in _INS:
        a = _np.ascontiguousarray(inputs[name])
        arrays["in_" + name] = a
        w[name] = nc.dram_tensor("in_" + name, a.shape, _mybir.dt.from_np(a.dtype), kind="ExternalInput").ap()
    out = nc.dram_tensor("out_x", (1, T, D), _mybir.dt.float32, kind="ExternalOutput").ap()
    trunk(nc, w, out)
    r = _run(nc, [arrays], core_ids=[0])
    return r.results[0]["out_x"]
```
